# Optimizing a Trainium2 kernel written in Bass

```python
import math
import jax
import jax.numpy as jnp
from jax import lax
import numpy as np

D_MODEL = 2048
BATCH = 1
SEQ = 256
DEPTH = 1

HY_WIDTH = D_MODEL // 2
HY_ORDER = 2
FILT_EMB = 33
FILT_BANDS = (FILT_EMB - 1) // 2
FILT_HIDDEN = 64
MIN_DECAY = math.log(1e-2) / 1.5
MAX_DECAY = math.log(1e-2) / 0.3
SG_CHUNK = 128
SG_GROUPS = 8
SG_WIDTH = D_MODEL // 2
SG_HEAD_DIM = SG_WIDTH // SG_GROUPS
N_HY_COLS = 3 * HY_WIDTH
N_SG_COLS = 2 * SG_WIDTH
N_GATE_COLS = 2 * D_MODEL
N_IN = N_HY_COLS + N_SG_COLS + N_GATE_COLS
N_EXPERT_GROUPS = 4
EXPERTS_PER_GROUP = 4
N_EXPERTS = N_EXPERT_GROUPS * EXPERTS_PER_GROUP
TOP_K_INNER = 2
D_EXPERT = D_MODEL // 4
EPS = 1e-6

kernel_name = 'hybrid_hyena_sgu_hmoe_encoder'

def rms_norm(x, g):
    xf = x.astype(jnp.float32)
    y = xf * lax.rsqrt(jnp.mean(xf * xf, axis=-1, keepdims=True) + EPS)
    return (y * g.astype(jnp.float32)).astype(x.dtype)

def hyena_filters(L, w1, b1, w2, b2, w3, freq):
    f32 = jnp.float32
    t = jnp.linspace(0.0, 1.0, L, dtype=f32)[:, None]
    bands = jnp.linspace(1e-4, FILT_BANDS - 1, FILT_BANDS, dtype=f32)
    w = (2.0 * math.pi / L) * jnp.arange(L, dtype=f32)[:, None]
    z = jnp.concatenate([t, jnp.cos(bands * w), -jnp.sin(bands * w)], axis=-1)
    fr = freq.astype(f32)
    a = jnp.sin(fr * (z @ w1.astype(f32) + b1.astype(f32)))
    a = jnp.sin(fr * (a @ w2.astype(f32) + b2.astype(f32)))
    h = (a @ w3.astype(f32)).reshape(L, 2, HY_ORDER, HY_WIDTH)
    deltas = jnp.abs(jnp.linspace(MIN_DECAY, MAX_DECAY, HY_WIDTH, dtype=f32))
    h = h * jnp.exp(-t * deltas)[:, None, None, :]
    fwd, bwd = h[:, 0], h[:, 1]
    fwd = fwd.at[0].add(bwd[0])
    return jnp.concatenate([fwd, jnp.zeros_like(fwd[:1]), bwd[:0:-1]], axis=0)

def hyena_mixer(z, conv_w, conv_b, k_circ, skip):
    L = z.shape[1]
    zp = jnp.pad(z, ((0, 0), (1, 1), (0, 0)))
    zc = conv_w[0] * zp[:, :-2] + conv_w[1] * zp[:, 1:-1] + conv_w[2] * zp[:, 2:] + conv_b
    x1, x2, v = jnp.split(zc.astype(jnp.float32), 3, axis=-1)
    k_f = jnp.fft.rfft(k_circ, axis=0)
    sk = skip.astype(jnp.float32)

    def long_conv(u, o):
        u_f = jnp.fft.rfft(u, n=2 * L, axis=1)
        y = jnp.fft.irfft(u_f * k_f[None, :, o], n=2 * L, axis=1)[:, :L]
        return y + u * sk[o]

    z1 = x1 * long_conv(v, 0)
    y = x2 * long_conv(z1, 1)
    return y.astype(z.dtype)

def spatial_gating(zu, zv, ln_g, ln_b, w_s, b_s):
    B, L, _ = zu.shape
    u = jax.nn.gelu(zu, approximate=False)
    v = jax.nn.gelu(zv.astype(jnp.float32), approximate=False)
    mu = jnp.mean(v, axis=-1, keepdims=True)
    var = jnp.mean(jnp.square(v - mu), axis=-1, keepdims=True)
    v = ((v - mu) * lax.rsqrt(var + EPS) * ln_g + ln_b).astype(zu.dtype)
    vc = v.reshape(B, L // SG_CHUNK, SG_CHUNK, SG_GROUPS, SG_HEAD_DIM)
    mix = jnp.einsum('gts,bcsgk->bctgk', w_s, vc) + b_s.T[:, :, None]
    return u * mix.reshape(B, L, SG_WIDTH)

def hier_moe(h, w_rg, b_rg, w_re, b_re, w_gate, w_up, w_down):
    f32 = jnp.float32
    hf = h.astype(f32)
    p_grp = jax.nn.softmax(hf @ w_rg.astype(f32) + b_rg.astype(f32), axis=-1)
    grp = jnp.argmax(p_grp, axis=-1)
    p_sel = jnp.take_along_axis(p_grp, grp[..., None], axis=-1)
    le = jnp.einsum('bsd,gde->bsge', hf, w_re.astype(f32)) + b_re.astype(f32)
    le = jnp.take_along_axis(le, grp[..., None, None], axis=2)[..., 0, :]
    top_v, top_i = lax.top_k(le, TOP_K_INNER)
    wts = p_sel * jax.nn.softmax(top_v, axis=-1)
    eid = grp[..., None] * EXPERTS_PER_GROUP + top_i
    comb = jnp.einsum('bske,bsk->bse', jax.nn.one_hot(eid, N_EXPERTS, dtype=f32), wts).astype(h.dtype)
    act = jax.nn.silu(jnp.einsum('bsd,edf->bsef', h, w_gate)) * jnp.einsum('bsd,edf->bsef', h, w_up)
    return jnp.einsum('bsef,efd->bsd', act * comb[..., None], w_down)

def setup_inputs(seed: int = 0) -> dict:
    key = jax.random.key(seed)
    ks = jax.random.split(key, 32)
    f32 = jnp.float32

    def nrm(k, shape, s):
        return s * jax.random.normal(k, shape, f32)

    D = D_MODEL
    return {
        'x': nrm(ks[0], (BATCH, SEQ, D), 1.0),
        'g_mix': 1.0 + nrm(ks[1], (DEPTH, D), 0.05),
        'w_in': nrm(ks[2], (DEPTH, D, N_IN), D ** -0.5),
        'b_in': nrm(ks[3], (DEPTH, N_IN), 0.01),
        'conv_w': nrm(ks[4], (DEPTH, 3, N_HY_COLS), 3 ** -0.5),
        'conv_b': nrm(ks[5], (DEPTH, N_HY_COLS), 0.01),
        'filt_w1': nrm(ks[6], (DEPTH, FILT_EMB, FILT_HIDDEN), FILT_EMB ** -0.5),
        'filt_b1': nrm(ks[7], (DEPTH, FILT_HIDDEN), 0.1),
        'filt_w2': nrm(ks[8], (DEPTH, FILT_HIDDEN, FILT_HIDDEN), FILT_HIDDEN ** -0.5),
        'filt_b2': nrm(ks[9], (DEPTH, FILT_HIDDEN), 0.1),
        'filt_w3': nrm(ks[10], (DEPTH, FILT_HIDDEN, 2 * HY_ORDER * HY_WIDTH), 2.0 * (FILT_HIDDEN * SEQ) ** -0.5),
        'filt_freq': 1.0 + nrm(ks[11], (DEPTH, FILT_HIDDEN), 0.1),
        'hy_skip': 1.0 + nrm(ks[12], (DEPTH, HY_ORDER, HY_WIDTH), 0.1),
        'sg_ln_g': 1.0 + nrm(ks[13], (DEPTH, SG_WIDTH), 0.05),
        'sg_ln_b': nrm(ks[14], (DEPTH, SG_WIDTH), 0.01),
        'sg_w': nrm(ks[15], (DEPTH, SG_GROUPS, SG_CHUNK, SG_CHUNK), SG_CHUNK ** -0.5),
        'sg_b': 1.0 + nrm(ks[16], (DEPTH, SG_GROUPS, SG_CHUNK), 0.01),
        'w_hy_out': nrm(ks[17], (DEPTH, HY_WIDTH, D), HY_WIDTH ** -0.5),
        'w_sg_out': nrm(ks[18], (DEPTH, SG_WIDTH, D), SG_WIDTH ** -0.5),
        'w_out': nrm(ks[19], (DEPTH, D, D), D ** -0.5),
        'g_ffn': 1.0 + nrm(ks[20], (DEPTH, D), 0.05),
        'w_rg': nrm(ks[21], (DEPTH, D, N_EXPERT_GROUPS), D ** -0.5),
        'b_rg': nrm(ks[22], (DEPTH, N_EXPERT_GROUPS), 0.01),
        'w_re': nrm(ks[23], (DEPTH, N_EXPERT_GROUPS, D, EXPERTS_PER_GROUP), D ** -0.5),
        'b_re': nrm(ks[24], (DEPTH, N_EXPERT_GROUPS, EXPERTS_PER_GROUP), 0.01),
        'w_gate': nrm(ks[25], (DEPTH, N_EXPERTS, D, D_EXPERT), D ** -0.5),
        'w_up': nrm(ks[26], (DEPTH, N_EXPERTS, D, D_EXPERT), D ** -0.5),
        'w_down': nrm(ks[27], (DEPTH, N_EXPERTS, D_EXPERT, D), D_EXPERT ** -0.5),
        'g_final': 1.0 + nrm(ks[28], (D,), 0.05),
    }

def reference(x, g_mix, w_in, b_in, conv_w, conv_b, filt_w1, filt_b1, filt_w2, filt_b2, filt_w3,
              filt_freq, hy_skip, sg_ln_g, sg_ln_b, sg_w, sg_b, w_hy_out, w_sg_out, w_out, g_ffn,
              w_rg, b_rg, w_re, b_re, w_gate, w_up, w_down, g_final):
    L = x.shape[1]
    c_u = N_HY_COLS
    c_v = N_HY_COLS + SG_WIDTH
    c_g = N_HY_COLS + N_SG_COLS
    for i in range(DEPTH):
        xn = rms_norm(x, g_mix[i])
        zin = xn @ w_in[i] + b_in[i]
        z_hy = zin[..., :c_u]
        z_u = zin[..., c_u:c_v]
        z_v = zin[..., c_v:c_g]
        gate_hy = jax.nn.sigmoid(zin[..., c_g:c_g + D_MODEL])
        gate_sg = jax.nn.sigmoid(zin[..., c_g + D_MODEL:])
        k_circ = hyena_filters(L, filt_w1[i], filt_b1[i], filt_w2[i], filt_b2[i], filt_w3[i], filt_freq[i])
        y_hy = hyena_mixer(z_hy, conv_w[i], conv_b[i], k_circ, hy_skip[i])
        y_sg = spatial_gating(z_u, z_v, sg_ln_g[i], sg_ln_b[i], sg_w[i], sg_b[i])
        merged = gate_hy * (y_hy @ w_hy_out[i]) + gate_sg * (y_sg @ w_sg_out[i])
        x = x + merged @ w_out[i]
        x = x + hier_moe(rms_norm(x, g_ffn[i]), w_rg[i], b_rg[i], w_re[i], b_re[i],
                         w_gate[i], w_up[i], w_down[i])
    return rms_norm(x, g_final)


_drawn_inputs = setup_inputs


def setup_inputs(seed=0):
    import zlib

    import numpy as np

    out = dict(_drawn_inputs(seed))
    spreads = {}
    factors = {'conv_b': 11.991,
     'sg_ln_b': 48.195,
     'sg_b': 44.111,
     'b_rg': 11.422,
     'b_re': 32.045,
     'b_in': 4.62,
     'filt_b1': 3.441,
     'filt_b2': 2.746,
     'filt_freq': 5.352,
     'sg_ln_g': 7.855,
     'g_ffn': 3.958}
    for name, (base, spread) in spreads.items():
        noise = np.random.default_rng([zlib.crc32(name.encode()), seed]).standard_normal(out[name].shape)
        drawn = base * np.exp(spread * noise) if base else spread * noise
        out[name] = jnp.asarray(drawn.astype(out[name].dtype))
    for name, factor in factors.items():
        out[name] = (out[name] * factor).astype(out[name].dtype)
    return out
```

```python
import math
from contextlib import ExitStack

import concourse.bass as bass
from concourse import mybir

F32 = mybir.dt.float32
F32R = mybir.dt.float32r
I32 = mybir.dt.int32
ACT = mybir.ActivationFunctionType
ALU = mybir.AluOpType
AX = mybir.AxisListType.X

P = 128
L = 256
TB = L // P
D = 2048
KD = D // P
W = D // 2
CT = W // P
N = 512
HALVES = W // N
C_U = 3 * W
C_GHY = 5 * W
C_GSG = 7 * W
EMB, HID = 33, 64
GROUPS, PER = 4, 4
FE = D // 4
CAP = 128
EPS = 1e-6
UK = 2
RAW, SPLIT = 8, 4
MAGIC = 1.5 * 2.0 ** 23
PI_HI = 6.28125
PI_LO = 2.0 * math.pi - PI_HI

GATE_AT = [0] + [16 + 24 * e for e in range(PER - 1)]
DOWN_AT = [32 + 24 * e for e in range(PER - 1)] + [88]
A8, B8, C8, D8, E8, M8 = 0, 4, 10, 16, 22, 26


def static_le(value, bound):
    return isinstance(value, int) and value <= bound


def build(nc, x, w_in, w_hy_out, w_sg_out, w_out, w_gate, w_up, w_down, b_in, filt_w3, hy_skip,
          ln_g, ln_b, g_ffn, g_final, b_router,
          g_mix_c, conv_w_c, conv_b_c, b_hy_c, filt_w1, filt_w2, filt_vec, sg_w_t, sg_b_t, w_router,
          zpos, decay, dft, idft, ident_in, before_in, ones_in, slots_in, rank_in, out):
    ctx = ExitStack()
    with ctx:
        def sb(name, shape, dt=F32):
            return ctx.enter_context(nc.sbuf_tensor(name, shape, dt))

        def sem(name):
            return ctx.enter_context(nc.semaphore(name))

        def region(name, words, *layouts):
            made = []
            for layout in layouts:
                with ExitStack() as sub:
                    made.append([sub.enter_context(nc.sbuf_tensor(n, s, d)) for n, s, d in layout])
            sb(name, [P, words])
            return made

        raw = sb("raw", [P, RAW, UK, N])
        w_hi = sb("w_hi", [P, SPLIT, UK, N], F32R)
        w_lo = sb("w_lo", [P, SPLIT, UK, N], F32R)
        feat_hi = sb("feat_hi", [P, KD * L], F32R)
        feat_lo = sb("feat_lo", [P, KD * L], F32R)
        mid_hi = sb("mid_hi", [P, CT * L], F32R)
        mid_lo = sb("mid_lo", [P, CT * L], F32R)
        wide = sb("wide", [P, TB * D])
        ident = sb("ident", [P, P])
        before = sb("before", [P, P])
        ones = sb("ones", [P, P])
        slots = sb("slots", [P, CAP])
        rank = sb("rank", [P, TB, 4])
        bias = sb("bias", [P, 2, N])
        conv_w = sb("conv_w", [P, 3 * CT, 3])
        conv_b = sb("conv_b", [P, 3 * CT])
        b_hy = sb("b_hy", [P, 3 * CT])
        g_mix = sb("g_mix", [P, KD])
        fvec = sb("fvec", [P, 4])
        sgb = sb("sgb", [P, CT])
        wr = sb("wr", [P, KD, 20])
        brt = sb("brt", [P, TB, 20])
        stat = sb("stat", [P, 64])
        var = sb("var", [P, 4, TB])
        rstd = sb("rstd", [P, 4, TB])
        minus_half = sb("minus_half", [P, TB])

        (x_tok,), (prod_y, k_resp), (zt, zpad), (x2_tok,) = region(
            "region_x", TB * D,
            [("x_tok", [P, TB, D], F32)],
            [("prod_y", [P, 4, N], F32), ("k_resp", [P, 4, N], F32)],
            [("zt", [P, TB, N], F32), ("zpad", [P, 4, L + 2], F32)],
            [("x2_tok", [P, TB, D], F32)])
        (z_all, v_tok), (_, yhy_hi, yhy_lo), (gf_row, h_t), moe = region(
            "region_z", 4 * CT * L,
            [("z_all", [P, 3, CT * L], F32), ("v_tok", [P, TB, W], F32)],
            [("skip_v", [P, CT * L], F32), ("yhy_hi", [P, CT * L], F32R), ("yhy_lo", [P, CT * L], F32R)],
            [("gf_row", [P, D], F32), ("h_t", [P, KD, L], F32)],
            [("sil", [P, N], F32), ("prod", [P, N], F32), ("perm", [P, TB, CAP], F32R),
             ("perm_f", [P, TB, CAP], F32), ("perm_t", [P, TB * CAP], F32R), ("skip_m", [P, L], F32),
             ("y_hi", [P, D], F32R), ("y_lo", [P, D], F32R),
             ("act_hi", [P, 2, N], F32R), ("act_lo", [P, 2, N], F32R)])
        sil, prod, perm, perm_f, perm_t, _, y_hi, y_lo, act_hi, act_lo = moe
        (dft_f, dft_i, dec, w3s, hp_skip), (lng, lnb, sgw), filt_mem, (gl_row,) = region(
            "region_t", 8 * N,
            [("dft_f", [P, TB, N], F32), ("dft_i", [P, 4, L], F32), ("dec", [P, TB, N], F32), ("w3s", [P, N], F32),
             ("hp_skip", [1, N], F32)],
            [("lng", [P, W], F32), ("lnb", [P, W], F32), ("sgw", [P, 8, P], F32)],
            [("filt_a", [P, L], F32), ("filt_b", [P, L], F32), ("filt_c", [P, L], F32), ("w1s", [EMB, HID], F32),
             ("w2s", [HID, P], F32), ("zp", [EMB, L], F32)],
            [("gl_row", [P, D], F32)])
        filt_a, filt_b, filt_c, w1s, w2s, zp = filt_mem
        vt = z_all[:, 0]
        a2 = sb("a2", [P, 2, L])
        sig = sb("sig", [P, TB, N])
        oh = sb("oh", [P, 12, TB, 4])
        posi = sb("posi", [P, 8, TB])
        comb = sb("comb", [P, TB, 4])
        comb_hi = sb("comb_hi", [P, TB, 4], F32R)
        comb_lo = sb("comb_lo", [P, TB, 4], F32R)
        combg = sb("combg", [P, 4])
        lesel = sb("lesel", [P, TB, 16])
        logits = sb("logits", [P, TB, 20])
        rounds = sb("rounds", [P, 1], I32)
        bank = ctx.enter_context(nc.psum_tensor("bank", [P, 8, N], F32))

        ld = [sem(f"weights_loaded_{i}") for i in range(RAW)]
        hi_done, lo_done, unit_done = sem("hi_done"), sem("lo_done"), sem("unit_done")
        bias_in = [sem("bias_in_0"), sem("bias_in_1")]
        S = {n: sem(n) for n in (
            "a2_ready", "act_hi_s", "act_lo_s", "act_order", "act_t", "biased", "comb_mm", "combg_s", "consts_in",
            "conv_done", "dve_order", "f_arg", "f_mm", "f_sin", "filt_in", "filt_mm", "ga_hi", "ga_lo", "ga_mm",
            "gelu_done", "gf_in", "gl_in", "h3_in_0", "h3_in_1", "h_ev_act", "h_ev_dve", "h_hi_s", "h_lo_s", "h_ready", "h_tr",
            "half_in", "hsd_ready", "inv_mm", "k_mm", "k_ready", "ln_done", "m_hi", "m_lo", "m_t", "merged_ready",
            "mix_done", "moe_done", "oh_ready", "ot_ready", "out_done", "perm_r", "perm_ready", "perm_t_s",
            "perm_tr", "pos_mm", "prod_done", "r_exp", "r_exp2", "r_log", "r_m12", "r_mm", "route_ready",
            "rstd_ready", "sc_add", "sc_mm", "sg_in", "sig_ready", "silu_done", "sumsq", "sumsq2", "sumsq3",
            "tables_in", "u_mm", "v_t", "var_ready", "vtok_ready", "x_again", "x_in", "x_mid", "xr", "xr_hi",
            "xr_lo", "xr_t", "y_out", "y_ready", "yg_hi", "yg_lo", "yhy_hi_s", "yhy_lo_s", "ysg", "ysg_hi", "ysg_lo",
            "ysg_t", "z_t", "zpad_ready", "zt_ready")}

        class Order:
            def __init__(self, eng, s):
                self.eng, self.s, self.base, self.k = eng, s, 0, 0

            def link(self, ins):
                ins.then_inc(self.s, 1)
                self.k += 1
                self.eng.wait_ge(self.s, self.base + self.k)

            def enter(self, base):
                self.base, self.k = base, 0

        feat_hi_k = feat_hi[:].rearrange("p (k t) -> p k t", k=KD)
        feat_lo_k = feat_lo[:].rearrange("p (k t) -> p k t", k=KD)
        mid_hi_k = mid_hi[:].rearrange("p (k t) -> p k t", k=CT)
        mid_lo_k = mid_lo[:].rearrange("p (k t) -> p k t", k=CT)
        yhy_hi_k = yhy_hi[:].rearrange("p (k t) -> p k t", k=CT)
        yhy_lo_k = yhy_lo[:].rearrange("p (k t) -> p k t", k=CT)
        h_hi = feat_hi[:].rearrange("p (b d) -> p b d", b=TB)
        h_lo = feat_lo[:].rearrange("p (b d) -> p b d", b=TB)
        xg_hi = mid_hi[:].rearrange("p (k s) -> p k s", k=KD)
        xg_lo = mid_lo[:].rearrange("p (k s) -> p k s", k=KD)
        wide_t = wide[:].rearrange("p (b d) -> p b d", b=TB)
        vt_c = vt.rearrange("p (c t) -> p c t", c=CT)
        z_flat = z_all[:].rearrange("p r n -> p (r n)")

        def pair(c):
            return bank[:, 2 * (c % 2):2 * (c % 2) + 2, :]

        block = ctx.enter_context(nc.Block())

        @block.sync
        def _(sp):
            def load(idx8, u, src):
                n = 8 * idx8 + u - RAW + 1
                if not static_le(n, 0):
                    sp.wait_ge(lo_done, n)
                sp.dma_start(raw[:, u % RAW], src).then_inc(ld[u % RAW], 16)

            def rows(w):
                return w.rearrange("(u j p) n -> u p j n", j=UK, p=P)

            win, why, wsg, wo = rows(w_in[0]), rows(w_hy_out[0]), rows(w_sg_out[0]), rows(w_out[0])
            for b in range(TB):
                sp.dma_start(x_tok[:, b], x[0, b * P:(b + 1) * P]).then_inc(S["x_in"], 16)

            def bias_chunk(k, col):
                sp.dma_start(bias[:, k], b_in[0:1, bass.ds(col, N)].partition_broadcast(P)).then_inc(bias_in[k], 16)

            for c in range(4):
                if c >= 2:
                    sp.wait_ge(S["biased"], c - 1)
                bias_chunk(c % 2, C_U + c * N)
                for u in range(8):
                    load(A8 + c, u, win[u, :, :, C_U + c * N:C_U + (c + 1) * N])
            for c in range(2):
                for u in range(8):
                    load(B8 + c, u, win[u, :, :, 2 * W + c * N:2 * W + (c + 1) * N])
            with sp.Fori(2, 6) as c:
                for u in range(8):
                    load(B8 + c, u, win[u, :, :, bass.ds((c - 2) * N, N)])

            def gate_turns(p8, col, proj, biased):
                with sp.Fori(1, 3) as o:
                    for h in range(2):
                        sp.wait_ge(S["biased"], 2 * o + (biased + h - 3))
                        at = sp.snap((2 * o + h) * N)
                        bias_chunk(h, at + (col - 2 * N))
                        for u in range(8):
                            load(p8 - 3 + 3 * o, 12 * h + u, win[u, :, :, bass.ds(at + (col - 2 * N), N)])
                        for u in range(4):
                            load(p8 - 3 + 3 * o, 12 * h + 8 + u, proj[u, :, :, bass.ds(at - 2 * N, N)])

            gate_turns(C8, C_GSG, wsg, 4)
            gate_turns(D8, C_GHY, why, 8)
            sp.wait_ge(S["ot_ready"], 5)
            for b in range(TB):
                sp.dma_start(x2_tok[:, b], x[0, b * P:(b + 1) * P]).then_inc(S["x_again"], 16)
            with sp.Fori(0, 4) as c:
                for u in range(8):
                    load(E8 + c, u, wo[u, :, :, bass.ds(c * N, N)])

            def expert(i8, pos, e, kinds):
                for kind in kinds:
                    if kind in "gu":
                        w = (w_gate if kind == "g" else w_up)[0]
                        for u in range(8):
                            src = w[bass.ds(e, 1), u * UK * P:(u + 1) * UK * P, :].rearrange(
                                "e (j p) n -> p (e j) n", p=P)
                            load(i8, pos, src)
                            pos += 1
                    else:
                        for c in range(4):
                            for u in range(2):
                                src = w_down[0][bass.ds(e, 1), u * UK * P:(u + 1) * UK * P,
                                                c * N:(c + 1) * N].rearrange("e (j p) n -> p (e j) n", p=P)
                                load(i8, pos, src)
                                pos += 1
                return pos

            def group(i8, g):
                pos = expert(i8, 0, g * PER, "gu")
                for e in range(1, PER):
                    pos = expert(i8, pos, g * PER + e, "gu")
                    pos = expert(i8, pos, g * PER + e - 1, "d")
                assert expert(i8, pos, g * PER + PER - 1, "d") == 96

            with sp.Fori(0, GROUPS) as g:
                group(M8 + 12 * g, g)
            sp.wait_ge(S["route_ready"], 1)
            more = sp.value_load(rounds[0:1, 0:1], min_val=0, max_val=1)
            with sp.If(more != 0):
                with sp.Fori(0, GROUPS) as g:
                    group(M8 + 12 * GROUPS + 12 * g, g)
            for b in range(TB):
                sp.wait_ge(S["y_out"], b + 1)
                sp.dma_start(out[0, b * P:(b + 1) * P], wide_t[:, b]).then_inc(S["out_done"], 16)
            sp.wait_ge(S["out_done"], 16 * TB)

        @block.gpsimd
        def _(pool):
            pool.memset(minus_half[:], -0.5).then_inc(S["half_in"], 1)
            pool.wait_ge(S["half_in"], 1)
            for n in range(4):
                pool.wait_ge(S["var_ready"], n + 1)
                pool.tensor_tensor(rstd[:, n], var[:, n], minus_half[:], ALU.pow).then_inc(S["rstd_ready"], 1)

        @block.scalar
        def _(act):
            order = Order(act, S["act_order"])

            def split_hi(i8, u, nxt=None):
                act.wait_ge(ld[u % RAW], 16 * (i8 + u // RAW) + 16)
                n = 8 * i8 + u - SPLIT + 1
                if not static_le(n, 0):
                    act.wait_ge(unit_done, n)
                nc.scalar.activation(w_hi[:, u % SPLIT], raw[:, u % RAW], ACT.Copy).then_inc(hi_done, 1)

            def splits(i8, lo_, hi_, hooks={}):
                for u in range(lo_, hi_):
                    split_hi(i8, u)
                    for f in hooks.get(u, ()):
                        f()

            for dst, src in ((ident, ident_in), (g_mix, g_mix_c), (conv_w, conv_w_c), (conv_b, conv_b_c),
                             (b_hy, b_hy_c), (fvec, filt_vec), (before, before_in), (ones, ones_in),
                             (slots, slots_in), (rank, rank_in), (sgb, sg_b_t), (wr, w_router)):
                act.dma_start(dst[:], src).then_inc(S["consts_in"], 16)
            n_const = 12
            act.dma_start(brt[:], b_router.partition_broadcast(P)).then_inc(S["consts_in"], 16)
            n_const += 1
            for dst, src in ((w1s, filt_w1[0]), (w2s, filt_w2), (zp, zpos)):
                act.dma_start(dst[:], src).then_inc(S["filt_in"], 16)

            act.wait_ge(S["x_in"], 16 * TB)
            for b in range(TB):
                nc.scalar.activation(wide_t[:, b], x_tok[:, b], ACT.Square,
                                     accum_out=stat[:, b:b + 1]).then_inc(S["sumsq"], 1)
            act.wait_ge(S["rstd_ready"], 1)
            for b in range(TB):
                nc.scalar.activation(wide_t[:, b], x_tok[:, b], ACT.Copy,
                                     scale=rstd[:, 0, b:b + 1]).then_inc(S["xr"], 1)
            act.wait_ge(S["consts_in"], 16 * n_const)
            for q in range(KD // 2):
                act.wait_ge(S["xr_t"], q + 1)
                for j in range(2):
                    k = 2 * q + j
                    ins = nc.scalar.activation(feat_hi_k[:, k], bank[:, 4 + q % 4, j * L:(j + 1) * L], ACT.Copy,
                                               scale=g_mix[:, k:k + 1])
                    ins.then_inc(S["xr_hi"], 1)

            def gelu(c):
                act.wait_ge(S["biased"], c + 1)
                nc.scalar.activation(wide_t[:, 0:2, bass.ds(c * N, N)], wide_t[:, 0:2, bass.ds(c * N, N)],
                                     ACT.Gelu).then_inc(S["gelu_done"], 1)

            def filter_sine(n, dst):
                act.wait_ge(S["f_arg"], n)
                nc.scalar.activation(dst, filt_c[0:HID if n == 1 else P], ACT.Sin).then_inc(S["f_sin"], 1)

            filter_sine(1, filt_a[0:HID])
            filter_sine(2, a2[:, 0])
            splits(A8, 0, 8)
            act.wait_ge(S["a2_ready"], 1)
            act.dma_start(lng[:], ln_g.partition_broadcast(P)).then_inc(S["sg_in"], 16)
            act.dma_start(lnb[:], ln_b.partition_broadcast(P)).then_inc(S["sg_in"], 16)
            act.dma_start(sgw[:], sg_w_t).then_inc(S["sg_in"], 16)
            for c in range(1, 4):
                splits(A8 + c, 0, 8, {4: [lambda c=c: gelu(c - 1)]})

            def z_evac(c, parity):
                act.wait_ge(unit_done, 8 * (B8 + c) + 8)
                nc.scalar.activation(zt[:], pair(parity), ACT.Copy).then_inc(S["zt_ready"], 1)

            def z_bias(c):
                act.wait_ge(S["z_t"], c + 1)
                if not static_le(c, 0):
                    act.wait_ge(S["conv_done"], c)
                for j in range(4):
                    ins = nc.scalar.activation(zpad[:, j, 1:L + 1], bank[:, 4 + j // 2, (j % 2) * L:(j % 2 + 1) * L],
                                               ACT.Identity, bias=b_hy[:, bass.ds(4 * c + j, 1)])
                ins.then_inc(S["zpad_ready"], 1)

            def mix_evac_hi():
                act.wait_ge(S["ysg_t"], 1)
                for q in range(4):
                    nc.scalar.activation(mid_hi[:, q * N:(q + 1) * N], bank[:, 4 + q], ACT.Copy).then_inc(S["ysg_hi"], 1)

            splits(B8, 0, 8, {0: [lambda: gelu(3)]})
            splits(B8 + 1, 0, 8, {3: [lambda: z_evac(0, 0)], 4: [mix_evac_hi], 7: [lambda: z_bias(0)]})
            act.wait_ge(S["mix_done"], 1)
            act.dma_start(dft_f[:], dft).then_inc(S["tables_in"], 16)
            act.dma_start(dft_i[:], idft).then_inc(S["tables_in"], 16)
            with act.Fori(1, 3) as h:
                for p in range(2):
                    splits(B8 + 2 * h + p, 0, 8, {3: [lambda: z_evac(2 * h + p - 1, 1 - p)],
                                                  7: [lambda: z_bias(2 * h + p - 1)]})
            z_evac(5, 1)
            z_bias(5)

            def h3_load(o, h):
                w3v = filt_w3[0].rearrange("h (d o n) -> d h o n", d=2, o=2)
                for d in range(2):
                    act.dma_start(w3s[d * HID:(d + 1) * HID, :],
                                  w3v[d, :, bass.ds(o, 1), h * N:(h + 1) * N].rearrange("h o n -> h (o n)")
                                  ).then_inc(S[f"h3_in_{h}"], 16)
                act.dma_start(dec[:], decay[:, :, h * N:(h + 1) * N]).then_inc(S[f"h3_in_{h}"], 16)
                act.dma_start(hp_skip[:], hy_skip[0, bass.ds(o, 1), h * N:(h + 1) * N]).then_inc(S[f"h3_in_{h}"], 16)

            def v_evac(o):
                for q in range(4):
                    act.wait_ge(S["v_t"], 4 * o + q + 1)
                    c, b = 4 * (q // 2), q % 2
                    nc.scalar.activation(v_tok[:, b, c * P:(c + 4) * P], bank[:, 4 + q], ACT.Copy
                                         ).then_inc(S["vtok_ready"], 1)

            def k_evac(s):
                act.wait_ge(S["k_mm"], s + 1)
                for q in range(2):
                    ins = nc.scalar.activation(k_resp[:, 2 * q:2 * q + 2], bank[:, 4 + 2 * q:6 + 2 * q], ACT.Copy)
                ins.then_inc(S["k_ready"], 1)

            def sigmoid(n):
                act.wait_ge(S["biased"], n + 5)
                nc.scalar.activation(sig[:], sig[:], ACT.Sigmoid).then_inc(S["sig_ready"], 1)

            def next_h3(s, o, h):
                act.wait_ge(S["hsd_ready"], s + 1)
                h3_load(o, h)

            h3_load(0, 0)
            with act.Fori(0, 2) as o:
                splits(C8 + 3 * o, 0, 24, {
                    4: [lambda: v_evac(o)],
                    6: [lambda: next_h3(2 * o, o, 1)],
                    8: [lambda: k_evac(2 * o)],
                    11: [lambda: sigmoid(2 * o)],
                    18: [lambda: k_evac(2 * o + 1)],
                    23: [lambda: sigmoid(2 * o + 1)]})
                act.wait_ge(S["hsd_ready"], 2 * o + 2)
                h3_load(1, 0)
            act.wait_ge(S["ot_ready"], 5)
            nc.scalar.activation(yhy_hi[:], vt, ACT.Copy).then_inc(S["yhy_hi_s"], 1)
            with act.Fori(0, 2) as o:
                splits(D8 + 3 * o, 0, 24, {
                    11: [lambda: sigmoid(4 + 2 * o)],
                    23: [lambda: sigmoid(4 + 2 * o + 1)]})
            act.wait_ge(S["yhy_lo_s"], 1)
            act.dma_start(gf_row[:], g_ffn.partition_broadcast(P)).then_inc(S["gf_in"], 16)
            act.wait_ge(S["h3_in_0"], 192)
            act.dma_start(gl_row[:], g_final.partition_broadcast(P)).then_inc(S["gl_in"], 16)
            for q in range(KD // 2):
                act.wait_ge(S["m_t"], q + 1)
                nc.scalar.activation(feat_hi[:, q * N:(q + 1) * N], bank[:, 4 + q % 4], ACT.Copy).then_inc(S["m_hi"], 1)
            splits(E8, 0, 8)
            with act.Fori(1, 4) as c:
                splits(E8 + c, 0, 8)
            act.wait_ge(S["x_mid"], 4)
            for b in range(TB):
                nc.scalar.activation(wide_t[:, b], x2_tok[:, b], ACT.Square,
                                     accum_out=stat[:, 4 + b:5 + b]).then_inc(S["sumsq2"], 1)
            for b in range(TB):
                act.wait_ge(S["h_ready"], b + 1)
                nc.scalar.activation(h_hi[:, b], wide_t[:, b], ACT.Copy).then_inc(S["h_hi_s"], 1)
            for q in range(0, KD // 2, 2):
                act.wait_ge(S["h_tr"], q + 1)
                nc.scalar.activation(h_t[:, 2 * q:2 * q + 2].rearrange("p k t -> p (k t)"), bank[:, 4 + q % 4],
                                     ACT.Copy).then_inc(S["h_ev_act"], 1)
            act.wait_ge(S["r_log"], 1)
            nc.scalar.activation(oh[:, 1], oh[:, 0], ACT.Exp).then_inc(S["r_exp"], 1)
            act.wait_ge(S["r_m12"], 1)
            nc.scalar.activation(stat[:, 16:18], stat[:, 14:16], ACT.Exp).then_inc(S["r_exp2"], 1)

            def group(i8, i, g):
                act.wait_ge(S["perm_ready"], i + 1)
                nc.scalar.activation(perm[:], perm_f[:], ACT.Copy).then_inc(S["perm_r"], 1)
                act.wait_ge(S["perm_tr"], i + 1)
                nc.scalar.activation(perm_t[:], bank[:, 3, 0:L], ACT.Copy).then_inc(S["perm_t_s"], 1)
                for q in range(4):
                    act.wait_ge(S["ga_mm"], 4 * i + q + 1)
                    nc.scalar.activation(mid_hi[:, q * N:(q + 1) * N], bank[:, 4 + q], ACT.Copy).then_inc(S["ga_hi"], 1)

                def silu(e):
                    act.wait_ge(unit_done, 8 * i8 + GATE_AT[e] + 8)
                    if e:
                        act.wait_ge(S["prod_done"], PER * i + e)
                    nc.scalar.activation(sil[:], bank[:, 0], ACT.Silu).then_inc(S["silu_done"], 1)

                def act_split_hi(e):
                    act.wait_ge(S["act_t"], PER * i + e + 1)
                    if e >= 2:
                        act.wait_ge(unit_done, 8 * i8 + DOWN_AT[e - 2] + 8)
                    nc.scalar.activation(act_hi[:, e % 2], bank[:, 2], ACT.Copy).then_inc(S["act_hi_s"], 1)

                splits(i8, 0, 16, {11: [lambda: silu(0)]})
                for e in range(1, PER):
                    p = 16 + 24 * (e - 1)
                    hooks = {p + 11: [lambda e=e: act_split_hi(e - 1), lambda e=e: silu(e)]}
                    if e == PER - 1:
                        hooks[p + 23] = [lambda e=e: act_split_hi(e)]
                    splits(i8, p, p + 24, hooks)
                splits(i8, 88, 96)
                for q in range(4):
                    act.wait_ge(unit_done, 8 * i8 + 96)
                    nc.scalar.activation(y_hi[:, q * N:(q + 1) * N], bank[:, 4 + q], ACT.Copy).then_inc(S["yg_hi"], 1)

            with act.Fori(0, GROUPS) as g:
                group(M8 + 12 * g, g, g)
            act.wait_ge(S["route_ready"], 1)
            more = act.value_load(rounds[0:1, 0:1], min_val=0, max_val=1)
            with act.If(more != 0):
                with act.Fori(0, GROUPS) as g:
                    group(M8 + 12 * GROUPS + 12 * g, GROUPS + g, g)
            act.wait_ge(S["moe_done"], 1)
            for b in range(TB):
                nc.scalar.activation(wide_t[:, b], x2_tok[:, b], ACT.Square,
                                     accum_out=stat[:, 20 + b:21 + b]).then_inc(S["sumsq3"], 1)

        @block.vector
        def _(dve):
            order = Order(dve, S["dve_order"])
            link = order.link
            V = nc.vector

            def splits(i8, lo_, hi_, hooks={}):
                for u in range(lo_, hi_):
                    dve.wait_ge(hi_done, 8 * i8 + u + 1)
                    V.tensor_tensor(w_lo[:, u % SPLIT], raw[:, u % RAW], w_hi[:, u % SPLIT],
                                    ALU.subtract).then_inc(lo_done, 1)
                    for f in hooks.get(u, ()):
                        f()

            def mean_square(n, src):
                V.tensor_scalar(var[:, n], src, 1.0 / D, EPS, ALU.mult, ALU.add).then_inc(S["var_ready"], 1)

            dve.wait_ge(S["sumsq"], TB)
            mean_square(0, stat[:, 0:2])
            for q in range(KD // 2):
                for j in range(2):
                    k = 2 * q + j
                    dve.wait_ge(S["xr_hi"], 2 * q + 2)
                    V.scalar_tensor_tensor(feat_lo_k[:, k], bank[:, 4 + q % 4, j * L:(j + 1) * L], g_mix[:, k:k + 1],
                                           feat_hi_k[:, k], ALU.mult, ALU.subtract).then_inc(S["xr_lo"], 1)

            def filter_arg(n, h, bcol):
                dve.wait_ge(S["f_mm"], n)
                link(V.tensor_scalar(filt_b[0:h], bank[0:h, 4, 0:L], fvec[0:h, bcol:bcol + 1], fvec[0:h, 0:1],
                                     ALU.add, ALU.mult))
                link(V.tensor_scalar(filt_c[0:h], filt_b[0:h], 1.0 / (2.0 * math.pi), MAGIC, ALU.mult, ALU.add))
                link(V.tensor_scalar(filt_c[0:h], filt_c[0:h], MAGIC, None, ALU.subtract))
                link(V.scalar_tensor_tensor(filt_b[0:h], filt_c[0:h], -PI_HI, filt_b[0:h], ALU.mult, ALU.add))
                link(V.scalar_tensor_tensor(filt_b[0:h], filt_c[0:h], -PI_LO, filt_b[0:h], ALU.mult, ALU.add))
                V.tensor_scalar(filt_c[0:h], filt_b[0:h], math.pi, -math.pi, ALU.min, ALU.max).then_inc(S["f_arg"], 1)

            filter_arg(1, HID, 1)
            filter_arg(2, P, 2)
            dve.wait_ge(S["f_sin"], 2)
            V.tensor_scalar(a2[:, 1], a2[:, 0], fvec[:, 3:4], None, ALU.mult).then_inc(S["a2_ready"], 1)

            def sg_add(c, par):
                dve.wait_ge(unit_done, 8 * (A8 + c) + 8)
                dve.wait_ge(bias_in[par], 16 * (c // 2 + 1))
                for b in range(TB):
                    ins = V.tensor_tensor(wide_t[:, b, c * N:(c + 1) * N], pair(par)[:, b], bias[:, par], ALU.add)
                ins.then_inc(S["biased"], 1)

            splits(A8, 0, 8)
            for c in range(1, 4):
                splits(A8 + c, 0, 8, {3: [lambda c=c: sg_add(c - 1, (c - 1) % 2)]})

            def layer_norm():
                dve.wait_ge(S["gelu_done"], 4)
                dve.wait_ge(S["sg_in"], 48)
                for b in range(TB):
                    for s in range(2):
                        link(V.bn_stats(oh_flat[:, 6 * s:6 * s + 6], wide_t[:, b, W + s * N:W + (s + 1) * N]))
                    link(V.bn_aggr(stat[:, 8 + 2 * b:10 + 2 * b], oh_flat[:, 0:12]))
                moments = stat[:, 8:12].rearrange("p (b m) -> p b m", m=2)
                V.tensor_scalar(var[:, 1], moments[:, :, 1], EPS, None, ALU.add).then_inc(S["var_ready"], 1)
                dve.wait_ge(S["rstd_ready"], 2)
                for b in range(TB):
                    v = wide_t[:, b, W:2 * W]
                    link(V.tensor_scalar(v, v, moments[:, b, 0:1], rstd[:, 1, b:b + 1], ALU.subtract, ALU.mult))
                    link(V.tensor_tensor(v, v, lng[:], ALU.mult))
                    V.tensor_tensor(v, v, lnb[:], ALU.add).then_inc(S["ln_done"], 1)

            oh_flat = oh[:].rearrange("p a b c -> p (a b c)")

            def mix():
                dve.wait_ge(S["mix_done"], 1)
                for g in range(8):
                    V.scalar_tensor_tensor(wide_t[:, :, g * P:(g + 1) * P],
                                           bank[:, 4 + g // 2, (g % 2) * L:(g % 2 + 1) * L].rearrange(
                                               "p (b k) -> p b k", b=TB),
                                           sgb[:, g:g + 1], wide_t[:, :, g * P:(g + 1) * P],
                                           ALU.add, ALU.mult).then_inc(S["ysg"], 1)

            def mix_evac_lo():
                for q in range(4):
                    dve.wait_ge(S["ysg_hi"], q + 1)
                    V.tensor_tensor(mid_lo[:, q * N:(q + 1) * N], bank[:, 4 + q], mid_hi[:, q * N:(q + 1) * N],
                                    ALU.subtract).then_inc(S["ysg_lo"], 1)

            def conv(c):
                dve.wait_ge(S["zpad_ready"], c + 1)
                dst = z_flat[:, bass.ds(c * 4 * L, 4 * L)].rearrange("p (j t) -> p j t", j=4)
                w = conv_w[:, bass.ds(4 * c, 4), :]
                cb = conv_b[:, bass.ds(4 * c, 4)]
                for tap in range(3):
                    for j in range(4):
                        z = zpad[:, j, tap:tap + L]
                        if tap == 0:
                            ins = V.tensor_scalar(dst[:, j], z, w[:, j, 0:1], cb[:, j:j + 1], ALU.mult, ALU.add)
                        else:
                            ins = V.scalar_tensor_tensor(dst[:, j], z, w[:, j, tap:tap + 1], dst[:, j],
                                                         ALU.mult, ALU.add)
                    if tap < 2:
                        link(ins)
                ins.then_inc(S["conv_done"], 1)

            splits(B8, 0, 8, {0: [lambda: sg_add(3, 1)], 3: [layer_norm]})
            link(V.memset(zpad[:, :, 0:1], 0.0))
            link(V.memset(zpad[:, :, L + 1:L + 2], 0.0))
            mix()
            splits(B8 + 1, 0, 8, {4: [mix_evac_lo], 7: [lambda: conv(0)]})
            k0 = order.base + order.k
            with dve.Fori(1, 3) as h:
                order.enter(k0 + 4 * (h - 1))
                for p in range(2):
                    splits(B8 + 2 * h + p, 0, 8, {7: [lambda: conv(2 * h + p - 1)]})
                assert order.k == 4
            order.enter(k0 + 8)
            conv(5)
            dve.wait_ge(S["conv_done"], 6)
            dve.sem_inc(S["ot_ready"], 1)
            dve.sem_inc(S["merged_ready"], 1)

            def h_evac(s, o, h):
                dve.wait_ge(S["filt_mm"], s + 1)
                dve.wait_ge(S[f"h3_in_{h}"], 64 * o + 64)
                link(V.tensor_tensor(prod_y[:, 0:2], bank[:, 4:6], dec[:], ALU.mult))
                link(V.tensor_tensor(prod_y[0:1, 0], prod_y[0:1, 0], hp_skip[:], ALU.add))
                V.tensor_tensor(prod_y[:, 2:4], bank[:, 6:8], dec[:], ALU.mult).then_inc(S["hsd_ready"], 1)

            def products(s):
                dve.wait_ge(S["u_mm"], s + 1)
                dve.wait_ge(S["k_ready"], s + 1)
                uc, us = bank[:, 4:6], bank[:, 6:8]
                kc, ks = k_resp[:, 0:2], k_resp[:, 2:4]
                link(V.tensor_tensor(prod_y[:, 0:2], uc, kc, ALU.mult))
                link(V.tensor_tensor(sig[:], us, ks, ALU.mult))
                link(V.tensor_tensor(prod_y[:, 0:2], prod_y[:, 0:2], sig[:], ALU.subtract))
                link(V.tensor_tensor(prod_y[:, 2:4], uc, ks, ALU.mult))
                link(V.tensor_tensor(sig[:], us, kc, ALU.mult))
                V.tensor_tensor(prod_y[:, 2:4], prod_y[:, 2:4], sig[:], ALU.add).then_inc(S["y_ready"], 1)
                dve.wait_ge(S["y_ready"], s + 1)

            def ot(s, o, h):
                dve.wait_ge(S["inv_mm"], s + 1)
                dst = z_flat[:, h * 4 * L:(h + 1) * 4 * L]
                src = bank[:, 4:6].rearrange("p b n -> p (b n)")
                V.tensor_tensor(dst, src, z_flat[:, bass.ds(o * CT * L + (CT + 4 * h) * L, 4 * L)],
                                ALU.mult).then_inc(S["ot_ready"], 1)

            def gate_add(n, par, turn):
                dve.wait_ge(bias_in[par], 16 * (turn + 3))
                for b in range(TB):
                    ins = V.tensor_tensor(sig[:, b], bank[:, b], bias[:, par], ALU.add)
                ins.then_inc(S["biased"], 1)

            def merge(n, chunk, add):
                dve.wait_ge(S["sig_ready"], n + 1)
                dst = wide_t[:, :, bass.ds(chunk * N, N)]
                if add:
                    link(V.tensor_tensor(sig[:], bank[:, 2:4], sig[:], ALU.mult))
                    V.tensor_tensor(dst, dst, sig[:], ALU.add).then_inc(S["merged_ready"], 1)
                else:
                    V.tensor_tensor(dst, bank[:, 2:4], sig[:], ALU.mult).then_inc(S["merged_ready"], 1)

            def gate_done(i8, u):
                dve.wait_ge(unit_done, 8 * i8 + u)

            def turn(i8, n0, t0, o, add, extra):
                hooks = {}
                def g0():
                    gate_done(i8, 8)
                    gate_add(n0, 0, t0)
                def p0():
                    gate_done(i8, 12)
                    merge(n0, 2 * o, add)
                def g1():
                    gate_done(i8, 20)
                    gate_add(n0 + 1, 1, t0)
                hooks[11] = [g0]
                hooks[15] = [p0]
                hooks[23] = [g1]
                for u, fs in extra.items():
                    hooks[u] = fs + hooks.get(u, [])
                splits(i8, 0, 24, hooks)
                gate_done(i8, 24)
                merge(n0 + 1, 2 * o + 1, add)

            k0 = order.base + order.k
            per = 2 * (2 + 5)
            with dve.Fori(0, 2) as o:
                order.enter(k0 + per * o)
                turn(C8 + 3 * o, 2 * o, o, o, False, {
                    6: [lambda: h_evac(2 * o, o, 0)],
                    10: [lambda: products(2 * o)],
                    14: [lambda: ot(2 * o, o, 0)],
                    16: [lambda: h_evac(2 * o + 1, o, 1)],
                    19: [lambda: products(2 * o + 1)],
                    23: [lambda: ot(2 * o + 1, o, 1)]})
                assert order.k == per, order.k
            order.enter(k0 + 2 * per)
            dve.wait_ge(S["yhy_hi_s"], 1)
            V.tensor_tensor(yhy_lo[:], vt, yhy_hi[:], ALU.subtract).then_inc(S["yhy_lo_s"], 1)
            k0 = order.base + order.k
            per = 2
            with dve.Fori(0, 2) as o:
                order.enter(k0 + per * o)
                turn(D8 + 3 * o, 4 + 2 * o, 2 + o, o, True, {})
                assert order.k == per, order.k
            order.enter(k0 + 2 * per)
            for q in range(KD // 2):
                dve.wait_ge(S["m_hi"], q + 1)
                V.tensor_tensor(feat_lo[:, q * N:(q + 1) * N], bank[:, 4 + q % 4], feat_hi[:, q * N:(q + 1) * N],
                                ALU.subtract).then_inc(S["m_lo"], 1)

            def residual(c):
                dve.wait_ge(unit_done, 8 * (E8 + c) + 8)
                if isinstance(c, int) and c == 0:
                    dve.wait_ge(S["x_again"], 16 * TB)
                dst = x2_tok[:, :, bass.ds(c * N, N)]
                V.tensor_tensor(dst, bank[:, 0:2], dst, ALU.add).then_inc(S["x_mid"], 1)

            splits(E8, 0, 8)
            residual(0)
            with dve.Fori(1, 4) as c:
                splits(E8 + c, 0, 8)
                residual(c)

            dve.wait_ge(S["sumsq2"], TB)
            mean_square(2, stat[:, 4:6])
            dve.wait_ge(S["rstd_ready"], 3)
            dve.wait_ge(S["gf_in"], 16)
            for b in range(TB):
                V.scalar_tensor_tensor(wide_t[:, b], x2_tok[:, b], rstd[:, 2, b:b + 1], gf_row[:],
                                       ALU.mult, ALU.mult).then_inc(S["h_ready"], 1)
            for q in range(1, KD // 2, 2):
                dve.wait_ge(S["h_tr"], q + 1)
                V.tensor_copy(h_t[:, 2 * q:2 * q + 2].rearrange("p k t -> p (k t)"), bank[:, 4 + q % 4]
                              ).then_inc(S["h_ev_dve"], 1)
            dve.wait_ge(S["r_mm"], TB)
            for b in range(TB):
                link(V.tensor_tensor(logits[:, b], bank[:, 2 + b, 0:20], brt[:, b], ALU.add))
            lg = logits[:, :, 0:4]
            le = logits[:, :, 4:20].rearrange("p b (g e) -> p b g e", g=GROUPS)

            def bc4(v):
                return v.unsqueeze(2).to_broadcast([P, TB, 4])

            mg, m1, m2 = stat[:, 24:26], stat[:, 26:28], stat[:, 28:30]
            tie = stat[:, 30:32]

            def first_max(dst, vals, m):
                link(V.tensor_reduce(m, vals, AX, ALU.max))
                link(V.tensor_tensor(dst, vals, bc4(m), ALU.is_equal))
                link(V.tensor_tensor(dst, dst, rank[:], ALU.mult))
                link(V.tensor_reduce(tie, dst, AX, ALU.max))
                link(V.tensor_tensor(dst, dst, bc4(tie), ALU.is_equal))

            G1 = oh[:, 2]
            E1, E2, le1, le2 = oh[:, 3], oh[:, 4], oh[:, 5], oh[:, 6]
            first_max(G1, lg, mg)
            link(V.tensor_tensor(oh[:, 0], lg, bc4(mg), ALU.subtract))
            dve.sem_inc(S["r_log"], 1)
            dve.sem_inc(S["oh_ready"], 1)
            sel = lesel[:].rearrange("p b (g e) -> p b g e", g=GROUPS)
            for b in range(TB):
                link(V.tensor_tensor(sel[:, b], le[:, b], G1[:, b].unsqueeze(2).to_broadcast([P, 4, 4]), ALU.mult))
            link(V.tensor_reduce(le1, sel.rearrange("p b g e -> p b e g"), AX, ALU.add))
            first_max(E1, le1, m1)
            link(V.scalar_tensor_tensor(le2, E1, -3.0e38, le1, ALU.mult, ALU.add))
            first_max(E2, le2, m2)
            link(V.tensor_tensor(stat[:, 14:16], m2, m1, ALU.subtract))
            dve.sem_inc(S["r_m12"], 1)
            dve.wait_ge(S["r_exp"], 1)
            psel = stat[:, 32:34]
            link(V.tensor_reduce(psel, oh[:, 1], AX, ALU.add))
            dve.wait_ge(S["r_exp2"], 1)
            t2, w1_, w2_ = stat[:, 16:18], stat[:, 34:36], stat[:, 36:38]
            link(V.tensor_scalar(w1_, t2, 1.0, None, ALU.add))
            link(V.tensor_tensor(w1_, w1_, psel, ALU.mult))
            link(V.reciprocal(w1_, w1_))
            link(V.tensor_tensor(w2_, w1_, t2, ALU.mult))
            link(V.tensor_tensor(comb[:], E1, bc4(w1_), ALU.mult))
            link(V.tensor_tensor(oh[:, 7], E2, bc4(w2_), ALU.mult))
            link(V.tensor_tensor(comb[:], comb[:], oh[:, 7], ALU.add))
            link(V.tensor_copy(comb_hi[:], comb[:]))
            link(V.tensor_tensor(comb_lo[:], comb[:], comb_hi[:], ALU.subtract))
            dve.wait_ge(S["pos_mm"], 1)
            pos = oh[:, 8]
            for b in range(TB):
                link(V.scalar_tensor_tensor(pos[:, b], bank[:, 2 + b, 32:36], 1.0, G1[:, b], ALU.add, ALU.mult))
            for r in range(2):
                for b in range(TB):
                    link(V.tensor_scalar(posi[:, 4 * r:4 * r + 4, b], pos[:, b], 1.0 + CAP * r, None, ALU.subtract))
            link(V.tensor_copy(oh[:, 9, 0], bank[:, 2, 64:68]))
            link(V.tensor_reduce(stat[:, 40:41], oh[:, 9, 0], AX, ALU.max))
            link(V.tensor_scalar(stat[:, 41:42], stat[:, 40:41], CAP + 0.5, None, ALU.is_gt))
            link(V.tensor_copy(rounds[:], stat[:, 41:42]))
            dve.sem_inc(S["route_ready"], 1)
            for b in range(TB):
                dve.wait_ge(S["h_hi_s"], b + 1)
                V.tensor_tensor(h_lo[:, b], wide_t[:, b], h_hi[:, b], ALU.subtract).then_inc(S["h_lo_s"], 1)

            def make_perm(i):
                pv = posi[:, bass.ds(i, 1), :].rearrange("p i b -> p (i b)")
                for b in range(TB):
                    ins = V.tensor_scalar(perm_f[:, b], slots[:], pv[:, b:b + 1], None, ALU.is_equal)
                    if b == 0:
                        link(ins)
                ins.then_inc(S["perm_ready"], 1)

            def group(i8, i, g):
                make_perm(i)
                dve.wait_ge(S["comb_mm"], i + 1)
                V.tensor_copy(combg[:], bank[:, 2, 0:4]).then_inc(S["combg_s"], 1)
                for q in range(4):
                    dve.wait_ge(S["ga_hi"], 4 * i + q + 1)
                    V.tensor_tensor(mid_lo[:, q * N:(q + 1) * N], bank[:, 4 + q], mid_hi[:, q * N:(q + 1) * N],
                                    ALU.subtract).then_inc(S["ga_lo"], 1)
                dve.wait_ge(S["combg_s"], i + 1)

                def product(e):
                    dve.wait_ge(S["silu_done"], PER * i + e + 1)
                    dve.wait_ge(unit_done, 8 * i8 + GATE_AT[e] + 16)
                    if e:
                        dve.wait_ge(S["act_t"], PER * i + e)
                    V.scalar_tensor_tensor(prod[:], bank[:, 1], combg[:, e:e + 1], sil[:],
                                           ALU.mult, ALU.mult).then_inc(S["prod_done"], 1)

                def act_split_lo(e):
                    dve.wait_ge(S["act_hi_s"], PER * i + e + 1)
                    V.tensor_tensor(act_lo[:, e % 2], bank[:, 2], act_hi[:, e % 2],
                                    ALU.subtract).then_inc(S["act_lo_s"], 1)

                splits(i8, 0, 16)
                for e in range(1, PER):
                    p = 16 + 24 * (e - 1)
                    hooks = {p + 3: [lambda e=e: product(e - 1)], p + 11: [lambda e=e: act_split_lo(e - 1)]}
                    if e == PER - 1:
                        hooks[p + 19] = [lambda e=e: product(e)]
                        hooks[p + 23] = [lambda e=e: act_split_lo(e)]
                    splits(i8, p, p + 24, hooks)
                splits(i8, 88, 96)
                for q in range(4):
                    dve.wait_ge(S["yg_hi"], 4 * i + q + 1)
                    V.tensor_tensor(y_lo[:, q * N:(q + 1) * N], bank[:, 4 + q], y_hi[:, q * N:(q + 1) * N],
                                    ALU.subtract).then_inc(S["yg_lo"], 1)
                for s in range(8):
                    b, q = s // 4, s % 4
                    dve.wait_ge(S["sc_mm"], 8 * i + s + 1)
                    dst = x2_tok[:, b, q * N:(q + 1) * N]
                    V.tensor_tensor(dst, bank[:, s % 4], dst, ALU.add).then_inc(S["sc_add"], 1)
                dve.wait_ge(S["sc_add"], 8 * i + 8)

            k0 = order.base + order.k
            with dve.Fori(0, GROUPS) as g:
                order.enter(k0 + g)
                group(M8 + 12 * g, g, g)
                assert order.k == 1
            more = dve.value_load(rounds[0:1, 0:1], min_val=0, max_val=1)
            with dve.If(more != 0):
                with dve.Fori(0, GROUPS) as g:
                    order.enter(k0 + GROUPS + g)
                    group(M8 + 12 * GROUPS + 12 * g, GROUPS + g, g)
            dve.wait_ge(S["gl_in"], 16)
            dve.sem_inc(S["moe_done"], 1)
            dve.wait_ge(S["sumsq3"], TB)
            mean_square(3, stat[:, 20:22])
            dve.wait_ge(S["rstd_ready"], 4)
            for b in range(TB):
                V.scalar_tensor_tensor(wide_t[:, b], x2_tok[:, b], rstd[:, 3, b:b + 1], gl_row[:],
                                       ALU.mult, ALU.mult).then_inc(S["y_out"], 1)

        @block.tensor
        def _(pe):
            mm = nc.tensor.matmul

            def gemm(i8, u0, n, lhs, acc, hooks={}, rows=TB, start=True, stop=True, k0=0, kend=None):
                hi, lo = lhs
                for u in range(n):
                    pe.wait_ge(lo_done, 8 * i8 + u0 + u + 1)
                    s = (u0 + u) % SPLIT
                    for j in range(UK):
                        k = k0 + UK * u + j
                        first, last_k = start and u == 0 and j == 0, stop and u == n - 1 and j == UK - 1
                        for b in range(rows):
                            cols = slice(b * P, (b + 1) * P)
                            mm(acc[b], hi[:, k, cols], w_hi[:, s, j], start=first, stop=False)
                            mm(acc[b], hi[:, k, cols], w_lo[:, s, j], start=False, stop=False)
                            last = mm(acc[b], lo[:, k, cols], w_hi[:, s, j], start=False, stop=last_k)
                    last.then_inc(unit_done, 1)
                    for f in hooks.get(u0 + u, ()):
                        f()
                return last

            def acc(p):
                return [bank[:, 2 * p], bank[:, 2 * p + 1]]

            feat = (feat_hi_k, feat_lo_k)
            mid = (mid_hi_k, mid_lo_k)
            yhy = (yhy_hi_k, yhy_lo_k)

            n_const = 13
            pe.wait_ge(S["consts_in"], 16 * n_const)
            pe.wait_ge(S["xr"], TB)
            for q in range(KD // 2):
                if q >= 4:
                    pe.wait_ge(S["xr_lo"], 2 * (q - 4) + 2)
                for j in range(2):
                    for b in range(TB):
                        k = 2 * q + j
                        last = nc.tensor.transpose(bank[:, 4 + q % 4, j * L + b * P:j * L + (b + 1) * P],
                                                   wide_t[:, b, k * P:(k + 1) * P], ident[:])
                last.then_inc(S["xr_t"], 1)
            pe.wait_ge(S["xr_lo"], KD)
            pe.wait_ge(S["filt_in"], 48)
            mm(bank[0:HID, 4, 0:L], w1s[:], zp[:], start=True, stop=True).then_inc(S["f_mm"], 1)
            pe.wait_ge(S["f_sin"], 1)
            mm(bank[:, 4, 0:L], w2s[:], filt_a[0:HID], start=True, stop=True).then_inc(S["f_mm"], 1)

            for c in range(4):
                if c >= 2:
                    pe.wait_ge(S["biased"], c - 1)
                gemm(A8 + c, 0, 8, feat, acc(c % 2))

            def sgu_mix():
                pe.wait_ge(S["ln_done"], TB)
                pe.wait_ge(S["f_arg"], 2)
                for g in range(8):
                    last = mm(bank[:, 4 + g // 2, (g % 2) * L:(g % 2 + 1) * L].rearrange("p (b k) -> p b k", b=TB),
                              sgw[:, g], wide_t[:, :, W + g * P:W + (g + 1) * P], start=True, stop=True)
                last.then_inc(S["mix_done"], 1)

            def sgu_transpose():
                pe.wait_ge(S["ysg"], 8)
                for k in range(CT):
                    for b in range(TB):
                        last = nc.tensor.transpose(bank[:, 4 + k // 2, (k % 2) * L + b * P:(k % 2) * L + (b + 1) * P],
                                                   wide_t[:, b, k * P:(k + 1) * P], ident[:])
                last.then_inc(S["ysg_t"], 1)

            def z_transpose(c):
                pe.wait_ge(S["zt_ready"], c + 1)
                if isinstance(c, int) and c == 0:
                    pe.wait_ge(S["ysg_lo"], 4)
                else:
                    pe.wait_ge(S["zpad_ready"], c)
                for j in range(4):
                    for b in range(TB):
                        last = nc.tensor.transpose(bank[:, 4 + j // 2, (j % 2) * L + b * P:(j % 2) * L + (b + 1) * P],
                                                   zt[:, b, j * P:(j + 1) * P], ident[:])
                last.then_inc(S["z_t"], 1)

            pe.wait_ge(S["biased"], 3)
            gemm(B8, 0, 8, feat, acc(0), {7: [sgu_mix]})
            pe.wait_ge(S["biased"], 4)
            gemm(B8 + 1, 0, 8, feat, acc(1), {1: [sgu_transpose], 5: [lambda: z_transpose(0)]})
            with pe.Fori(1, 3) as h:
                for p in range(2):
                    pe.wait_ge(S["zt_ready"], 2 * h + p - 1)
                    gemm(B8 + 2 * h + p, 0, 8, feat, acc(p), {5: [lambda: z_transpose(2 * h + p - 1)]})
            z_transpose(5)

            def v_transpose(o):
                pe.wait_ge(S["ot_ready"], 2 * o + 1)
                for q in range(4):
                    c, b = 4 * (q // 2), q % 2
                    for j in range(4):
                        last = nc.tensor.transpose(bank[:, 4 + q, j * P:(j + 1) * P],
                                                   vt_c[:, c + j, b * P:(b + 1) * P], ident[:])
                    last.then_inc(S["v_t"], 1)

            def filt(s, o, h):
                pe.wait_ge(S["h3_in_%d" % h], 64 * o + 64)
                if h == 0:
                    pe.wait_ge(S["vtok_ready"], 4 * o + 4)
                else:
                    pe.wait_ge(S["ot_ready"], 2 * o + 2)
                for d in range(2):
                    for b in range(TB):
                        last = mm(bank[:, 4 + 2 * d + b], a2[:, d, b * P:(b + 1) * P], w3s[:], start=True, stop=True)
                last.then_inc(S["filt_mm"], 1)

            def transform(rhs_c, rhs_s):
                for f in range(4):
                    rhs = rhs_c if f < 2 else rhs_s
                    for b in range(TB):
                        last = mm(bank[:, 4 + f], dft_f[:, b, f * P:(f + 1) * P], rhs[b], start=b == 0, stop=b == TB - 1)
                return last

            def response(s):
                pe.wait_ge(S["hsd_ready"], s + 1)
                pe.wait_ge(S["tables_in"], 32)
                transform([prod_y[:, 0], prod_y[:, 1]], [prod_y[:, 2], prod_y[:, 3]]).then_inc(S["k_mm"], 1)

            def spectrum(s, h):
                pe.wait_ge(S["k_ready"], s + 1)
                v = [v_tok[:, b, h * N:(h + 1) * N] for b in range(TB)]
                transform(v, v).then_inc(S["u_mm"], 1)

            def inverse(s):
                pe.wait_ge(S["y_ready"], s + 1)
                for j in range(4):
                    for f in range(4):
                        last = mm(bank[:, 4 + j // 2, (j % 2) * L:(j % 2 + 1) * L], prod_y[:, f, j * P:(j + 1) * P],
                                  dft_i[:, f], start=f == 0, stop=f == 3)
                last.then_inc(S["inv_mm"], 1)

            def turn(i8, n0, o, proj, hooks):
                pe.wait_ge(S["biased"], n0 + 4)
                gemm(i8, 0, 8, feat, acc(0), hooks)
                pe.wait_ge(S["merged_ready"], n0 + 1)
                gemm(i8, 8, 4, proj, acc(1), hooks)
                pe.wait_ge(S["biased"], n0 + 5)
                gemm(i8, 12, 8, feat, acc(0), hooks)
                pe.wait_ge(S["merged_ready"], n0 + 2)
                gemm(i8, 20, 4, proj, acc(1), hooks)

            pe.wait_ge(S["zt_ready"], 6)
            pe.wait_ge(S["ysg_lo"], 4)
            with pe.Fori(0, 2) as o:
                turn(C8 + 3 * o, 2 * o, o, mid, {
                    0: [lambda: v_transpose(o)],
                    2: [lambda: filt(2 * o, o, 0)],
                    4: [lambda: response(2 * o)],
                    6: [lambda: spectrum(2 * o, 0)],
                    10: [lambda: inverse(2 * o)],
                    12: [lambda: filt(2 * o + 1, o, 1)],
                    14: [lambda: response(2 * o + 1)],
                    15: [lambda: spectrum(2 * o + 1, 1)],
                    19: [lambda: inverse(2 * o + 1)]})
            pe.wait_ge(S["yhy_lo_s"], 1)
            with pe.Fori(0, 2) as o:
                turn(D8 + 3 * o, 4 + 2 * o, o, yhy, {})
            pe.wait_ge(S["merged_ready"], 9)
            for q in range(KD // 2):
                if q >= 4:
                    pe.wait_ge(S["m_lo"], q - 3)
                for j in range(2):
                    for b in range(TB):
                        k = 2 * q + j
                        last = nc.tensor.transpose(bank[:, 4 + q % 4, j * L + b * P:j * L + (b + 1) * P],
                                                   wide_t[:, b, k * P:(k + 1) * P], ident[:])
                last.then_inc(S["m_t"], 1)
            pe.wait_ge(S["m_lo"], KD // 2)
            gemm(E8, 0, 8, feat, acc(0))
            with pe.Fori(1, 4) as c:
                pe.wait_ge(S["x_mid"], c)
                gemm(E8 + c, 0, 8, feat, acc(0))

            pe.wait_ge(S["h_ready"], TB)
            for q in range(KD // 2):
                if q >= 4:
                    pe.wait_ge(S["h_ev_dve" if q % 2 else "h_ev_act"], (q - 4) // 2 + 1)
                for j in range(2):
                    for b in range(TB):
                        k = 2 * q + j
                        last = nc.tensor.transpose(bank[:, 4 + q % 4, j * L + b * P:j * L + (b + 1) * P],
                                                   wide_t[:, b, k * P:(k + 1) * P], ident[:])
                last.then_inc(S["h_tr"], 1)
            pe.wait_ge(S["h_ev_act"], KD // 4)
            pe.wait_ge(S["h_ev_dve"], KD // 4)
            for b in range(TB):
                for k in range(KD):
                    last = mm(bank[:, 2 + b, 0:20], h_t[:, k, b * P:(b + 1) * P], wr[:, k], start=k == 0, stop=k == KD - 1)
                last.then_inc(S["r_mm"], 1)
            pe.wait_ge(S["oh_ready"], 1)
            mm(bank[:, 2, 32:36], before[:], oh[:, 2, 0], start=True, stop=True)
            mm(bank[:, 3, 32:36], ones[:], oh[:, 2, 0], start=True, stop=False)
            mm(bank[:, 3, 32:36], before[:], oh[:, 2, 1], start=False, stop=True)
            mm(bank[:, 2, 64:68], ones[:], oh[:, 2, 0], start=True, stop=False)
            mm(bank[:, 2, 64:68], ones[:], oh[:, 2, 1], start=False, stop=True).then_inc(S["pos_mm"], 1)
            pe.wait_ge(S["route_ready"], 1)
            pe.wait_ge(S["h_lo_s"], TB)

            def group(i8, i, g):
                pe.wait_ge(S["perm_ready"], i + 1)
                for b in range(TB):
                    last = nc.tensor.transpose(bank[:, 3, b * P:(b + 1) * P], perm_f[:, b], ident[:])
                last.then_inc(S["perm_tr"], 1)
                pe.wait_ge(S["perm_r"], i + 1)
                for b in range(TB):
                    mm(bank[:, 2, 0:4], perm[:, b], comb_hi[:, b], start=b == 0, stop=False)
                    last = mm(bank[:, 2, 0:4], perm[:, b], comb_lo[:, b], start=False, stop=b == TB - 1)
                last.then_inc(S["comb_mm"], 1)
                for q in range(4):
                    for kk in range(4):
                        k = 4 * q + kk
                        dst = bank[:, 4 + q, kk * CAP:(kk + 1) * CAP]
                        for b in range(TB):
                            mm(dst, h_hi[:, b, k * P:(k + 1) * P], perm[:, b], start=b == 0, stop=False)
                            last = mm(dst, h_lo[:, b, k * P:(k + 1) * P], perm[:, b], start=False, stop=b == TB - 1)
                    last.then_inc(S["ga_mm"], 1)
                pe.wait_ge(S["ga_lo"], 4 * i + 4)
                pe.wait_ge(S["combg_s"], i + 1)

                def gate(e):
                    if e:
                        pe.wait_ge(S["silu_done"], PER * i + e)
                    gemm(i8, GATE_AT[e], 8, (xg_hi, xg_lo), [bank[:, 0]], rows=1)

                def up(e):
                    if e:
                        pe.wait_ge(S["prod_done"], PER * i + e)
                    gemm(i8, GATE_AT[e] + 8, 8, (xg_hi, xg_lo), [bank[:, 1]], rows=1)

                def act_transpose(e):
                    pe.wait_ge(S["prod_done"], PER * i + e + 1)
                    if e:
                        pe.wait_ge(S["act_lo_s"], PER * i + e)
                    for k in range(4):
                        last = nc.tensor.transpose(bank[:, 2, k * P:(k + 1) * P], prod[:, k * P:(k + 1) * P], ident[:])
                    last.then_inc(S["act_t"], 1)

                def down(e, hooks={}):
                    pe.wait_ge(S["act_lo_s"], PER * i + e + 1)
                    for c in range(4):
                        gemm(i8, DOWN_AT[e] + 2 * c, 2,
                             (act_hi[:, e % 2].rearrange("p (k s) -> p k s", k=4),
                              act_lo[:, e % 2].rearrange("p (k s) -> p k s", k=4)),
                             [bank[:, 4 + c]], hooks, rows=1, start=e == 0, stop=e == PER - 1)

                gate(0)
                up(0)
                for e in range(1, PER):
                    gate(e)
                    act_transpose(e - 1)
                    up(e)
                    down(e - 1, {DOWN_AT[e - 1] + 5: [lambda e=e: act_transpose(e)]} if e == PER - 1 else {})
                down(PER - 1)
                pe.wait_ge(S["perm_t_s"], i + 1)
                pe.wait_ge(S["yg_lo"], 4 * i + 4)
                for s in range(8):
                    b, q = s // 4, s % 4
                    if s >= 4:
                        pe.wait_ge(S["sc_add"], 8 * i + s - 3)
                    mm(bank[:, s % 4], perm_t[:, b * P:(b + 1) * P], y_hi[:, q * N:(q + 1) * N], start=True, stop=False)
                    mm(bank[:, s % 4], perm_t[:, b * P:(b + 1) * P], y_lo[:, q * N:(q + 1) * N], start=False,
                       stop=True).then_inc(S["sc_mm"], 1)
                pe.wait_ge(S["sc_add"], 8 * i + 8)

            with pe.Fori(0, GROUPS) as g:
                group(M8 + 12 * g, g, g)
            more = pe.value_load(rounds[0:1, 0:1], min_val=0, max_val=1)
            with pe.If(more != 0):
                with pe.Fori(0, GROUPS) as g:
                    group(M8 + 12 * GROUPS + 12 * g, GROUPS + g, g)


def tables():
    import numpy as np
    f32 = np.float32
    t = np.linspace(0.0, 1.0, L, dtype=f32)[:, None]
    bands = np.linspace(1e-4, (EMB - 1) // 2 - 1, (EMB - 1) // 2, dtype=f32)
    w = (f32(2.0 * math.pi / L) * np.arange(L, dtype=f32))[:, None]
    z = np.concatenate([t, np.cos(bands * w), -np.sin(bands * w)], axis=-1).astype(f32)
    deltas = np.abs(np.linspace(math.log(1e-2) / 1.5, math.log(1e-2) / 0.3, W, dtype=f32))
    decay = np.exp(-t * deltas).astype(f32)
    angle = np.outer(np.arange(L), 2 * np.arange(L) + 1) * (2.0 * math.pi / (4 * L))
    f = np.concatenate([np.cos(angle), np.sin(angle)], axis=1)
    row = np.arange(P)
    return {
        "zpos": np.ascontiguousarray(z.T),
        "decay": np.ascontiguousarray(decay.reshape(TB, P, W).transpose(1, 0, 2)),
        "dft": np.ascontiguousarray(f.astype(f32).reshape(TB, P, 2 * L).transpose(1, 0, 2)),
        "idft": np.ascontiguousarray((f.T / L).astype(f32).reshape(4, P, L).transpose(1, 0, 2)),
        "ident_in": np.eye(P, dtype=f32),
        "before_in": (row[:, None] < row[None, :]).astype(f32),
        "ones_in": np.ones((P, P), f32),
        "slots_in": np.ascontiguousarray(np.broadcast_to(np.arange(CAP, dtype=f32), (P, CAP))),
        "rank_in": np.ascontiguousarray(np.broadcast_to(np.arange(4, 0, -1, dtype=f32), (P, TB, 4))),
    }


def kernel(**inputs):
    import numpy as np
    import concourse.bacc as bacc
    from concourse.bass_utils import run_bass_kernel_spmd as run

    a = {k: np.asarray(v) for k, v in inputs.items()}

    def cols(v, order=None):
        m = v.reshape(-1, P).T
        return m if order is None else m[:, order]

    vfirst = list(range(2 * CT, 3 * CT)) + list(range(2 * CT))
    laid = {n: a[n] for n in ("x", "w_in", "w_hy_out", "w_sg_out", "w_out", "w_gate", "w_up", "w_down", "b_in",
                              "filt_w3", "hy_skip")}
    laid.update(
        ln_g=a["sg_ln_g"], ln_b=a["sg_ln_b"], g_ffn=a["g_ffn"], g_final=a["g_final"][None],
        b_router=np.tile(np.concatenate([a["b_rg"][0], a["b_re"][0].reshape(-1)])[None], (1, TB)).reshape(1, TB, 20),
        g_mix_c=cols(a["g_mix"][0]),
        conv_w_c=np.stack([cols(a["conv_w"][0, j], vfirst) for j in range(3)], axis=-1),
        conv_b_c=cols(a["conv_b"][0], vfirst),
        b_hy_c=cols(a["b_in"][0, :3 * W], vfirst),
        filt_w1=a["filt_w1"],
        filt_w2=np.concatenate([a["filt_w2"][0]] * 2, axis=1),
        filt_vec=np.stack([np.tile(a["filt_freq"][0], 2), np.tile(a["filt_b1"][0], 2), np.tile(a["filt_b2"][0], 2),
                           np.repeat(np.array([1.0, -1.0], np.float32), HID)], axis=1),
        sg_w_t=a["sg_w"][0].transpose(2, 0, 1),
        sg_b_t=a["sg_b"][0].T,
        w_router=np.concatenate([a["w_rg"][0], a["w_re"][0].transpose(1, 0, 2).reshape(D, -1)], axis=1)
        .reshape(KD, P, 20).transpose(1, 0, 2))
    laid.update(tables())

    nc = bacc.Bacc("TRN2", target_bir_lowering=False, num_devices=1)
    arrays, args = {}, {}
    for name, v in laid.items():
        v = np.ascontiguousarray(v)
        arrays["in_" + name] = v
        args[name] = nc.dram_tensor("in_" + name, v.shape, mybir.dt.from_np(v.dtype), kind="ExternalInput").ap()
    args["out"] = nc.dram_tensor("out_0", (1, L, D), F32, kind="ExternalOutput").ap()
    build(nc, **args)
    r = run(nc, [arrays], core_ids=[0])
    return r.results[0]["out_0"]
```

```python
import math
from contextlib import ExitStack

import concourse.bass as bass
from concourse import mybir

F32 = mybir.dt.float32
F32R = mybir.dt.float32r
I32 = mybir.dt.int32
ACT = mybir.ActivationFunctionType
ALU = mybir.AluOpType
AX = mybir.AxisListType.X

P = 128
L = 256
TB = L // P
D = 2048
KD = D // P
W = D // 2
CT = W // P
N = 512
HALVES = W // N
C_U = 3 * W
C_GHY = 5 * W
C_GSG = 7 * W
EMB, HID = 33, 64
GROUPS, PER = 4, 4
FE = D // 4
CAP = 128
EPS = 1e-6
UK = 2
RAW, SPLIT = 8, 4
MAGIC = 1.5 * 2.0 ** 23
PI_HI = 6.28125
PI_LO = 2.0 * math.pi - PI_HI

GATHER_AT, GATHER_BANK = [81, 84, 87, 90], [3, 0, 1, 3]
GATE_AT = [0] + [16 + 24 * e for e in range(PER - 1)]
DOWN_AT = [32 + 24 * e for e in range(PER - 1)] + [88]
A8, B8, C8, D8, E8, M8 = 0, 4, 10, 16, 22, 26


def static_le(value, bound):
    return isinstance(value, int) and value <= bound


def build(nc, x, w_in, w_hy_out, w_sg_out, w_out, w_gate, w_up, w_down, b_in, filt_w3, hy_skip,
          ln_g, ln_b, g_ffn, g_final, b_router,
          g_mix_c, conv_w_c, conv_b_c, b_hy_c, filt_w1, filt_w2, filt_vec, sg_w_t, sg_b_t, w_router,
          zpos, decay, dft, idft, ident_in, before_in, ones_in, slots_in, rank_in, out):
    ctx = ExitStack()
    with ctx:
        def sb(name, shape, dt=F32):
            return ctx.enter_context(nc.sbuf_tensor(name, shape, dt))

        def sem(name):
            return ctx.enter_context(nc.semaphore(name))

        def region(name, words, *layouts):
            made = []
            for layout in layouts:
                with ExitStack() as sub:
                    made.append([sub.enter_context(nc.sbuf_tensor(n, s, d)) for n, s, d in layout])
            sb(name, [P, words])
            return made

        raw = sb("raw", [P, RAW, UK, N])
        w_hi = sb("w_hi", [P, SPLIT, UK, N], F32R)
        w_lo = sb("w_lo", [P, SPLIT, UK, N], F32R)
        feat_hi = sb("feat_hi", [P, KD * L], F32R)
        feat_lo = sb("feat_lo", [P, KD * L], F32R)
        mid_hi = sb("mid_hi", [P, CT * L], F32R)
        mid_lo = sb("mid_lo", [P, CT * L], F32R)
        wide = sb("wide", [P, TB * D])
        ident = sb("ident", [P, P])
        before = sb("before", [P, P])
        ones = sb("ones", [P, P])
        slots = sb("slots", [P, CAP])
        rank = sb("rank", [P, TB, 4])
        bias = sb("bias", [P, 2, N])
        conv_w = sb("conv_w", [P, 3 * CT, 3])
        conv_b = sb("conv_b", [P, 3 * CT])
        b_hy = sb("b_hy", [P, 3 * CT])
        g_mix = sb("g_mix", [P, KD])
        fvec = sb("fvec", [P, 4])
        sgb = sb("sgb", [P, CT])
        wr = sb("wr", [P, KD, 20])
        brt = sb("brt", [P, TB, 20])
        stat = sb("stat", [P, 64])
        var = sb("var", [P, 4, TB])
        rstd = sb("rstd", [P, 4, TB])
        minus_half = sb("minus_half", [P, TB])

        (x_tok,), (prod_y, k_resp), (zt, zpad), (x2_tok,) = region(
            "region_x", TB * D,
            [("x_tok", [P, TB, D], F32)],
            [("prod_y", [P, 4, N], F32), ("k_resp", [P, 4, N], F32)],
            [("zt", [P, TB, N], F32), ("zpad", [P, 4, L + 2], F32)],
            [("x2_tok", [P, TB, D], F32)])
        (z_all, v_tok), (_, yhy_hi, yhy_lo), (gf_row, h_t), moe = region(
            "region_z", 4 * CT * L,
            [("z_all", [P, 3, CT * L], F32), ("v_tok", [P, TB, W], F32)],
            [("skip_v", [P, CT * L], F32), ("yhy_hi", [P, CT * L], F32R), ("yhy_lo", [P, CT * L], F32R)],
            [("gf_row", [P, D], F32), ("h_t", [P, KD, L], F32)],
            [("sil", [P, N], F32), ("prod", [P, N], F32), ("perm", [P, TB, CAP], F32),
             ("perm_t", [P, TB * CAP], F32R), ("skip_m", [P, 2 * L], F32),
             ("y_hi", [P, D], F32R), ("y_lo", [P, D], F32R),
             ("act_hi", [P, 2, N], F32R), ("act_lo", [P, 2, N], F32R)])
        sil, prod, perm, perm_t, _, y_hi, y_lo, act_hi, act_lo = moe
        (dft_f, dft_i, dec, w3s, hp_skip), (lng, lnb, sgw), filt_mem, (gl_row,) = region(
            "region_t", 8 * N,
            [("dft_f", [P, TB, N], F32), ("dft_i", [P, 4, L], F32), ("dec", [P, TB, N], F32), ("w3s", [P, N], F32),
             ("hp_skip", [1, N], F32)],
            [("lng", [P, W], F32), ("lnb", [P, W], F32), ("sgw", [P, 8, P], F32)],
            [("filt_a", [P, L], F32), ("filt_b", [P, L], F32), ("filt_c", [P, L], F32), ("w1s", [EMB, HID], F32),
             ("w2s", [HID, P], F32), ("zp", [EMB, L], F32)],
            [("gl_row", [P, D], F32)])
        filt_a, filt_b, filt_c, w1s, w2s, zp = filt_mem
        vt = z_all[:, 0]
        a2 = sb("a2", [P, 2, L])
        sig = sb("sig", [P, TB, N])
        oh = sb("oh", [P, 12, TB, 4])
        posi = sb("posi", [P, 9, TB])
        comb = sb("comb", [P, TB, 4])
        combg = sb("combg", [P, 4])
        lesel = sb("lesel", [P, TB, 16])
        logits = sb("logits", [P, TB, 20])
        rounds = sb("rounds", [P, 1], I32)
        bank = ctx.enter_context(nc.psum_tensor("bank", [P, 8, N], F32))

        ld = [sem(f"weights_loaded_{i}") for i in range(RAW)]
        hi_done, lo_done, unit_done = sem("hi_done"), sem("lo_done"), sem("unit_done")
        bias_in = [sem("bias_in_0"), sem("bias_in_1")]
        S = {n: sem(n) for n in (
            "a2_ready", "act_hi_s", "act_lo_s", "act_order", "act_t", "biased", "comb_mm", "combg_s", "consts_in",
            "conv_done", "dve_order", "f_arg", "f_mm", "f_sin", "filt_in", "filt_mm", "ga_hi", "ga_lo", "ga_mm",
            "gelu_done", "gf_in", "gl_in", "h3_in_0", "h3_in_1", "h_ev_act", "h_ev_dve", "h_ready", "h_tr",
            "h_norm", "half_in", "hsd_ready", "inv_mm", "k_mm", "k_ready", "ln_done", "m_hi", "m_lo", "m_t", "merged_ready",
            "mix_done", "moe_done", "oh_ready", "ot_ready", "out_done", "perm_ready", "perm_t_s",
            "perm_tr", "pos_mm", "prod_done", "r_exp", "r_exp2", "r_log", "r_m12", "r_mm", "route_ready",
            "rstd_ready", "sc_add", "sc_mm", "sg_in", "sig_ready", "silu_done", "sumsq", "sumsq2", "sumsq3",
            "tables_in", "u_mm", "v_t", "var_ready", "vtok_ready", "x_again", "x_in", "x_mid", "xr", "xr_hi",
            "xr_lo", "xr_t", "y_out", "y_ready", "yg_hi", "yg_lo", "yhy_hi_s", "yhy_lo_s", "ysg", "ysg_hi", "ysg_lo",
            "ysg_t", "z_t", "zpad_ready", "zt_ready")}

        class Order:
            def __init__(self, eng, s):
                self.eng, self.s, self.base, self.k = eng, s, 0, 0

            def link(self, ins):
                ins.then_inc(self.s, 1)
                self.k += 1
                self.eng.wait_ge(self.s, self.base + self.k)

            def enter(self, base):
                self.base, self.k = base, 0

        feat_hi_k = feat_hi[:].rearrange("p (k t) -> p k t", k=KD)
        feat_lo_k = feat_lo[:].rearrange("p (k t) -> p k t", k=KD)
        mid_hi_k = mid_hi[:].rearrange("p (k t) -> p k t", k=CT)
        mid_lo_k = mid_lo[:].rearrange("p (k t) -> p k t", k=CT)
        yhy_hi_k = yhy_hi[:].rearrange("p (k t) -> p k t", k=CT)
        yhy_lo_k = yhy_lo[:].rearrange("p (k t) -> p k t", k=CT)
        xg_hi = mid_hi[:].rearrange("p (k s) -> p k s", k=KD)
        xg_lo = mid_lo[:].rearrange("p (k s) -> p k s", k=KD)
        wide_t = wide[:].rearrange("p (b d) -> p b d", b=TB)
        vt_c = vt.rearrange("p (c t) -> p c t", c=CT)
        z_flat = z_all[:].rearrange("p r n -> p (r n)")

        def pair(c):
            return bank[:, 2 * (c % 2):2 * (c % 2) + 2, :]

        block = ctx.enter_context(nc.Block())

        @block.sync
        def _(sp):
            def load(idx8, u, src):
                n = 8 * idx8 + u - RAW + 1
                if not static_le(n, 0):
                    sp.wait_ge(lo_done, n)
                sp.dma_start(raw[:, u % RAW], src).then_inc(ld[u % RAW], 16)

            def rows(w):
                return w.rearrange("(u j p) n -> u p j n", j=UK, p=P)

            win, why, wsg, wo = rows(w_in[0]), rows(w_hy_out[0]), rows(w_sg_out[0]), rows(w_out[0])
            for b in range(TB):
                sp.dma_start(x_tok[:, b], x[0, b * P:(b + 1) * P]).then_inc(S["x_in"], 16)

            def bias_chunk(k, col):
                sp.dma_start(bias[:, k], b_in[0:1, bass.ds(col, N)].partition_broadcast(P)).then_inc(bias_in[k], 16)

            for c in range(4):
                if c >= 2:
                    sp.wait_ge(S["biased"], c - 1)
                bias_chunk(c % 2, C_U + c * N)
                for u in range(8):
                    load(A8 + c, u, win[u, :, :, C_U + c * N:C_U + (c + 1) * N])
            for c in range(2):
                for u in range(8):
                    load(B8 + c, u, win[u, :, :, 2 * W + c * N:2 * W + (c + 1) * N])
            with sp.Fori(2, 6) as c:
                for u in range(8):
                    load(B8 + c, u, win[u, :, :, bass.ds((c - 2) * N, N)])

            def gate_turns(p8, col, proj, biased):
                with sp.Fori(1, 3) as o:
                    for h in range(2):
                        sp.wait_ge(S["biased"], 2 * o + (biased + h - 3))
                        at = sp.snap((2 * o + h) * N)
                        bias_chunk(h, at + (col - 2 * N))
                        for u in range(8):
                            load(p8 - 3 + 3 * o, 12 * h + u, win[u, :, :, bass.ds(at + (col - 2 * N), N)])
                        for u in range(4):
                            load(p8 - 3 + 3 * o, 12 * h + 8 + u, proj[u, :, :, bass.ds(at - 2 * N, N)])

            gate_turns(C8, C_GSG, wsg, 4)
            gate_turns(D8, C_GHY, why, 8)
            sp.wait_ge(S["ot_ready"], 5)
            for b in range(TB):
                sp.dma_start(x2_tok[:, b], x[0, b * P:(b + 1) * P]).then_inc(S["x_again"], 16)
            with sp.Fori(0, 4) as c:
                for u in range(8):
                    load(E8 + c, u, wo[u, :, :, bass.ds(c * N, N)])

            def expert(i8, pos, e, kinds):
                for kind in kinds:
                    if kind in "gu":
                        w = (w_gate if kind == "g" else w_up)[0]
                        for u in range(8):
                            src = w[bass.ds(e, 1), u * UK * P:(u + 1) * UK * P, :].rearrange(
                                "e (j p) n -> p (e j) n", p=P)
                            load(i8, pos, src)
                            pos += 1
                    else:
                        for c in range(4):
                            for u in range(2):
                                src = w_down[0][bass.ds(e, 1), u * UK * P:(u + 1) * UK * P,
                                                c * N:(c + 1) * N].rearrange("e (j p) n -> p (e j) n", p=P)
                                load(i8, pos, src)
                                pos += 1
                return pos

            def group(i8, g):
                pos = expert(i8, 0, g * PER, "gu")
                for e in range(1, PER):
                    pos = expert(i8, pos, g * PER + e, "gu")
                    pos = expert(i8, pos, g * PER + e - 1, "d")
                assert expert(i8, pos, g * PER + PER - 1, "d") == 96

            with sp.Fori(0, GROUPS) as g:
                group(M8 + 12 * g, g)
            sp.wait_ge(S["route_ready"], 1)
            more = sp.value_load(rounds[0:1, 0:1], min_val=0, max_val=1)
            with sp.If(more != 0):
                with sp.Fori(0, GROUPS) as g:
                    group(M8 + 12 * GROUPS + 12 * g, g)
            for b in range(TB):
                sp.wait_ge(S["y_out"], b + 1)
                sp.dma_start(out[0, b * P:(b + 1) * P], wide_t[:, b]).then_inc(S["out_done"], 16)
            sp.wait_ge(S["out_done"], 16 * TB)

        @block.gpsimd
        def _(pool):
            pool.memset(minus_half[:], -0.5).then_inc(S["half_in"], 1)
            pool.wait_ge(S["half_in"], 1)
            for n in range(4):
                pool.wait_ge(S["var_ready"], n + 1)
                pool.tensor_tensor(rstd[:, n], var[:, n], minus_half[:], ALU.pow).then_inc(S["rstd_ready"], 1)

        @block.scalar
        def _(act):
            order = Order(act, S["act_order"])

            def split_hi(i8, u, nxt=None):
                act.wait_ge(ld[u % RAW], 16 * (i8 + u // RAW) + 16)
                n = 8 * i8 + u - SPLIT + 1
                if not static_le(n, 0):
                    act.wait_ge(unit_done, n)
                nc.scalar.activation(w_hi[:, u % SPLIT], raw[:, u % RAW], ACT.Copy).then_inc(hi_done, 1)

            def splits(i8, lo_, hi_, hooks={}):
                for u in range(lo_, hi_):
                    split_hi(i8, u)
                    for f in hooks.get(u, ()):
                        f()

            for dst, src in ((ident, ident_in), (g_mix, g_mix_c), (conv_w, conv_w_c), (conv_b, conv_b_c),
                             (b_hy, b_hy_c), (fvec, filt_vec), (before, before_in), (ones, ones_in),
                             (slots, slots_in), (rank, rank_in), (sgb, sg_b_t), (wr, w_router)):
                act.dma_start(dst[:], src).then_inc(S["consts_in"], 16)
            n_const = 12
            act.dma_start(brt[:], b_router.partition_broadcast(P)).then_inc(S["consts_in"], 16)
            n_const += 1
            for dst, src in ((w1s, filt_w1[0]), (w2s, filt_w2), (zp, zpos)):
                act.dma_start(dst[:], src).then_inc(S["filt_in"], 16)

            act.wait_ge(S["x_in"], 16 * TB)
            for b in range(TB):
                nc.scalar.activation(wide_t[:, b], x_tok[:, b], ACT.Square,
                                     accum_out=stat[:, b:b + 1]).then_inc(S["sumsq"], 1)
            act.wait_ge(S["rstd_ready"], 1)
            for b in range(TB):
                nc.scalar.activation(wide_t[:, b], x_tok[:, b], ACT.Copy,
                                     scale=rstd[:, 0, b:b + 1]).then_inc(S["xr"], 1)
            act.wait_ge(S["consts_in"], 16 * n_const)
            for q in range(KD // 2):
                act.wait_ge(S["xr_t"], q + 1)
                for j in range(2):
                    k = 2 * q + j
                    ins = nc.scalar.activation(feat_hi_k[:, k], bank[:, 4 + q % 4, j * L:(j + 1) * L], ACT.Copy,
                                               scale=g_mix[:, k:k + 1])
                    ins.then_inc(S["xr_hi"], 1)

            def gelu(c):
                act.wait_ge(S["biased"], c + 1)
                nc.scalar.activation(wide_t[:, 0:2, bass.ds(c * N, N)], wide_t[:, 0:2, bass.ds(c * N, N)],
                                     ACT.Gelu).then_inc(S["gelu_done"], 1)

            def filter_sine(n, dst):
                act.wait_ge(S["f_arg"], n)
                nc.scalar.activation(dst, filt_c[0:HID if n == 1 else P], ACT.Sin).then_inc(S["f_sin"], 1)

            filter_sine(1, filt_a[0:HID])
            filter_sine(2, a2[:, 0])
            def z_evac(c, parity):
                act.wait_ge(unit_done, 8 * (B8 + c) + 8)
                nc.scalar.activation(zt[:], pair(parity), ACT.Copy).then_inc(S["zt_ready"], 1)

            def z_bias(c):
                act.wait_ge(S["z_t"], c + 1)
                if not static_le(c, 0):
                    act.wait_ge(S["conv_done"], c)
                for j in range(4):
                    ins = nc.scalar.activation(zpad[:, j, 1:L + 1], bank[:, 4 + j // 2, (j % 2) * L:(j % 2 + 1) * L],
                                               ACT.Identity, bias=b_hy[:, bass.ds(4 * c + j, 1)])
                ins.then_inc(S["zpad_ready"], 1)

            def mix_evac_hi():
                act.wait_ge(S["ysg_t"], 1)
                for q in range(4):
                    nc.scalar.activation(mid_hi[:, q * N:(q + 1) * N], bank[:, 4 + q], ACT.Copy).then_inc(S["ysg_hi"], 1)

            def ln_load():
                act.wait_ge(S["a2_ready"], 1)
                act.dma_start(lng[:], ln_g.partition_broadcast(P)).then_inc(S["sg_in"], 16)
                act.dma_start(lnb[:], ln_b.partition_broadcast(P)).then_inc(S["sg_in"], 16)
                act.dma_start(sgw[:], sg_w_t).then_inc(S["sg_in"], 16)

            def table_load():
                act.wait_ge(S["mix_done"], 1)
                act.dma_start(dft_f[:], dft).then_inc(S["tables_in"], 16)
                act.dma_start(dft_i[:], idft).then_inc(S["tables_in"], 16)

            splits(A8, 0, 52, {
                7: [ln_load], 12: [lambda: gelu(0)], 20: [lambda: gelu(1)], 28: [lambda: gelu(2)],
                36: [lambda: gelu(3)], 43: [lambda: z_evac(0, 0)], 45: [lambda: z_bias(0)],
                49: [table_load], 51: [lambda: z_evac(1, 1), mix_evac_hi]})
            with act.Fori(1, 3) as h:
                for p in range(2):
                    splits(B8 + 2 * h + p, 4, 12, {6: [lambda: z_bias(2 * h + p - 1)],
                                                   11: [lambda: z_evac(2 * h + p, p)]})
            z_bias(5)

            def h3_load(o, h):
                w3v = filt_w3[0].rearrange("h (d o n) -> d h o n", d=2, o=2)
                for d in range(2):
                    act.dma_start(w3s[d * HID:(d + 1) * HID, :],
                                  w3v[d, :, bass.ds(o, 1), h * N:(h + 1) * N].rearrange("h o n -> h (o n)")
                                  ).then_inc(S[f"h3_in_{h}"], 16)
                act.dma_start(dec[:], decay[:, :, h * N:(h + 1) * N]).then_inc(S[f"h3_in_{h}"], 16)
                act.dma_start(hp_skip[:], hy_skip[0, bass.ds(o, 1), h * N:(h + 1) * N]).then_inc(S[f"h3_in_{h}"], 16)

            def v_evac(o):
                for q in range(4):
                    act.wait_ge(S["v_t"], 4 * o + q + 1)
                    c, b = 4 * (q // 2), q % 2
                    nc.scalar.activation(v_tok[:, b, c * P:(c + 4) * P], bank[:, 4 + q], ACT.Copy
                                         ).then_inc(S["vtok_ready"], 1)

            def k_evac(s):
                act.wait_ge(S["k_mm"], s + 1)
                for q in range(2):
                    ins = nc.scalar.activation(k_resp[:, 2 * q:2 * q + 2], bank[:, 4 + 2 * q:6 + 2 * q], ACT.Copy)
                ins.then_inc(S["k_ready"], 1)

            def sigmoid(n):
                act.wait_ge(S["biased"], n + 5)
                nc.scalar.activation(sig[:], sig[:], ACT.Sigmoid).then_inc(S["sig_ready"], 1)

            def next_h3(s, o, h):
                act.wait_ge(S["hsd_ready"], s + 1)
                h3_load(o, h)

            h3_load(0, 0)
            with act.Fori(0, 2) as o:
                splits(C8 + 3 * o, 4, 28, {
                    5: [lambda: v_evac(o)],
                    8: [lambda: next_h3(2 * o, o, 1)],
                    9: [lambda: k_evac(2 * o)],
                    11: [lambda: sigmoid(2 * o)],
                    20: [lambda: k_evac(2 * o + 1)],
                    23: [lambda: sigmoid(2 * o + 1)]})
                act.wait_ge(S["hsd_ready"], 2 * o + 2)
                h3_load(1, 0)
            act.wait_ge(S["ot_ready"], 5)
            nc.scalar.activation(yhy_hi[:], vt, ACT.Copy).then_inc(S["yhy_hi_s"], 1)

            def m_evac(n, dst):
                act.wait_ge(S["m_t"], n + 1)
                for q in range(2):
                    ins = nc.scalar.activation(dst[:, q * N:(q + 1) * N], bank[:, 4 + q], ACT.Copy)
                ins.then_inc(S["m_hi"], 1)

            for o in range(2):
                splits(D8 + 3 * o, 4, 28, {
                    11: [lambda: sigmoid(4 + 2 * o)],
                    19: [lambda: m_evac(o, mid_hi[:, o * 2 * N:(o + 1) * 2 * N])],
                    23: [lambda: sigmoid(4 + 2 * o + 1)]})
            act.wait_ge(S["yhy_lo_s"], 1)
            act.dma_start(gf_row[:], g_ffn.partition_broadcast(P)).then_inc(S["gf_in"], 16)
            act.wait_ge(S["h3_in_0"], 192)
            act.dma_start(gl_row[:], g_final.partition_broadcast(P)).then_inc(S["gl_in"], 16)
            m_evac(2, feat_hi[:, 2 * N:4 * N])

            def square(c):
                act.wait_ge(S["x_mid"], c + 1)
                for b in range(TB):
                    nc.scalar.activation(sig[:, b], x2_tok[:, b, c * N:(c + 1) * N], ACT.Square,
                                         accum_out=stat[:, 48 + 4 * b + c:49 + 4 * b + c]).then_inc(S["sumsq2"], 1)

            def h_evac(c):
                act.wait_ge(S["h_tr"], c + 1)
                nc.scalar.activation(h_t[:, 4 * c:4 * c + 2].rearrange("p k t -> p (k t)"), bank[:, 4],
                                     ACT.Copy).then_inc(S["h_ev_act"], 1)

            hooks = {4: [lambda: m_evac(3, feat_hi[:, 6 * N:8 * N])]}
            for c in range(3):
                hooks[8 * c + 12] = [lambda c=c: square(c)]
                hooks[8 * c + 15] = [lambda c=c: h_evac(c)]
            splits(E8, 4, 32, hooks)
            square(3)
            h_evac(3)
            act.wait_ge(S["rstd_ready"], 3)
            act.wait_ge(S["h_tr"], 4)
            for b in range(TB):
                nc.scalar.activation(wide_t[:, b], wide_t[:, b], ACT.Copy,
                                     scale=rstd[:, 2, b:b + 1]).then_inc(S["h_norm"], 1)
            nc.scalar.activation(perm_t[:, 0:P], ident[:], ACT.Copy, scale=0.0)
            nc.scalar.activation(perm_t[:, P:2 * P], ident[:], ACT.Copy, scale=0.0).then_inc(S["perm_t_s"], 1)
            act.wait_ge(S["r_log"], 1)
            nc.scalar.activation(oh[:, 1], oh[:, 0], ACT.Exp).then_inc(S["r_exp"], 1)
            act.wait_ge(S["r_m12"], 1)
            nc.scalar.activation(stat[:, 16:18], stat[:, 14:16], ACT.Exp).then_inc(S["r_exp2"], 1)

            def gather_evac(n, q, src):
                act.wait_ge(S["ga_mm"], 4 * n + q + 1)
                nc.scalar.activation(mid_hi[:, q * N:(q + 1) * N], bank[:, src], ACT.Copy).then_inc(S["ga_hi"], 1)

            def y_evac(q):
                nc.scalar.activation(y_hi[:, q * N:(q + 1) * N], bank[:, 4 + q], ACT.Copy).then_inc(S["yg_hi"], 1)

            for q in range(4):
                gather_evac(0, q, 4 + q)
            act.wait_ge(S["ga_lo"], 4)
            y_evac(0)
            y_evac(1)

            def group(i8, i):
                def y_evac_last(q):
                    act.wait_ge(unit_done, 8 * i8 + (2 * q - 6))
                    y_evac(q)

                def y_evac_here(q):
                    act.wait_ge(unit_done, 8 * i8 + (90 + 2 * q))
                    y_evac(q)

                def perm_evac():
                    act.wait_ge(S["perm_tr"], i + 1)
                    act.wait_ge(S["sc_mm"], 8 * i + 8)
                    nc.scalar.activation(perm_t[:], bank[:, 3, 0:L], ACT.Copy).then_inc(S["perm_t_s"], 1)

                def silu(e):
                    act.wait_ge(unit_done, 8 * i8 + GATE_AT[e] + 8)
                    if e:
                        act.wait_ge(S["prod_done"], PER * i + e)
                    else:
                        act.wait_ge(S["ga_lo"], 4 * i + 4)
                    nc.scalar.activation(sil[:], bank[:, 0], ACT.Silu).then_inc(S["silu_done"], 1)

                def act_split_hi(e):
                    act.wait_ge(S["act_t"], PER * i + e + 1)
                    if e >= 2:
                        act.wait_ge(unit_done, 8 * i8 + DOWN_AT[e - 2] + 8)
                    nc.scalar.activation(act_hi[:, e % 2], bank[:, 2], ACT.Copy).then_inc(S["act_hi_s"], 1)

                hooks = {1: [lambda: y_evac_last(2)], 3: [lambda: y_evac_last(3)], 11: [lambda: silu(0)],
                         15: [perm_evac], 93: [lambda: y_evac_here(0)], 95: [lambda: y_evac_here(1)]}
                for e in range(1, PER):
                    hooks[GATE_AT[e] + 11] = [lambda e=e: act_split_hi(e - 1), lambda e=e: silu(e)]
                hooks[87] = [lambda: act_split_hi(PER - 1)]
                for q in range(4):
                    hooks.setdefault(GATHER_AT[q] + 4, []).append(lambda q=q: gather_evac(i + 1, q, GATHER_BANK[q]))
                splits(i8, 0, 96, hooks)

            with act.Fori(0, GROUPS) as g:
                group(M8 + 12 * g, g)
            act.wait_ge(S["route_ready"], 1)
            more = act.value_load(rounds[0:1, 0:1], min_val=0, max_val=1)
            with act.If(more != 0):
                with act.Fori(0, GROUPS) as g:
                    group(M8 + 12 * GROUPS + 12 * g, GROUPS + g)
            act.wait_ge(unit_done, more * (96 * GROUPS) + (8 * M8 + 96 * GROUPS))
            y_evac(2)
            y_evac(3)
            act.wait_ge(S["moe_done"], 1)
            for b in range(TB):
                nc.scalar.activation(wide_t[:, b], x2_tok[:, b], ACT.Square,
                                     accum_out=stat[:, 20 + b:21 + b]).then_inc(S["sumsq3"], 1)

        @block.vector
        def _(dve):
            order = Order(dve, S["dve_order"])
            link = order.link
            V = nc.vector

            def splits(i8, lo_, hi_, hooks={}):
                for u in range(lo_, hi_):
                    dve.wait_ge(hi_done, 8 * i8 + u + 1)
                    V.tensor_tensor(w_lo[:, u % SPLIT], raw[:, u % RAW], w_hi[:, u % SPLIT],
                                    ALU.subtract).then_inc(lo_done, 1)
                    for f in hooks.get(u, ()):
                        f()

            def mean_square(n, src):
                V.tensor_scalar(var[:, n], src, 1.0 / D, EPS, ALU.mult, ALU.add).then_inc(S["var_ready"], 1)

            dve.wait_ge(S["sumsq"], TB)
            mean_square(0, stat[:, 0:2])
            for q in range(KD // 2):
                for j in range(2):
                    k = 2 * q + j
                    dve.wait_ge(S["xr_hi"], 2 * q + 2)
                    V.scalar_tensor_tensor(feat_lo_k[:, k], bank[:, 4 + q % 4, j * L:(j + 1) * L], g_mix[:, k:k + 1],
                                           feat_hi_k[:, k], ALU.mult, ALU.subtract).then_inc(S["xr_lo"], 1)

            def filter_arg(n, h, bcol):
                dve.wait_ge(S["f_mm"], n)
                link(V.tensor_scalar(filt_b[0:h], bank[0:h, 4, 0:L], fvec[0:h, bcol:bcol + 1], fvec[0:h, 0:1],
                                     ALU.add, ALU.mult))
                link(V.tensor_scalar(filt_c[0:h], filt_b[0:h], 1.0 / (2.0 * math.pi), MAGIC, ALU.mult, ALU.add))
                link(V.tensor_scalar(filt_c[0:h], filt_c[0:h], MAGIC, None, ALU.subtract))
                link(V.scalar_tensor_tensor(filt_b[0:h], filt_c[0:h], -PI_HI, filt_b[0:h], ALU.mult, ALU.add))
                link(V.scalar_tensor_tensor(filt_b[0:h], filt_c[0:h], -PI_LO, filt_b[0:h], ALU.mult, ALU.add))
                V.tensor_scalar(filt_c[0:h], filt_b[0:h], math.pi, -math.pi, ALU.min, ALU.max).then_inc(S["f_arg"], 1)

            filter_arg(1, HID, 1)
            filter_arg(2, P, 2)
            dve.wait_ge(S["f_sin"], 2)
            V.tensor_scalar(a2[:, 1], a2[:, 0], fvec[:, 3:4], None, ALU.mult).then_inc(S["a2_ready"], 1)

            def sg_add(c, par):
                dve.wait_ge(unit_done, 8 * (A8 + c) + 8)
                dve.wait_ge(bias_in[par], 16 * (c // 2 + 1))
                for b in range(TB):
                    ins = V.tensor_tensor(wide_t[:, b, c * N:(c + 1) * N], pair(par)[:, b], bias[:, par], ALU.add)
                ins.then_inc(S["biased"], 1)

            moments = stat[:, 8:12].rearrange("p (b m) -> p b m", m=2)

            def ln_moments():
                dve.wait_ge(S["gelu_done"], 4)
                for b in range(TB):
                    for s in range(2):
                        link(V.bn_stats(oh_flat[:, 6 * s:6 * s + 6], wide_t[:, b, W + s * N:W + (s + 1) * N]))
                    link(V.bn_aggr(stat[:, 8 + 2 * b:10 + 2 * b], oh_flat[:, 0:12]))
                V.tensor_scalar(var[:, 1], moments[:, :, 1], EPS, None, ALU.add).then_inc(S["var_ready"], 1)

            def layer_norm(b):
                dve.wait_ge(S["sg_in"], 48)
                dve.wait_ge(S["rstd_ready"], 2)
                v = wide_t[:, b, W:2 * W]
                link(V.tensor_scalar(v, v, moments[:, b, 0:1], rstd[:, 1, b:b + 1], ALU.subtract, ALU.mult))
                link(V.tensor_tensor(v, v, lng[:], ALU.mult))
                V.tensor_tensor(v, v, lnb[:], ALU.add).then_inc(S["ln_done"], 1)

            oh_flat = oh[:].rearrange("p a b c -> p (a b c)")

            def mix():
                dve.wait_ge(S["mix_done"], 1)
                for g in range(8):
                    V.scalar_tensor_tensor(wide_t[:, :, g * P:(g + 1) * P],
                                           bank[:, 4 + g // 2, (g % 2) * L:(g % 2 + 1) * L].rearrange(
                                               "p (b k) -> p b k", b=TB),
                                           sgb[:, g:g + 1], wide_t[:, :, g * P:(g + 1) * P],
                                           ALU.add, ALU.mult).then_inc(S["ysg"], 1)

            def mix_evac_lo():
                for q in range(4):
                    dve.wait_ge(S["ysg_hi"], q + 1)
                    V.tensor_tensor(mid_lo[:, q * N:(q + 1) * N], bank[:, 4 + q], mid_hi[:, q * N:(q + 1) * N],
                                    ALU.subtract).then_inc(S["ysg_lo"], 1)

            def conv(c):
                dve.wait_ge(S["zpad_ready"], c + 1)
                dst = z_flat[:, bass.ds(c * 4 * L, 4 * L)].rearrange("p (j t) -> p j t", j=4)
                w = conv_w[:, bass.ds(4 * c, 4), :]
                cb = conv_b[:, bass.ds(4 * c, 4)]
                for tap in range(3):
                    for j in range(4):
                        z = zpad[:, j, tap:tap + L]
                        if tap == 0:
                            ins = V.tensor_scalar(dst[:, j], z, w[:, j, 0:1], cb[:, j:j + 1], ALU.mult, ALU.add)
                        else:
                            ins = V.scalar_tensor_tensor(dst[:, j], z, w[:, j, tap:tap + 1], dst[:, j],
                                                         ALU.mult, ALU.add)
                    if tap < 2:
                        link(ins)
                ins.then_inc(S["conv_done"], 1)

            link(V.memset(zpad[:, :, 0:1], 0.0))
            link(V.memset(zpad[:, :, L + 1:L + 2], 0.0))
            hooks = {8 * c + 11: [lambda c=c: sg_add(c, c % 2)] for c in range(4)}
            hooks.update({37: [ln_moments], 39: [lambda: layer_norm(0)], 41: [lambda: layer_norm(1)],
                          45: [lambda: conv(0)], 47: [mix], 51: [mix_evac_lo]})
            splits(A8, 0, 52, hooks)
            k0 = order.base + order.k
            with dve.Fori(1, 3) as h:
                order.enter(k0 + 4 * (h - 1))
                for p in range(2):
                    splits(B8 + 2 * h + p, 4, 12, {6: [lambda: conv(2 * h + p - 1)]})
                assert order.k == 4
            order.enter(k0 + 8)
            conv(5)
            dve.wait_ge(S["conv_done"], 6)
            dve.sem_inc(S["ot_ready"], 1)
            dve.sem_inc(S["merged_ready"], 1)

            def h_evac(s, o, h):
                dve.wait_ge(S["filt_mm"], s + 1)
                dve.wait_ge(S[f"h3_in_{h}"], 64 * o + 64)
                link(V.tensor_tensor(prod_y[:, 0:2], bank[:, 4:6], dec[:], ALU.mult))
                link(V.tensor_tensor(prod_y[0:1, 0], prod_y[0:1, 0], hp_skip[:], ALU.add))
                V.tensor_tensor(prod_y[:, 2:4], bank[:, 6:8], dec[:], ALU.mult).then_inc(S["hsd_ready"], 1)

            def products(s):
                dve.wait_ge(S["u_mm"], s + 1)
                dve.wait_ge(S["k_ready"], s + 1)
                uc, us = bank[:, 4:6], bank[:, 6:8]
                kc, ks = k_resp[:, 0:2], k_resp[:, 2:4]
                link(V.tensor_tensor(prod_y[:, 0:2], uc, kc, ALU.mult))
                link(V.tensor_tensor(sig[:], us, ks, ALU.mult))
                link(V.tensor_tensor(prod_y[:, 0:2], prod_y[:, 0:2], sig[:], ALU.subtract))
                link(V.tensor_tensor(prod_y[:, 2:4], uc, ks, ALU.mult))
                link(V.tensor_tensor(sig[:], us, kc, ALU.mult))
                V.tensor_tensor(prod_y[:, 2:4], prod_y[:, 2:4], sig[:], ALU.add).then_inc(S["y_ready"], 1)
                dve.wait_ge(S["y_ready"], s + 1)

            def ot(s, o, h):
                dve.wait_ge(S["inv_mm"], s + 1)
                dst = z_flat[:, h * 4 * L:(h + 1) * 4 * L]
                src = bank[:, 4:6].rearrange("p b n -> p (b n)")
                V.tensor_tensor(dst, src, z_flat[:, bass.ds(o * CT * L + (CT + 4 * h) * L, 4 * L)],
                                ALU.mult).then_inc(S["ot_ready"], 1)

            def gate_add(n, par, turn):
                dve.wait_ge(bias_in[par], 16 * (turn + 3))
                for b in range(TB):
                    ins = V.tensor_tensor(sig[:, b], bank[:, b], bias[:, par], ALU.add)
                ins.then_inc(S["biased"], 1)

            def merge(n, chunk, add):
                dve.wait_ge(S["sig_ready"], n + 1)
                dst = wide_t[:, :, bass.ds(chunk * N, N)]
                if add:
                    link(V.tensor_tensor(sig[:], bank[:, 2:4], sig[:], ALU.mult))
                    V.tensor_tensor(dst, dst, sig[:], ALU.add).then_inc(S["merged_ready"], 1)
                else:
                    V.tensor_tensor(dst, bank[:, 2:4], sig[:], ALU.mult).then_inc(S["merged_ready"], 1)

            def gate_done(i8, u):
                dve.wait_ge(unit_done, 8 * i8 + u)

            def turn(i8, n0, t0, o, add, extra):
                hooks = {}
                def g0():
                    gate_done(i8, 8)
                    gate_add(n0, 0, t0)
                def p0():
                    gate_done(i8, 12)
                    merge(n0, 2 * o, add)
                def g1():
                    gate_done(i8, 20)
                    gate_add(n0 + 1, 1, t0)
                hooks[11] = [g0]
                hooks[15] = [p0]
                hooks[23] = [g1]
                def p1():
                    gate_done(i8, 24)
                    merge(n0 + 1, 2 * o + 1, add)
                hooks[27] = [p1]
                for u, fs in extra.items():
                    hooks[u] = fs + hooks.get(u, [])
                splits(i8, 4, 28, hooks)

            k0 = order.base + order.k
            per = 2 * (2 + 5)
            with dve.Fori(0, 2) as o:
                order.enter(k0 + per * o)
                turn(C8 + 3 * o, 2 * o, o, o, False, {
                    7: [lambda: h_evac(2 * o, o, 0)],
                    11: [lambda: products(2 * o)],
                    16: [lambda: ot(2 * o, o, 0)],
                    18: [lambda: h_evac(2 * o + 1, o, 1)],
                    22: [lambda: products(2 * o + 1)],
                    26: [lambda: ot(2 * o + 1, o, 1)]})
                assert order.k == per, order.k
            order.enter(k0 + 2 * per)
            dve.wait_ge(S["yhy_hi_s"], 1)
            V.tensor_tensor(yhy_lo[:], vt, yhy_hi[:], ALU.subtract).then_inc(S["yhy_lo_s"], 1)

            def m_evac(n, hi, lo):
                dve.wait_ge(S["m_hi"], n + 1)
                for q in range(2):
                    ins = V.tensor_tensor(lo[:, q * N:(q + 1) * N], bank[:, 4 + q], hi[:, q * N:(q + 1) * N],
                                          ALU.subtract)
                ins.then_inc(S["m_lo"], 1)

            for o in range(2):
                turn(D8 + 3 * o, 4 + 2 * o, 2 + o, o, True,
                     {19: [lambda: m_evac(o, *(m[:, o * 2 * N:(o + 1) * 2 * N] for m in (mid_hi, mid_lo)))]})
            m_evac(2, feat_hi[:, 2 * N:4 * N], feat_lo[:, 2 * N:4 * N])

            def residual(c):
                dve.wait_ge(unit_done, 8 * (E8 + c) + 8)
                if c == 0:
                    dve.wait_ge(S["x_again"], 16 * TB)
                    dve.wait_ge(S["gf_in"], 16)
                cols = slice(c * N, (c + 1) * N)
                dst = x2_tok[:, :, cols]
                V.tensor_tensor(dst, bank[:, 2 * (c % 2):2 * (c % 2) + 2], dst, ALU.add).then_inc(S["x_mid"], 1)
                dve.wait_ge(S["x_mid"], c + 1)
                for b in range(TB):
                    ins = V.tensor_tensor(wide_t[:, b, cols], x2_tok[:, b, cols], gf_row[:, cols], ALU.mult)
                ins.then_inc(S["h_ready"], 1)

            def h_evac(c):
                dve.wait_ge(S["h_tr"], c + 1)
                V.tensor_copy(h_t[:, 4 * c + 2:4 * c + 4].rearrange("p k t -> p (k t)"), bank[:, 5]
                              ).then_inc(S["h_ev_dve"], 1)

            hooks = {4: [lambda: m_evac(3, feat_hi[:, 6 * N:8 * N], feat_lo[:, 6 * N:8 * N])]}
            for c in range(3):
                hooks[8 * c + 11] = [lambda c=c: residual(c)]
                hooks[8 * c + 15] = [lambda c=c: h_evac(c)]
            splits(E8, 4, 32, hooks)
            residual(3)
            h_evac(3)

            dve.wait_ge(S["sumsq2"], 4 * TB)
            link(V.tensor_reduce(stat[:, 4:6], stat[:, 48:56].rearrange("p (b c) -> p b c", b=TB), AX, ALU.add))
            mean_square(2, stat[:, 4:6])
            link(V.memset(posi[:, 8], -1.0))
            dve.wait_ge(S["rstd_ready"], 3)
            dve.wait_ge(S["r_mm"], 1)
            for b in range(TB):
                ins = V.scalar_tensor_tensor(logits[:, b], bank[:, 6 + b, 0:20], rstd[:, 2, b:b + 1], brt[:, b],
                                             ALU.mult, ALU.add)
            link(ins)
            lg = logits[:, :, 0:4]
            le = logits[:, :, 4:20].rearrange("p b (g e) -> p b g e", g=GROUPS)

            def bc4(v):
                return v.unsqueeze(2).to_broadcast([P, TB, 4])

            mg, m1, m2 = stat[:, 24:26], stat[:, 26:28], stat[:, 28:30]
            tie = stat[:, 30:32]

            def first_max(dst, vals, m):
                link(V.tensor_reduce(m, vals, AX, ALU.max))
                link(V.tensor_tensor(dst, vals, bc4(m), ALU.is_equal))
                link(V.tensor_tensor(dst, dst, rank[:], ALU.mult))
                link(V.tensor_reduce(tie, dst, AX, ALU.max))
                link(V.tensor_tensor(dst, dst, bc4(tie), ALU.is_equal))

            def make_perm(i):
                pv = posi[:, bass.ds(i, 1), :].rearrange("p i b -> p (i b)")
                for b in range(TB):
                    ins = V.tensor_scalar(perm[:, b], slots[:], pv[:, b:b + 1], None, ALU.is_equal)
                ins.then_inc(S["perm_ready"], 1)

            G1 = oh[:, 2]
            E1, E2, le1, le2 = oh[:, 3], oh[:, 4], oh[:, 5], oh[:, 6]
            first_max(G1, lg, mg)
            link(V.tensor_tensor(oh[:, 0], lg, bc4(mg), ALU.subtract))
            dve.sem_inc(S["r_log"], 1)
            dve.sem_inc(S["oh_ready"], 1)
            sel = lesel[:].rearrange("p b (g e) -> p b g e", g=GROUPS)
            for b in range(TB):
                link(V.tensor_tensor(sel[:, b], le[:, b], G1[:, b].unsqueeze(2).to_broadcast([P, 4, 4]), ALU.mult))
            link(V.tensor_reduce(le1, sel.rearrange("p b g e -> p b e g"), AX, ALU.add))
            first_max(E1, le1, m1)
            link(V.scalar_tensor_tensor(le2, E1, -3.0e38, le1, ALU.mult, ALU.add))
            first_max(E2, le2, m2)
            link(V.tensor_tensor(stat[:, 14:16], m2, m1, ALU.subtract))
            dve.sem_inc(S["r_m12"], 1)
            dve.wait_ge(S["pos_mm"], 1)
            pos = oh[:, 8]
            for b in range(TB):
                link(V.scalar_tensor_tensor(pos[:, b], bank[:, 2 + b, 32:36], 1.0, G1[:, b], ALU.add, ALU.mult))
            for r in range(2):
                for b in range(TB):
                    link(V.tensor_scalar(posi[:, 4 * r:4 * r + 4, b], pos[:, b], 1.0 + CAP * r, None, ALU.subtract))
            make_perm(0)
            link(V.tensor_copy(oh[:, 9, 0], bank[:, 2, 64:68]))
            link(V.tensor_reduce(stat[:, 40:41], oh[:, 9, 0], AX, ALU.max))
            link(V.tensor_scalar(stat[:, 41:42], stat[:, 40:41], CAP + 0.5, None, ALU.is_gt))
            link(V.tensor_copy(rounds[:], stat[:, 41:42]))
            dve.wait_ge(S["r_exp"], 1)
            psel = stat[:, 32:34]
            link(V.tensor_reduce(psel, oh[:, 1], AX, ALU.add))
            dve.wait_ge(S["r_exp2"], 1)
            t2, w1_, w2_ = stat[:, 16:18], stat[:, 34:36], stat[:, 36:38]
            link(V.tensor_scalar(w1_, t2, 1.0, None, ALU.add))
            link(V.tensor_tensor(w1_, w1_, psel, ALU.mult))
            link(V.reciprocal(w1_, w1_))
            link(V.tensor_tensor(w2_, w1_, t2, ALU.mult))
            link(V.tensor_tensor(comb[:], E1, bc4(w1_), ALU.mult))
            link(V.tensor_tensor(oh[:, 7], E2, bc4(w2_), ALU.mult))
            link(V.tensor_tensor(comb[:], comb[:], oh[:, 7], ALU.add))
            dve.sem_inc(S["route_ready"], 1)

            def gather_evac(n, q, src):
                dve.wait_ge(S["ga_hi"], 4 * n + q + 1)
                V.tensor_tensor(mid_lo[:, q * N:(q + 1) * N], bank[:, src], mid_hi[:, q * N:(q + 1) * N],
                                ALU.subtract).then_inc(S["ga_lo"], 1)

            def y_evac(n, q):
                dve.wait_ge(S["yg_hi"], 4 * n + q + 1)
                V.tensor_tensor(y_lo[:, q * N:(q + 1) * N], bank[:, 4 + q], y_hi[:, q * N:(q + 1) * N],
                                ALU.subtract).then_inc(S["yg_lo"], 1)

            def scatter_add(n, s, src):
                dve.wait_ge(S["sc_mm"], 8 * n + s + 1)
                dst = x2_tok[:, s % 2, (s // 2) * N:(s // 2 + 1) * N]
                V.tensor_tensor(dst, bank[:, src], dst, ALU.add).then_inc(S["sc_add"], 1)

            def combg_copy(n):
                dve.wait_ge(S["comb_mm"], n + 1)
                if not static_le(n, 0):
                    dve.wait_ge(S["prod_done"], PER * n)
                V.tensor_copy(combg[:], bank[:, 2, 0:4]).then_inc(S["combg_s"], 1)

            for q in range(4):
                gather_evac(0, q, 4 + q)
            combg_copy(0)
            y_evac(0, 0)
            y_evac(0, 1)

            def group(i8, i):
                def product(e):
                    dve.wait_ge(S["silu_done"], PER * i + e + 1)
                    dve.wait_ge(unit_done, 8 * i8 + GATE_AT[e] + 16)
                    if e:
                        dve.wait_ge(S["act_t"], PER * i + e)
                    else:
                        dve.wait_ge(S["combg_s"], i + 1)
                    V.scalar_tensor_tensor(prod[:], bank[:, 1], combg[:, e:e + 1], sil[:],
                                           ALU.mult, ALU.mult).then_inc(S["prod_done"], 1)

                def act_split_lo(e):
                    dve.wait_ge(S["act_hi_s"], PER * i + e + 1)
                    V.tensor_tensor(act_lo[:, e % 2], bank[:, 2], act_hi[:, e % 2],
                                    ALU.subtract).then_inc(S["act_lo_s"], 1)

                def next_perm():
                    dve.wait_ge(S["perm_tr"], i + 1)
                    make_perm(i + 1)

                hooks = {1: [lambda: y_evac(i, 2)], 3: [lambda: y_evac(i, 3)], 60: [next_perm],
                         84: [lambda: combg_copy(i + 1)], 93: [lambda: y_evac(i + 1, 0)], 95: [lambda: y_evac(i + 1, 1)]}
                for e in range(PER):
                    hooks.setdefault(GATE_AT[e] + 19, []).append(lambda e=e: product(e))
                for e in range(1, PER):
                    hooks.setdefault(GATE_AT[e] + 11, []).append(lambda e=e: act_split_lo(e - 1))
                hooks[87] = [lambda: act_split_lo(PER - 1)]
                for q in range(4):
                    hooks.setdefault(GATHER_AT[q] + 4, []).append(lambda q=q: gather_evac(i + 1, q, GATHER_BANK[q]))
                for s in range(8):
                    hooks.setdefault(s + 5, []).append(lambda s=s: scatter_add(i, s, 2 + s % 2))
                splits(i8, 0, 96, hooks)

            with dve.Fori(0, GROUPS) as g:
                group(M8 + 12 * g, g)
            more = dve.value_load(rounds[0:1, 0:1], min_val=0, max_val=1)
            with dve.If(more != 0):
                with dve.Fori(0, GROUPS) as g:
                    group(M8 + 12 * GROUPS + 12 * g, GROUPS + g)
            n = more * GROUPS + GROUPS
            y_evac(n, 2)
            y_evac(n, 3)
            for s in range(8):
                scatter_add(n, s, s % 4)
            dve.wait_ge(S["sc_add"], 8 * n + 8)
            dve.wait_ge(S["gl_in"], 16)
            dve.sem_inc(S["moe_done"], 1)
            dve.wait_ge(S["sumsq3"], TB)
            mean_square(3, stat[:, 20:22])
            dve.wait_ge(S["rstd_ready"], 4)
            for b in range(TB):
                V.scalar_tensor_tensor(wide_t[:, b], x2_tok[:, b], rstd[:, 3, b:b + 1], gl_row[:],
                                       ALU.mult, ALU.mult).then_inc(S["y_out"], 1)

        @block.tensor
        def _(pe):
            mm = nc.tensor.matmul

            def gemm(i8, u0, n, lhs, acc, hooks={}, rows=TB, start=True, stop=True, k0=0, kend=None):
                hi, lo = lhs
                for u in range(n):
                    pe.wait_ge(lo_done, 8 * i8 + u0 + u + 1)
                    s = (u0 + u) % SPLIT
                    for j in range(UK):
                        k = k0 + UK * u + j
                        first, last_k = start and u == 0 and j == 0, stop and u == n - 1 and j == UK - 1
                        for b in range(rows):
                            cols = slice(b * P, (b + 1) * P)
                            mm(acc[b], hi[:, k, cols], w_hi[:, s, j], start=first, stop=False)
                            mm(acc[b], hi[:, k, cols], w_lo[:, s, j], start=False, stop=False)
                            last = mm(acc[b], lo[:, k, cols], w_hi[:, s, j], start=False, stop=last_k)
                    last.then_inc(unit_done, 1)
                    for f in hooks.get(u0 + u, ()):
                        f()
                return last

            def acc(p):
                return [bank[:, 2 * p], bank[:, 2 * p + 1]]

            feat = (feat_hi_k, feat_lo_k)
            mid = (mid_hi_k, mid_lo_k)
            yhy = (yhy_hi_k, yhy_lo_k)

            n_const = 13
            pe.wait_ge(S["consts_in"], 16 * n_const)
            pe.wait_ge(S["xr"], TB)
            for q in range(KD // 2):
                if q >= 4:
                    pe.wait_ge(S["xr_lo"], 2 * (q - 4) + 2)
                for j in range(2):
                    for b in range(TB):
                        k = 2 * q + j
                        last = nc.tensor.transpose(bank[:, 4 + q % 4, j * L + b * P:j * L + (b + 1) * P],
                                                   wide_t[:, b, k * P:(k + 1) * P], ident[:])
                last.then_inc(S["xr_t"], 1)
            pe.wait_ge(S["xr_lo"], KD)
            pe.wait_ge(S["filt_in"], 48)
            mm(bank[0:HID, 4, 0:L], w1s[:], zp[:], start=True, stop=True).then_inc(S["f_mm"], 1)
            pe.wait_ge(S["f_sin"], 1)
            mm(bank[:, 4, 0:L], w2s[:], filt_a[0:HID], start=True, stop=True).then_inc(S["f_mm"], 1)

            for c in range(4):
                if c >= 2:
                    pe.wait_ge(S["biased"], c - 1)
                gemm(A8 + c, 0, 8, feat, acc(c % 2))

            def sgu_mix():
                pe.wait_ge(S["ln_done"], TB)
                pe.wait_ge(S["zpad_ready"], 1)
                pe.wait_ge(S["f_arg"], 2)
                for g in range(8):
                    last = mm(bank[:, 4 + g // 2, (g % 2) * L:(g % 2 + 1) * L].rearrange("p (b k) -> p b k", b=TB),
                              sgw[:, g], wide_t[:, :, W + g * P:W + (g + 1) * P], start=True, stop=True)
                last.then_inc(S["mix_done"], 1)

            def sgu_transpose():
                pe.wait_ge(S["ysg"], 8)
                for k in range(CT):
                    for b in range(TB):
                        last = nc.tensor.transpose(bank[:, 4 + k // 2, (k % 2) * L + b * P:(k % 2) * L + (b + 1) * P],
                                                   wide_t[:, b, k * P:(k + 1) * P], ident[:])
                last.then_inc(S["ysg_t"], 1)

            def z_transpose(c):
                pe.wait_ge(S["zt_ready"], c + 1)
                if isinstance(c, int) and c == 0:
                    pe.wait_ge(S["f_arg"], 2)
                else:
                    pe.wait_ge(S["zpad_ready"], c)
                    pe.wait_ge(S["ysg_lo"], 4)
                for j in range(4):
                    for b in range(TB):
                        last = nc.tensor.transpose(bank[:, 4 + j // 2, (j % 2) * L + b * P:(j % 2) * L + (b + 1) * P],
                                                   zt[:, b, j * P:(j + 1) * P], ident[:])
                last.then_inc(S["z_t"], 1)

            pe.wait_ge(S["biased"], 3)
            gemm(B8, 0, 8, feat, acc(0), {})
            pe.wait_ge(S["biased"], 4)
            gemm(B8 + 1, 0, 8, feat, acc(1), {1: [lambda: z_transpose(0)], 4: [sgu_mix]})
            sgu_transpose()
            with pe.Fori(1, 3) as h:
                for p in range(2):
                    pe.wait_ge(S["zt_ready"], 2 * h + p - 1)
                    gemm(B8 + 2 * h + p, 0, 8, feat, acc(p), {2: [lambda: z_transpose(2 * h + p - 1)]})
            z_transpose(5)

            def v_transpose(o):
                pe.wait_ge(S["ot_ready"], 2 * o + 1)
                for q in range(4):
                    c, b = 4 * (q // 2), q % 2
                    for j in range(4):
                        last = nc.tensor.transpose(bank[:, 4 + q, j * P:(j + 1) * P],
                                                   vt_c[:, c + j, b * P:(b + 1) * P], ident[:])
                    last.then_inc(S["v_t"], 1)

            def filt(s, o, h):
                pe.wait_ge(S["h3_in_%d" % h], 64 * o + 64)
                if h == 0:
                    pe.wait_ge(S["vtok_ready"], 4 * o + 4)
                else:
                    pe.wait_ge(S["ot_ready"], 2 * o + 2)
                for d in range(2):
                    for b in range(TB):
                        last = mm(bank[:, 4 + 2 * d + b], a2[:, d, b * P:(b + 1) * P], w3s[:], start=True, stop=True)
                last.then_inc(S["filt_mm"], 1)

            def transform(rhs_c, rhs_s):
                for f in range(4):
                    rhs = rhs_c if f < 2 else rhs_s
                    for b in range(TB):
                        last = mm(bank[:, 4 + f], dft_f[:, b, f * P:(f + 1) * P], rhs[b], start=b == 0, stop=b == TB - 1)
                return last

            def response(s):
                pe.wait_ge(S["hsd_ready"], s + 1)
                pe.wait_ge(S["tables_in"], 32)
                transform([prod_y[:, 0], prod_y[:, 1]], [prod_y[:, 2], prod_y[:, 3]]).then_inc(S["k_mm"], 1)

            def spectrum(s, h):
                pe.wait_ge(S["k_ready"], s + 1)
                v = [v_tok[:, b, h * N:(h + 1) * N] for b in range(TB)]
                transform(v, v).then_inc(S["u_mm"], 1)

            def inverse(s):
                pe.wait_ge(S["y_ready"], s + 1)
                for j in range(4):
                    for f in range(4):
                        last = mm(bank[:, 4 + j // 2, (j % 2) * L:(j % 2 + 1) * L], prod_y[:, f, j * P:(j + 1) * P],
                                  dft_i[:, f], start=f == 0, stop=f == 3)
                last.then_inc(S["inv_mm"], 1)

            def turn(i8, n0, o, proj, hooks):
                pe.wait_ge(S["biased"], n0 + 4)
                gemm(i8, 0, 8, feat, acc(0), hooks)
                pe.wait_ge(S["merged_ready"], n0 + 1)
                gemm(i8, 8, 4, proj, acc(1), hooks)
                pe.wait_ge(S["biased"], n0 + 5)
                gemm(i8, 12, 8, feat, acc(0), hooks)
                pe.wait_ge(S["merged_ready"], n0 + 2)
                gemm(i8, 20, 4, proj, acc(1), hooks)

            pe.wait_ge(S["zt_ready"], 6)
            pe.wait_ge(S["ysg_lo"], 4)
            with pe.Fori(0, 2) as o:
                turn(C8 + 3 * o, 2 * o, o, mid, {
                    1: [lambda: v_transpose(o)],
                    3: [lambda: filt(2 * o, o, 0)],
                    5: [lambda: response(2 * o)],
                    7: [lambda: spectrum(2 * o, 0)],
                    12: [lambda: inverse(2 * o)],
                    14: [lambda: filt(2 * o + 1, o, 1)],
                    16: [lambda: response(2 * o + 1)],
                    18: [lambda: spectrum(2 * o + 1, 1)],
                    22: [lambda: inverse(2 * o + 1)]})

            def m_transpose(n, chunk):
                pe.wait_ge(S["yhy_lo_s"], 1)
                if not static_le(n, 0):
                    pe.wait_ge(S["m_lo"], n)
                for j in range(4):
                    for b in range(TB):
                        last = nc.tensor.transpose(bank[:, 4 + j // 2, (j % 2) * L + b * P:(j % 2) * L + (b + 1) * P],
                                                   wide_t[:, b, chunk * N + j * P:chunk * N + (j + 1) * P], ident[:])
                last.then_inc(S["m_t"], 1)

            def m_first(o):
                pe.wait_ge(S["merged_ready"], 4 + 2 * o + 2)
                m_transpose(o, 2 * o)

            for o in range(2):
                turn(D8 + 3 * o, 4 + 2 * o, o, yhy, {15: [lambda: m_first(o)]})
            m_transpose(2, 1)

            def h_transpose(c):
                pe.wait_ge(S["h_ready"], c + 1)
                if c:
                    pe.wait_ge(S["h_ev_act"], c)
                    pe.wait_ge(S["h_ev_dve"], c)
                for j in range(4):
                    for b in range(TB):
                        k = 4 * c + j
                        last = nc.tensor.transpose(bank[:, 4 + j // 2, (j % 2) * L + b * P:(j % 2) * L + (b + 1) * P],
                                                   wide_t[:, b, k * P:(k + 1) * P], ident[:])
                last.then_inc(S["h_tr"], 1)

            def router(c):
                pe.wait_ge(S["h_ev_act"], c + 1)
                pe.wait_ge(S["h_ev_dve"], c + 1)
                for b in range(TB):
                    for k in range(4 * c, 4 * c + 4):
                        last = mm(bank[:, 6 + b, 0:20], h_t[:, k, b * P:(b + 1) * P], wr[:, k],
                                  start=k == 0, stop=k == KD - 1)
                return last

            hooks = {}
            for c in range(3):
                hooks[8 * c + 12] = [lambda c=c: h_transpose(c)]
                if c < 2:
                    hooks[8 * c + 17] = [lambda c=c: router(c)]
            def m_last():
                pe.wait_ge(S["merged_ready"], 9)
                m_transpose(3, 3)

            hooks[1] = [m_last]
            for c in range(4):
                if c >= 2:
                    pe.wait_ge(S["x_mid"], c - 1)
                for q, (lhs, k0) in enumerate(((mid, 0), (feat, 4), (mid, 4), (feat, 12))):
                    if c == 0:
                        pe.wait_ge(S["m_lo"], (1, 3, 2, 4)[q])
                    if c < 2 and q == 0:
                        pe.wait_ge(S["merged_ready"], 8 + c)
                    gemm(E8, 8 * c + 2 * q, 2, lhs, acc(c % 2), hooks, start=q == 0, stop=q == 3, k0=k0)
            router(2)
            h_transpose(3)
            router(3).then_inc(S["r_mm"], 1)
            pe.wait_ge(S["oh_ready"], 1)
            mm(bank[:, 2, 32:36], before[:], oh[:, 2, 0], start=True, stop=True)
            mm(bank[:, 3, 32:36], ones[:], oh[:, 2, 0], start=True, stop=False)
            mm(bank[:, 3, 32:36], before[:], oh[:, 2, 1], start=False, stop=True)
            mm(bank[:, 2, 64:68], ones[:], oh[:, 2, 0], start=True, stop=False)
            mm(bank[:, 2, 64:68], ones[:], oh[:, 2, 1], start=False, stop=True).then_inc(S["pos_mm"], 1)

            def gather(n, q, dst):
                for kk in range(4):
                    k = 4 * q + kk
                    for b in range(TB):
                        last = mm(bank[:, dst, kk * CAP:(kk + 1) * CAP], wide_t[:, b, k * P:(k + 1) * P], perm[:, b],
                                  start=b == 0, stop=b == TB - 1)
                last.then_inc(S["ga_mm"], 1)

            def comb_gather(n):
                pe.wait_ge(S["perm_ready"], n + 1)
                for b in range(TB):
                    last = mm(bank[:, 2, 0:4], perm[:, b], comb[:, b], start=b == 0, stop=b == TB - 1)
                last.then_inc(S["comb_mm"], 1)

            def scatter(s, dst):
                b, q = s % 2, s // 2
                mm(bank[:, dst], perm_t[:, b * P:(b + 1) * P], y_hi[:, q * N:(q + 1) * N], start=True, stop=False)
                mm(bank[:, dst], perm_t[:, b * P:(b + 1) * P], y_lo[:, q * N:(q + 1) * N], start=False,
                   stop=True).then_inc(S["sc_mm"], 1)

            pe.wait_ge(S["perm_ready"], 1)
            pe.wait_ge(S["h_norm"], TB)
            for q in range(4):
                gather(0, q, 4 + q)
            pe.wait_ge(S["route_ready"], 1)
            comb_gather(0)

            def group(i8, i):
                def gate(e):
                    if e:
                        pe.wait_ge(S["silu_done"], PER * i + e)
                    gemm(i8, GATE_AT[e], 8, (xg_hi, xg_lo), [bank[:, 0]], hooks, rows=1)

                def up(e):
                    if e:
                        pe.wait_ge(S["prod_done"], PER * i + e)
                    gemm(i8, GATE_AT[e] + 8, 8, (xg_hi, xg_lo), [bank[:, 1]], hooks, rows=1)

                def act_transpose(e):
                    pe.wait_ge(S["prod_done"], PER * i + e + 1)
                    if e:
                        pe.wait_ge(S["act_lo_s"], PER * i + e)
                    else:
                        pe.wait_ge(S["sc_add"], 8 * i + 8)
                    if e == PER - 1:
                        pe.wait_ge(S["combg_s"], i + 2)
                    for k in range(4):
                        last = nc.tensor.transpose(bank[:, 2, k * P:(k + 1) * P], prod[:, k * P:(k + 1) * P], ident[:])
                    last.then_inc(S["act_t"], 1)

                def down(e):
                    pe.wait_ge(S["act_lo_s"], PER * i + e + 1)
                    for c in range(4):
                        gemm(i8, DOWN_AT[e] + 2 * c, 2,
                             (act_hi[:, e % 2].rearrange("p (k s) -> p k s", k=4),
                              act_lo[:, e % 2].rearrange("p (k s) -> p k s", k=4)),
                             [bank[:, 4 + c]], hooks, rows=1, start=e == 0, stop=e == PER - 1)

                def scatter_last(s):
                    if s % 2 == 0:
                        pe.wait_ge(S["yg_lo"], 4 * i + s // 2 + 1)
                    if s >= 2:
                        pe.wait_ge(S["sc_add"], 8 * i + s - 1)
                    scatter(s, 2 + s % 2)

                def perm_transpose():
                    pe.wait_ge(S["sc_add"], 8 * i + 8)
                    for b in range(TB):
                        last = nc.tensor.transpose(bank[:, 3, b * P:(b + 1) * P], perm[:, b], ident[:])
                    last.then_inc(S["perm_tr"], 1)

                def comb_next():
                    pe.wait_ge(S["act_lo_s"], PER * i + PER - 1)
                    comb_gather(i + 1)

                def gather_next(q):
                    pe.wait_ge(*((S["perm_t_s"], i + 2), (S["silu_done"], PER * i + PER),
                                 (S["prod_done"], PER * i + PER), (S["ga_lo"], 4 * i + 5))[q])
                    gather(i + 1, q, GATHER_BANK[q])

                hooks = {s + 1: [lambda s=s: scatter_last(s)] for s in range(8)}
                hooks[12] = [perm_transpose]
                hooks[79] = [comb_next]
                hooks[85] = [lambda: act_transpose(PER - 1)]
                for q in range(4):
                    hooks[GATHER_AT[q]] = [lambda q=q: gather_next(q)]
                pe.wait_ge(S["ga_lo"], 4 * i + 4)
                gate(0)
                up(0)
                for e in range(1, PER):
                    gate(e)
                    act_transpose(e - 1)
                    up(e)
                    down(e - 1)
                down(PER - 1)

            pe.wait_ge(S["perm_t_s"], 1)
            pe.wait_ge(S["combg_s"], 1)
            with pe.Fori(0, GROUPS) as g:
                group(M8 + 12 * g, g)
            more = pe.value_load(rounds[0:1, 0:1], min_val=0, max_val=1)
            with pe.If(more != 0):
                with pe.Fori(0, GROUPS) as g:
                    group(M8 + 12 * GROUPS + 12 * g, GROUPS + g)
            n = more * GROUPS + GROUPS
            for s in range(8):
                if s % 2 == 0:
                    pe.wait_ge(S["yg_lo"], 4 * n + s // 2 + 1)
                if s >= 4:
                    pe.wait_ge(S["sc_add"], 8 * n + s - 3)
                scatter(s, s % 4)


def tables():
    import numpy as np
    f32 = np.float32
    t = np.linspace(0.0, 1.0, L, dtype=f32)[:, None]
    bands = np.linspace(1e-4, (EMB - 1) // 2 - 1, (EMB - 1) // 2, dtype=f32)
    w = (f32(2.0 * math.pi / L) * np.arange(L, dtype=f32))[:, None]
    z = np.concatenate([t, np.cos(bands * w), -np.sin(bands * w)], axis=-1).astype(f32)
    deltas = np.abs(np.linspace(math.log(1e-2) / 1.5, math.log(1e-2) / 0.3, W, dtype=f32))
    decay = np.exp(-t * deltas).astype(f32)
    angle = np.outer(np.arange(L), 2 * np.arange(L) + 1) * (2.0 * math.pi / (4 * L))
    f = np.concatenate([np.cos(angle), np.sin(angle)], axis=1)
    row = np.arange(P)
    return {
        "zpos": np.ascontiguousarray(z.T),
        "decay": np.ascontiguousarray(decay.reshape(TB, P, W).transpose(1, 0, 2)),
        "dft": np.ascontiguousarray(f.astype(f32).reshape(TB, P, 2 * L).transpose(1, 0, 2)),
        "idft": np.ascontiguousarray((f.T / L).astype(f32).reshape(4, P, L).transpose(1, 0, 2)),
        "ident_in": np.eye(P, dtype=f32),
        "before_in": (row[:, None] < row[None, :]).astype(f32),
        "ones_in": np.ones((P, P), f32),
        "slots_in": np.ascontiguousarray(np.broadcast_to(np.arange(CAP, dtype=f32), (P, CAP))),
        "rank_in": np.ascontiguousarray(np.broadcast_to(np.arange(4, 0, -1, dtype=f32), (P, TB, 4))),
    }


def kernel(**inputs):
    import numpy as np
    import concourse.bacc as bacc
    from concourse.bass_utils import run_bass_kernel_spmd as run

    a = {k: np.asarray(v) for k, v in inputs.items()}

    def cols(v, order=None):
        m = v.reshape(-1, P).T
        return m if order is None else m[:, order]

    vfirst = list(range(2 * CT, 3 * CT)) + list(range(2 * CT))
    laid = {n: a[n] for n in ("x", "w_in", "w_hy_out", "w_sg_out", "w_out", "w_gate", "w_up", "w_down", "b_in",
                              "filt_w3", "hy_skip")}
    laid.update(
        ln_g=a["sg_ln_g"], ln_b=a["sg_ln_b"], g_ffn=a["g_ffn"], g_final=a["g_final"][None],
        b_router=np.tile(np.concatenate([a["b_rg"][0], a["b_re"][0].reshape(-1)])[None], (1, TB)).reshape(1, TB, 20),
        g_mix_c=cols(a["g_mix"][0]),
        conv_w_c=np.stack([cols(a["conv_w"][0, j], vfirst) for j in range(3)], axis=-1),
        conv_b_c=cols(a["conv_b"][0], vfirst),
        b_hy_c=cols(a["b_in"][0, :3 * W], vfirst),
        filt_w1=a["filt_w1"],
        filt_w2=np.concatenate([a["filt_w2"][0]] * 2, axis=1),
        filt_vec=np.stack([np.tile(a["filt_freq"][0], 2), np.tile(a["filt_b1"][0], 2), np.tile(a["filt_b2"][0], 2),
                           np.repeat(np.array([1.0, -1.0], np.float32), HID)], axis=1),
        sg_w_t=a["sg_w"][0].transpose(2, 0, 1),
        sg_b_t=a["sg_b"][0].T,
        w_router=np.concatenate([a["w_rg"][0], a["w_re"][0].transpose(1, 0, 2).reshape(D, -1)], axis=1)
        .reshape(KD, P, 20).transpose(1, 0, 2))
    laid.update(tables())

    nc = bacc.Bacc("TRN2", target_bir_lowering=False, num_devices=1)
    arrays, args = {}, {}
    for name, v in laid.items():
        v = np.ascontiguousarray(v)
        arrays["in_" + name] = v
        args[name] = nc.dram_tensor("in_" + name, v.shape, mybir.dt.from_np(v.dtype), kind="ExternalInput").ap()
    args["out"] = nc.dram_tensor("out_0", (1, L, D), F32, kind="ExternalOutput").ap()
    build(nc, **args)
    r = run(nc, [arrays], core_ids=[0])
    return r.results[0]["out_0"]
```

```python
import math
from contextlib import ExitStack

import concourse.bass as bass
from concourse import mybir

F32 = mybir.dt.float32
F32R = mybir.dt.float32r
I32 = mybir.dt.int32
ACT = mybir.ActivationFunctionType
ALU = mybir.AluOpType
AX = mybir.AxisListType.X

P = 128
L = 256
TB = L // P
D = 2048
KD = D // P
W = D // 2
CT = W // P
N = 512
HALVES = W // N
C_U = 3 * W
C_GHY = 5 * W
C_GSG = 7 * W
EMB, HID = 33, 64
GROUPS, PER = 4, 4
FE = D // 4
CAP = 128
EPS = 1e-6
CONSTS = 10
UK = 2
RAW, SPLIT = 8, 4
RAW_M = 16
MAGIC = 1.5 * 2.0 ** 23
PI_HI = 6.28125
PI_LO = 2.0 * math.pi - PI_HI

GATHER_AT, GATHER_BANK = [81, 84, 87, 90], [3, 0, 1, 3]
GATE_AT = [0] + [16 + 24 * e for e in range(PER - 1)]
DOWN_AT = [32 + 24 * e for e in range(PER - 1)] + [88]
A8, B8, C8, D8, E8, M8 = 0, 4, 10, 16, 22, 26


def static_le(value, bound):
    return isinstance(value, int) and value <= bound


def build(nc, x, w_in, w_hy_out, w_sg_out, w_out, w_gate, w_up, w_down, b_in, filt_w3, hy_skip,
          ln_g, ln_b, g_ffn, g_final, b_router,
          g_mix_c, conv_w_c, conv_b_c, b_hy_c, filt_w1, filt_w2, filt_vec, sg_w_t, sg_b_t, w_router,
          zpos, decay, dft, idft, ident_in, before_in, ones_in, slots_in, rank_in, out):
    ctx = ExitStack()
    with ctx:
        def sb(name, shape, dt=F32):
            return ctx.enter_context(nc.sbuf_tensor(name, shape, dt))

        def sem(name):
            return ctx.enter_context(nc.semaphore(name))

        def region(name, words, *layouts):
            made = []
            for layout in layouts:
                with ExitStack() as sub:
                    made.append([sub.enter_context(nc.sbuf_tensor(n, s, d)) for n, s, d in layout])
            sb(name, [P, words])
            return made

        raw = sb("raw", [P, RAW, UK, N])
        w_hi = sb("w_hi", [P, SPLIT, UK, N], F32R)
        w_lo = sb("w_lo", [P, SPLIT, UK, N], F32R)
        mid_hi = sb("mid_hi", [P, CT * L], F32R)
        mid_lo = sb("mid_lo", [P, CT * L], F32R)
        wide = sb("wide", [P, TB * D])
        ident = sb("ident", [P, P])
        before = sb("before", [P, P])
        ones = sb("ones", [P, P])
        slots = sb("slots", [P, CAP])
        rank = sb("rank", [P, TB, 4])
        bias = sb("bias", [P, 2, N])
        conv_w = sb("conv_w", [P, 3 * CT, 3])
        conv_b = sb("conv_b", [P, 3 * CT])
        b_hy = sb("b_hy", [P, 3 * CT])
        g_mix = sb("g_mix", [P, KD])
        fvec = sb("fvec", [P, 4])
        sgb = sb("sgb", [P, CT])
        wr = sb("wr", [P, KD, 20])
        brt = sb("brt", [P, TB, 20])
        stat = sb("stat", [P, 64])
        var = sb("var", [P, 4, TB])
        rstd = sb("rstd", [P, 4, TB])
        minus_half = sb("minus_half", [P, TB])

        (feat_hi, feat_lo), (raw_more,) = region(
            "region_f", 2 * KD * L,
            [("feat_hi", [P, KD * L], F32R), ("feat_lo", [P, KD * L], F32R)],
            [("raw_more", [P, RAW_M - RAW, UK, N], F32)])
        (x_tok,), (prod_y, k_resp), (zt, zpad), (x2_tok,) = region(
            "region_x", TB * D,
            [("x_tok", [P, TB, D], F32)],
            [("prod_y", [P, 4, N], F32), ("k_resp", [P, 4, N], F32)],
            [("zt", [P, TB, N], F32), ("zpad", [P, 4, L + 2], F32)],
            [("x2_tok", [P, TB, D], F32)])
        (z_all, v_tok), (_, yhy_hi, yhy_lo), (gf_row, h_t), moe = region(
            "region_z", 4 * CT * L,
            [("z_all", [P, 3, CT * L], F32), ("v_tok", [P, TB, W], F32)],
            [("skip_v", [P, CT * L], F32), ("yhy_hi", [P, CT * L], F32R), ("yhy_lo", [P, CT * L], F32R)],
            [("gf_row", [P, D], F32), ("h_t", [P, KD, L], F32)],
            [("sil", [P, N], F32), ("prod", [P, N], F32), ("perm", [P, TB, CAP], F32),
             ("perm_t", [P, TB * CAP], F32R), ("skip_m", [P, 2 * L], F32),
             ("y_hi", [P, D], F32R), ("y_lo", [P, D], F32R),
             ("act_hi", [P, 2, N], F32R), ("act_lo", [P, 2, N], F32R)])
        sil, prod, perm, perm_t, _, y_hi, y_lo, act_hi, act_lo = moe
        (dft_f, dft_i, dec, w3s, hp_skip, odd), (lng, lnb, sgw), filt_mem, (gl_row,) = region(
            "region_t", 8 * N,
            [("dft_f", [P, 2, L], F32), ("dft_i", [P, 4, P], F32), ("dec", [P, 2, N], F32), ("w3s", [P, N], F32),
             ("hp_skip", [1, N], F32), ("odd", [P, 2, N], F32)],
            [("lng", [P, W], F32), ("lnb", [P, W], F32), ("sgw", [P, 8, P], F32)],
            [("filt_a", [P, L], F32), ("filt_b", [P, L], F32), ("filt_c", [P, L], F32), ("w1s", [EMB, HID], F32),
             ("w2s", [HID, P], F32), ("zp", [EMB, L], F32)],
            [("gl_row", [P, D], F32)])
        filt_a, filt_b, filt_c, w1s, w2s, zp = filt_mem
        vt = z_all[:, 0]
        a2 = sb("a2", [P, 2, L])
        sig = sb("sig", [P, TB, N])
        oh = sb("oh", [P, 12, TB, 4])
        posi = sb("posi", [P, 9, TB])
        comb = sb("comb", [P, TB, 4])
        combg = sb("combg", [P, 4])
        lesel = sb("lesel", [P, TB, 16])
        logits = sb("logits", [P, TB, 20])
        rounds = sb("rounds", [P, 1], I32)
        bank = ctx.enter_context(nc.psum_tensor("bank", [P, 8, N], F32))

        ld = [sem(f"weights_loaded_{i}") for i in range(RAW_M)]
        hi_done, lo_done, unit_done = sem("hi_done"), sem("lo_done"), sem("unit_done")
        x_in = [sem(f"x_in_{c}") for c in range(D // N)]
        bias_in = [sem("bias_in_0"), sem("bias_in_1")]
        S = {n: sem(n) for n in (
            "a2_ready", "act_hi_s", "act_lo_s", "act_t", "biased", "comb_mm", "combg_s", "consts_in",
            "conv_done", "dve_order", "f_arg", "f_mm", "f_sin", "filt_in", "filt_mm", "ga_hi", "ga_lo", "ga_mm",
            "gelu_done", "gf_in", "gl_in", "h3_in_0", "h3_in_1", "h_ev_act", "h_ev_dve", "h_ready", "h_tr",
            "h_norm", "half_in", "hsd_ready", "inv_mm", "k_mm", "k_odd", "k_ready", "ln_done", "m_hi", "m_lo",
            "m_t", "merged_ready",
            "mix_done", "oh_ready", "ot_ready", "out_done", "perm_ready", "perm_t_s",
            "perm_tr", "pos_mm", "prod_done", "r_exp", "r_exp2", "r_log", "r_m12", "r_mm", "route_ready",
            "rstd_ready", "sc_add", "sc_mm", "sg_in", "sig_ready", "silu_done", "sumsq", "sumsq2", "sumsq3",
            "ident_ready", "g_mix_in", "tables_in", "u_mm", "u_odd", "v_t", "var_ready", "vtok_ready",
            "x_again", "x_mid", "x_hi",
            "x_lo", "x_t", "y_out", "y_ready", "yg_hi", "yg_lo", "yhy_hi_s", "yhy_lo_s", "ysg", "ysg_hi", "ysg_lo",
            "ysg_t", "z_t", "zpad_ready", "zt_ready")}

        def slot_m(u):
            s = u % RAW_M
            return raw[:, s] if s < RAW else raw_more[:, s - RAW]

        def loaded_m(i, u):
            before_m = M8 if u % RAW_M < RAW else 0
            return 16 * (96 // RAW_M) * i + 16 * (before_m + u // RAW_M + 1)

        class Order:
            def __init__(self, eng, s):
                self.eng, self.s, self.base, self.k = eng, s, 0, 0

            def link(self, ins):
                ins.then_inc(self.s, 1)
                self.k += 1
                self.eng.wait_ge(self.s, self.base + self.k)

            def enter(self, base):
                self.base, self.k = base, 0

        feat_hi_k = feat_hi[:].rearrange("p (k t) -> p k t", k=KD)
        feat_lo_k = feat_lo[:].rearrange("p (k t) -> p k t", k=KD)
        mid_hi_k = mid_hi[:].rearrange("p (k t) -> p k t", k=CT)
        mid_lo_k = mid_lo[:].rearrange("p (k t) -> p k t", k=CT)
        yhy_hi_k = yhy_hi[:].rearrange("p (k t) -> p k t", k=CT)
        yhy_lo_k = yhy_lo[:].rearrange("p (k t) -> p k t", k=CT)
        xg_hi = mid_hi[:].rearrange("p (k s) -> p k s", k=KD)
        xg_lo = mid_lo[:].rearrange("p (k s) -> p k s", k=KD)
        wide_t = wide[:].rearrange("p (b d) -> p b d", b=TB)
        vt_c = vt.rearrange("p (c t) -> p c t", c=CT)
        z_flat = z_all[:].rearrange("p r n -> p (r n)")

        def pair(c):
            return bank[:, 2 * (c % 2):2 * (c % 2) + 2, :]

        block = ctx.enter_context(nc.Block())

        @block.sync
        def _(sp):
            def load(idx8, u, src):
                n = 8 * idx8 + u - RAW + 1
                if not static_le(n, 0):
                    sp.wait_ge(lo_done, n)
                sp.dma_start(raw[:, u % RAW], src).then_inc(ld[u % RAW], 16)

            def load_m(i8, u, src):
                sp.wait_ge(lo_done, 8 * i8 + (u - RAW_M + 1))
                if u < RAW:
                    sp.wait_ge(lo_done, 8 * M8 - RAW + u + 1)
                elif u == RAW:
                    sp.wait_ge(unit_done, 8 * M8)
                s = u % RAW_M
                sp.dma_start(slot_m(u), src).then_inc(ld[s], 16)

            def rows(w):
                return w.rearrange("(u j p) n -> u p j n", j=UK, p=P)

            win, why, wsg, wo = rows(w_in[0]), rows(w_hy_out[0]), rows(w_sg_out[0]), rows(w_out[0])
            def bias_chunk(k, col):
                sp.dma_start(bias[:, k], b_in[0:1, bass.ds(col, N)].partition_broadcast(P)).then_inc(bias_in[k], 16)

            for c in range(4):
                if c >= 2:
                    sp.wait_ge(S["biased"], c - 1)
                if c:
                    bias_chunk(c % 2, C_U + c * N)
                for u in range(8):
                    if c == 0 and u < D // N:
                        sp.dma_start(x_tok[:, :, u * N:(u + 1) * N],
                                     x[0].rearrange("(b p) d -> p b d", p=P)[:, :, u * N:(u + 1) * N]
                                     ).then_inc(x_in[u], 16)
                    load(A8 + c, u, win[u, :, :, C_U + c * N:C_U + (c + 1) * N])
                if c == 0:
                    bias_chunk(0, C_U)
            for c in range(2):
                for u in range(8):
                    load(B8 + c, u, win[u, :, :, 2 * W + c * N:2 * W + (c + 1) * N])
            with sp.Fori(2, 6) as c:
                for u in range(8):
                    load(B8 + c, u, win[u, :, :, bass.ds((c - 2) * N, N)])

            def gate_turns(p8, col, proj, biased):
                with sp.Fori(1, 3) as o:
                    for h in range(2):
                        sp.wait_ge(S["biased"], 2 * o + (biased + h - 3))
                        at = sp.snap((2 * o + h) * N)
                        bias_chunk(h, at + (col - 2 * N))
                        for u in range(8):
                            load(p8 - 3 + 3 * o, 12 * h + u, win[u, :, :, bass.ds(at + (col - 2 * N), N)])
                        for u in range(4):
                            load(p8 - 3 + 3 * o, 12 * h + 8 + u, proj[u, :, :, bass.ds(at - 2 * N, N)])

            gate_turns(C8, C_GSG, wsg, 4)
            gate_turns(D8, C_GHY, why, 8)
            sp.wait_ge(S["ot_ready"], 5)
            for b in range(TB):
                sp.dma_start(x2_tok[:, b], x[0, b * P:(b + 1) * P]).then_inc(S["x_again"], 16)
            with sp.Fori(0, 4) as c:
                for u in range(8):
                    load(E8 + c, u, wo[u, :, :, bass.ds(c * N, N)])

            def expert(i8, pos, e, kinds):
                for kind in kinds:
                    if kind in "gu":
                        w = (w_gate if kind == "g" else w_up)[0]
                        for u in range(8):
                            src = w[bass.ds(e, 1), u * UK * P:(u + 1) * UK * P, :].rearrange(
                                "e (j p) n -> p (e j) n", p=P)
                            load_m(i8, pos, src)
                            pos += 1
                    else:
                        for c in range(4):
                            for u in range(2):
                                src = w_down[0][bass.ds(e, 1), u * UK * P:(u + 1) * UK * P,
                                                c * N:(c + 1) * N].rearrange("e (j p) n -> p (e j) n", p=P)
                                load_m(i8, pos, src)
                                pos += 1
                return pos

            def group(i8, g):
                pos = expert(i8, 0, g * PER, "gu")
                for e in range(1, PER):
                    pos = expert(i8, pos, g * PER + e, "gu")
                    pos = expert(i8, pos, g * PER + e - 1, "d")
                assert expert(i8, pos, g * PER + PER - 1, "d") == 96

            with sp.Fori(0, GROUPS) as g:
                group(M8 + 12 * g, g)
            sp.wait_ge(S["route_ready"], 1)
            more = sp.value_load(rounds[0:1, 0:1], min_val=0, max_val=1)
            with sp.If(more != 0):
                with sp.Fori(0, GROUPS) as g:
                    group(M8 + 12 * GROUPS + 12 * g, g)
            n8 = more * (12 * GROUPS) + (M8 + 12 * GROUPS)
            for u in range(SPLIT):
                load_m(n8, u, w_gate[0, 0, u * UK * P:(u + 1) * UK * P, :].rearrange("(j p) n -> p j n", p=P))
            for b in range(TB):
                for h in range(D // N):
                    cols = slice(h * N, (h + 1) * N)
                    sp.wait_ge(S["y_out"], D // N * b + h + 1)
                    sp.dma_start(out[0, b * P:(b + 1) * P, cols], wide_t[:, b, cols]).then_inc(S["out_done"], 16)
            sp.wait_ge(S["out_done"], 16 * D // N * TB)

        @block.gpsimd
        def _(pool):
            pool.memset(minus_half[:], -0.5).then_inc(S["half_in"], 1)
            pool.wait_ge(S["half_in"], 1)
            for n in range(4):
                pool.wait_ge(S["var_ready"], n + 1)
                pool.tensor_tensor(rstd[:, n], var[:, n], minus_half[:], ALU.pow).then_inc(S["rstd_ready"], 1)

        @block.scalar
        def _(act):
            def split_hi(i8, u):
                act.wait_ge(ld[u % RAW], 16 * (i8 + u // RAW) + 16)
                n = 8 * i8 + u - SPLIT + 1
                if not static_le(n, 0):
                    act.wait_ge(unit_done, n)
                nc.scalar.activation(w_hi[:, u % SPLIT], raw[:, u % RAW], ACT.Copy).then_inc(hi_done, 1)

            def splits(i8, lo_, hi_, hooks={}):
                for u in range(lo_, hi_):
                    split_hi(i8, u)
                    for f in hooks.get(u, ()):
                        f()

            def splits_m(i8, i, hooks):
                for u in range(SPLIT, 96 + SPLIT):
                    act.wait_ge(ld[u % RAW_M], loaded_m(i, u))
                    act.wait_ge(unit_done, 8 * i8 + (u - SPLIT + 1))
                    nc.scalar.activation(w_hi[:, u % SPLIT], slot_m(u), ACT.Copy).then_inc(hi_done, 1)
                    for f in hooks.get(u, ()):
                        f()

            act.dma_start(ident[:], ident_in).then_inc(S["ident_ready"], 16)
            act.dma_start(g_mix[:], g_mix_c).then_inc(S["g_mix_in"], 16)

            def filter_load():
                for dst, src in ((fvec, filt_vec), (w1s, filt_w1[0]), (w2s, filt_w2), (zp, zpos)):
                    act.dma_start(dst[:], src).then_inc(S["filt_in"], 16)

            def consts_load():
                for dst, src in ((conv_w, conv_w_c), (conv_b, conv_b_c), (b_hy, b_hy_c), (sgb, sg_b_t),
                                 (before, before_in), (ones, ones_in), (slots, slots_in), (rank, rank_in),
                                 (wr, w_router), (brt, b_router.partition_broadcast(P))):
                    act.dma_start(dst[:], src).then_inc(S["consts_in"], 16)

            def x_evac(q):
                act.wait_ge(S["x_t"], q + 1)
                for j in range(2):
                    k = 2 * q + j
                    ins = nc.scalar.activation(feat_hi_k[:, k], bank[:, 4 + q % 4, j * L:(j + 1) * L], ACT.Copy,
                                               scale=g_mix[:, k:k + 1])
                    ins.then_inc(S["x_hi"], 1)

            def x_square(b):
                nc.scalar.activation(wide_t[:, b], x_tok[:, b], ACT.Square,
                                     accum_out=stat[:, b:b + 1]).then_inc(S["sumsq"], 1)

            def gelu(c):
                act.wait_ge(S["biased"], c + 1)
                nc.scalar.activation(wide_t[:, 0:2, bass.ds(c * N, N)], wide_t[:, 0:2, bass.ds(c * N, N)],
                                     ACT.Gelu).then_inc(S["gelu_done"], 1)

            def filter_sine(n, dst):
                act.wait_ge(S["f_arg"], n)
                nc.scalar.activation(dst, filt_c[0:HID if n == 1 else P], ACT.Sin).then_inc(S["f_sin"], 1)

            def z_evac(c, parity):
                act.wait_ge(unit_done, 8 * (B8 + c) + 8)
                for b in range(TB):
                    ins = nc.scalar.activation(zt[:, b], pair(parity)[:, b], ACT.Copy, scale=rstd[:, 0, b:b + 1])
                ins.then_inc(S["zt_ready"], 1)

            def z_bias(c):
                act.wait_ge(S["z_t"], c + 1)
                act.wait_ge(S["consts_in"], 16 * CONSTS)
                if not static_le(c, 0):
                    act.wait_ge(S["conv_done"], c)
                for j in range(4):
                    ins = nc.scalar.activation(zpad[:, j, 1:L + 1], bank[:, 4 + j // 2, (j % 2) * L:(j % 2 + 1) * L],
                                               ACT.Identity, bias=b_hy[:, bass.ds(4 * c + j, 1)])
                ins.then_inc(S["zpad_ready"], 1)

            def mix_evac_hi():
                act.wait_ge(S["ysg_t"], 1)
                for q in range(4):
                    nc.scalar.activation(mid_hi[:, q * N:(q + 1) * N], bank[:, 4 + q],
                                         ACT.Copy).then_inc(S["ysg_hi"], 1)

            def ln_load():
                act.wait_ge(S["a2_ready"], 1)
                act.dma_start(lng[:], ln_g.partition_broadcast(P)).then_inc(S["sg_in"], 16)
                act.dma_start(lnb[:], ln_b.partition_broadcast(P)).then_inc(S["sg_in"], 16)
                act.dma_start(sgw[:], sg_w_t).then_inc(S["sg_in"], 16)

            def table_load():
                act.wait_ge(S["mix_done"], 1)
                act.dma_start(dft_f[:], dft).then_inc(S["tables_in"], 16)
                act.dma_start(dft_i[:], idft).then_inc(S["tables_in"], 16)

            act.wait_ge(S["g_mix_in"], 16)
            x_evac(0)
            splits(A8, 0, 52, {
                **{u: [lambda u=u: x_evac(u + 1)] for u in range(7)},
                7: [filter_load, lambda: x_square(0)], 8: [lambda: x_square(1)], 9: [consts_load],
                12: [lambda: gelu(0)], 14: [lambda: filter_sine(1, filt_a[0:HID])],
                18: [lambda: filter_sine(2, a2[:, 0])], 22: [ln_load], 20: [lambda: gelu(1)], 28: [lambda: gelu(2)],
                36: [lambda: gelu(3)], 43: [lambda: z_evac(0, 0)], 45: [lambda: z_bias(0)],
                49: [table_load], 51: [lambda: z_evac(1, 1), mix_evac_hi]})
            with act.Fori(1, 3) as h:
                for p in range(2):
                    splits(B8 + 2 * h + p, 4, 12, {6: [lambda: z_bias(2 * h + p - 1)],
                                                   10: [lambda: z_evac(2 * h + p, p)]})
            z_bias(5)

            def h3_load(o, h):
                w3v = filt_w3[0].rearrange("h (d o n) -> d h o n", d=2, o=2)
                for d in range(2):
                    act.dma_start(w3s[d * HID:(d + 1) * HID, :],
                                  w3v[d, :, bass.ds(o, 1), h * N:(h + 1) * N].rearrange("h o n -> h (o n)")
                                  ).then_inc(S[f"h3_in_{h}"], 16)
                act.dma_start(dec[:], decay[:, :, h * N:(h + 1) * N]).then_inc(S[f"h3_in_{h}"], 16)
                act.dma_start(hp_skip[:], hy_skip[0, bass.ds(o, 1), h * N:(h + 1) * N]).then_inc(S[f"h3_in_{h}"], 16)

            def v_evac(o):
                for q in range(4):
                    act.wait_ge(S["v_t"], 4 * o + q + 1)
                    c, b = 4 * (q // 2), q % 2
                    nc.scalar.activation(v_tok[:, b, c * P:(c + 4) * P], bank[:, 4 + q], ACT.Copy
                                         ).then_inc(S["vtok_ready"], 1)

            def odd_evac(s, made, free, free_count, done):
                for f in range(2):
                    act.wait_ge(S[made], 2 * s + f + 1)
                    act.wait_ge(S[free], free_count(f))
                    nc.scalar.activation(odd[:, f], bank[:, 5 + 2 * f], ACT.Copy).then_inc(S[done], 1)

            def k_odd(s):
                odd_evac(s, "k_mm", "y_ready", lambda f: s + 1, "k_odd")

            def u_odd(s):
                odd_evac(s, "u_mm", "k_ready", lambda f: 2 * s + f + 1, "u_odd")

            def sigmoid(n):
                act.wait_ge(S["biased"], n + 5)
                nc.scalar.activation(sig[:], sig[:], ACT.Sigmoid).then_inc(S["sig_ready"], 1)

            def next_h3(s, o, h):
                act.wait_ge(S["hsd_ready"], 2 * s + 2)
                h3_load(o, h)

            h3_load(0, 0)
            with act.Fori(0, 2) as o:
                splits(C8 + 3 * o, 4, 28, {
                    4: [lambda: v_evac(o)],
                    6: [lambda: k_odd(2 * o)],
                    7: [lambda: next_h3(2 * o, o, 1)],
                    8: [lambda: u_odd(2 * o)],
                    11: [lambda: sigmoid(2 * o)],
                    17: [lambda: k_odd(2 * o + 1)],
                    20: [lambda: next_h3(2 * o + 1, 1, 0)],
                    19: [lambda: u_odd(2 * o + 1)],
                    23: [lambda: sigmoid(2 * o + 1)]})
            act.wait_ge(S["ot_ready"], 5)
            nc.scalar.activation(yhy_hi[:], vt, ACT.Copy).then_inc(S["yhy_hi_s"], 1)

            def m_evac(n, dst):
                act.wait_ge(S["m_t"], n + 1)
                for q in range(2):
                    ins = nc.scalar.activation(dst[:, q * N:(q + 1) * N], bank[:, 4 + q], ACT.Copy)
                ins.then_inc(S["m_hi"], 1)

            for o in range(2):
                splits(D8 + 3 * o, 4, 28, {
                    11: [lambda: sigmoid(4 + 2 * o)],
                    19: [lambda: m_evac(o, mid_hi[:, o * 2 * N:(o + 1) * 2 * N])],
                    23: [lambda: sigmoid(4 + 2 * o + 1)]})
            act.wait_ge(S["yhy_lo_s"], 1)
            act.dma_start(gf_row[:], g_ffn.partition_broadcast(P)).then_inc(S["gf_in"], 16)
            act.wait_ge(S["h3_in_0"], 192)
            act.dma_start(gl_row[:], g_final.partition_broadcast(P)).then_inc(S["gl_in"], 16)
            m_evac(2, feat_hi[:, 2 * N:4 * N])

            def square(c):
                act.wait_ge(S["x_mid"], c + 1)
                for b in range(TB):
                    nc.scalar.activation(sig[:, b], x2_tok[:, b, c * N:(c + 1) * N], ACT.Square,
                                         accum_out=stat[:, 48 + 4 * b + c:49 + 4 * b + c]).then_inc(S["sumsq2"], 1)

            def h_evac(c):
                act.wait_ge(S["h_tr"], c + 1)
                nc.scalar.activation(h_t[:, 4 * c:4 * c + 2].rearrange("p k t -> p (k t)"), bank[:, 4],
                                     ACT.Copy).then_inc(S["h_ev_act"], 1)

            hooks = {4: [lambda: m_evac(3, feat_hi[:, 6 * N:8 * N])]}
            for c in range(3):
                hooks[8 * c + 12] = [lambda c=c: square(c)]
                hooks[8 * c + 15] = [lambda c=c: h_evac(c)]
            hooks[34] = [lambda: square(3), lambda: h_evac(3)]
            splits(E8, 4, 36, hooks)
            act.wait_ge(S["rstd_ready"], 3)
            act.wait_ge(S["h_tr"], 4)
            for b in range(TB):
                nc.scalar.activation(wide_t[:, b], wide_t[:, b], ACT.Copy,
                                     scale=rstd[:, 2, b:b + 1]).then_inc(S["h_norm"], 1)
            act.wait_ge(S["r_mm"], 1)
            nc.scalar.activation(perm_t[:, 0:P], ident[:], ACT.Copy, scale=0.0)
            nc.scalar.activation(perm_t[:, P:2 * P], ident[:], ACT.Copy, scale=0.0).then_inc(S["perm_t_s"], 1)
            act.wait_ge(S["r_log"], 1)
            nc.scalar.activation(oh[:, 1], oh[:, 0], ACT.Exp).then_inc(S["r_exp"], 1)
            act.wait_ge(S["r_m12"], 1)
            nc.scalar.activation(stat[:, 16:18], stat[:, 14:16], ACT.Exp).then_inc(S["r_exp2"], 1)

            def gather_evac(n, q, src):
                act.wait_ge(S["ga_mm"], 4 * n + q + 1)
                nc.scalar.activation(mid_hi[:, q * N:(q + 1) * N], bank[:, src], ACT.Copy).then_inc(S["ga_hi"], 1)

            def y_evac(q):
                nc.scalar.activation(y_hi[:, q * N:(q + 1) * N], bank[:, 4 + q], ACT.Copy).then_inc(S["yg_hi"], 1)

            for q in range(4):
                nc.scalar.activation(y_lo[:, q * N:(q + 1) * N], x2_tok[:, 0, q * N:(q + 1) * N], ACT.Copy)
                nc.scalar.activation(y_hi[:, q * N:(q + 1) * N], x2_tok[:, 0, q * N:(q + 1) * N], ACT.Copy
                                     ).then_inc(S["yg_hi"], 1)
            for q in range(4):
                gather_evac(0, q, 4 + q)

            def group(i8, i):
                def y_evac_here(q):
                    act.wait_ge(unit_done, 8 * i8 + (90 + 2 * q))
                    y_evac(q)

                def perm_evac():
                    act.wait_ge(S["perm_tr"], i + 1)
                    act.wait_ge(S["sc_mm"], 8 * i + 8)
                    nc.scalar.activation(perm_t[:], bank[:, 3, 0:L], ACT.Copy).then_inc(S["perm_t_s"], 1)

                def silu(e):
                    act.wait_ge(unit_done, 8 * i8 + GATE_AT[e] + 8)
                    if e:
                        act.wait_ge(S["prod_done"], PER * i + e)
                    else:
                        act.wait_ge(S["ga_lo"], 4 * i + 4)
                    nc.scalar.activation(sil[:], bank[:, 0], ACT.Silu).then_inc(S["silu_done"], 1)

                def act_split_hi(e):
                    act.wait_ge(S["act_t"], PER * i + e + 1)
                    if e >= 2:
                        act.wait_ge(unit_done, 8 * i8 + DOWN_AT[e - 2] + 8)
                    nc.scalar.activation(act_hi[:, e % 2], bank[:, 2], ACT.Copy).then_inc(S["act_hi_s"], 1)

                hooks = {11: [lambda: silu(0)], 19: [perm_evac]}
                for e in range(1, PER):
                    hooks[GATE_AT[e] + 11] = [lambda e=e: act_split_hi(e - 1), lambda e=e: silu(e)]
                hooks[87] = [lambda: act_split_hi(PER - 1)]
                for q in range(4):
                    hooks.setdefault(GATHER_AT[q] + 4, []).append(lambda q=q: gather_evac(i + 1, q, GATHER_BANK[q]))
                    hooks.setdefault((93, 95, 97, 98)[q], []).append(lambda q=q: y_evac_here(q))
                splits_m(i8, i, hooks)

            with act.Fori(0, GROUPS) as g:
                group(M8 + 12 * g, g)
            act.wait_ge(S["route_ready"], 1)
            more = act.value_load(rounds[0:1, 0:1], min_val=0, max_val=1)
            with act.If(more != 0):
                with act.Fori(0, GROUPS) as g:
                    group(M8 + 12 * GROUPS + 12 * g, GROUPS + g)
            n = more * GROUPS + GROUPS
            for s in range(8):
                b, q = s % 2, s // 2
                act.wait_ge(S["sc_add"], 8 * n + s + 1)
                nc.scalar.activation(wide_t[:, b, q * N:(q + 1) * N], x2_tok[:, b, q * N:(q + 1) * N], ACT.Square,
                                     accum_out=stat[:, 56 + 4 * b + q:57 + 4 * b + q]).then_inc(S["sumsq3"], 1)

        @block.vector
        def _(dve):
            order = Order(dve, S["dve_order"])
            link = order.link
            V = nc.vector

            def splits(i8, lo_, hi_, hooks={}, slot=lambda u: raw[:, u % RAW]):
                for u in range(lo_, hi_):
                    dve.wait_ge(hi_done, 8 * i8 + u + 1)
                    V.tensor_tensor(w_lo[:, u % SPLIT], slot(u), w_hi[:, u % SPLIT],
                                    ALU.subtract).then_inc(lo_done, 1)
                    for f in hooks.get(u, ()):
                        f()

            def mean_square(n, src):
                V.tensor_scalar(var[:, n], src, 1.0 / D, EPS, ALU.mult, ALU.add).then_inc(S["var_ready"], 1)

            def x_evac(q):
                dve.wait_ge(S["x_hi"], 2 * q + 2)
                for j in range(2):
                    k = 2 * q + j
                    V.scalar_tensor_tensor(feat_lo_k[:, k], bank[:, 4 + q % 4, j * L:(j + 1) * L], g_mix[:, k:k + 1],
                                           feat_hi_k[:, k], ALU.mult, ALU.subtract).then_inc(S["x_lo"], 1)

            def x_norm():
                dve.wait_ge(S["sumsq"], TB)
                mean_square(0, stat[:, 0:2])

            def filter_arg(n, h, bcol):
                dve.wait_ge(S["f_mm"], n)
                link(V.tensor_scalar(filt_b[0:h], bank[0:h, 4, 0:L], fvec[0:h, bcol:bcol + 1], fvec[0:h, 0:1],
                                     ALU.add, ALU.mult))
                link(V.tensor_scalar(filt_c[0:h], filt_b[0:h], 1.0 / (2.0 * math.pi), MAGIC, ALU.mult, ALU.add))
                link(V.tensor_scalar(filt_c[0:h], filt_c[0:h], MAGIC, None, ALU.subtract))
                link(V.scalar_tensor_tensor(filt_b[0:h], filt_c[0:h], -PI_HI, filt_b[0:h], ALU.mult, ALU.add))
                link(V.scalar_tensor_tensor(filt_b[0:h], filt_c[0:h], -PI_LO, filt_b[0:h], ALU.mult, ALU.add))
                V.tensor_scalar(filt_c[0:h], filt_b[0:h], math.pi, -math.pi, ALU.min, ALU.max).then_inc(S["f_arg"], 1)

            def filter_sign():
                dve.wait_ge(S["f_sin"], 2)
                V.tensor_scalar(a2[:, 1], a2[:, 0], fvec[:, 3:4], None, ALU.mult).then_inc(S["a2_ready"], 1)

            def sg_add(c, par):
                dve.wait_ge(unit_done, 8 * (A8 + c) + 8)
                dve.wait_ge(bias_in[par], 16 * (c // 2 + 1))
                dve.wait_ge(S["rstd_ready"], 1)
                for b in range(TB):
                    ins = V.scalar_tensor_tensor(wide_t[:, b, c * N:(c + 1) * N], pair(par)[:, b],
                                                 rstd[:, 0, b:b + 1], bias[:, par], ALU.mult, ALU.add)
                ins.then_inc(S["biased"], 1)

            moments = stat[:, 8:12].rearrange("p (b m) -> p b m", m=2)

            def ln_moments():
                dve.wait_ge(S["gelu_done"], 4)
                for b in range(TB):
                    for s in range(2):
                        link(V.bn_stats(oh_flat[:, 6 * s:6 * s + 6], wide_t[:, b, W + s * N:W + (s + 1) * N]))
                    link(V.bn_aggr(stat[:, 8 + 2 * b:10 + 2 * b], oh_flat[:, 0:12]))
                V.tensor_scalar(var[:, 1], moments[:, :, 1], EPS, None, ALU.add).then_inc(S["var_ready"], 1)

            def layer_norm(b):
                dve.wait_ge(S["sg_in"], 48)
                dve.wait_ge(S["rstd_ready"], 2)
                v = wide_t[:, b, W:2 * W]
                link(V.tensor_scalar(v, v, moments[:, b, 0:1], rstd[:, 1, b:b + 1], ALU.subtract, ALU.mult))
                link(V.tensor_tensor(v, v, lng[:], ALU.mult))
                V.tensor_tensor(v, v, lnb[:], ALU.add).then_inc(S["ln_done"], 1)

            oh_flat = oh[:].rearrange("p a b c -> p (a b c)")

            def mix():
                dve.wait_ge(S["mix_done"], 1)
                for g in range(8):
                    V.scalar_tensor_tensor(wide_t[:, :, g * P:(g + 1) * P],
                                           bank[:, 4 + g // 2, (g % 2) * L:(g % 2 + 1) * L].rearrange(
                                               "p (b k) -> p b k", b=TB),
                                           sgb[:, g:g + 1], wide_t[:, :, g * P:(g + 1) * P],
                                           ALU.add, ALU.mult).then_inc(S["ysg"], 1)

            def mix_evac_lo():
                for q in range(4):
                    dve.wait_ge(S["ysg_hi"], q + 1)
                    V.tensor_tensor(mid_lo[:, q * N:(q + 1) * N], bank[:, 4 + q], mid_hi[:, q * N:(q + 1) * N],
                                    ALU.subtract).then_inc(S["ysg_lo"], 1)

            def conv(c):
                dve.wait_ge(S["zpad_ready"], c + 1)
                dve.wait_ge(S["consts_in"], 16 * CONSTS)
                dst = z_flat[:, bass.ds(c * 4 * L, 4 * L)].rearrange("p (j t) -> p j t", j=4)
                w = conv_w[:, bass.ds(4 * c, 4), :]
                cb = conv_b[:, bass.ds(4 * c, 4)]
                for tap in range(3):
                    for j in range(4):
                        z = zpad[:, j, tap:tap + L]
                        if tap == 0:
                            ins = V.tensor_scalar(dst[:, j], z, w[:, j, 0:1], cb[:, j:j + 1], ALU.mult, ALU.add)
                        else:
                            ins = V.scalar_tensor_tensor(dst[:, j], z, w[:, j, tap:tap + 1], dst[:, j],
                                                         ALU.mult, ALU.add)
                    if tap < 2:
                        link(ins)
                ins.then_inc(S["conv_done"], 1)

            def pad_borders():
                link(V.memset(zpad[:, :, 0:1], 0.0))
                link(V.memset(zpad[:, :, L + 1:L + 2], 0.0))

            hooks = {8 * c + 11: [lambda c=c: sg_add(c, c % 2)] for c in range(4)}
            hooks.update({32: [pad_borders], 37: [ln_moments], 39: [lambda: layer_norm(0)], 41: [lambda: layer_norm(1)],
                          45: [lambda: conv(0)], 47: [mix], 51: [mix_evac_lo]})
            hooks.update({u: [lambda u=u: x_evac(u + 1)] for u in range(7)})
            hooks[9] = [x_norm]
            hooks[14] = [lambda: filter_arg(1, HID, 1)]
            hooks[18] = [lambda: filter_arg(2, P, 2)]
            hooks[20] = [filter_sign]
            x_evac(0)
            splits(A8, 0, 52, hooks)
            k0 = order.base + order.k
            with dve.Fori(1, 3) as h:
                order.enter(k0 + 4 * (h - 1))
                for p in range(2):
                    splits(B8 + 2 * h + p, 4, 12, {6: [lambda: conv(2 * h + p - 1)]})
                assert order.k == 4
            order.enter(k0 + 8)
            conv(5)
            dve.wait_ge(S["conv_done"], 6)
            dve.sem_inc(S["ot_ready"], 1)
            dve.sem_inc(S["y_ready"], 1)
            dve.sem_inc(S["merged_ready"], 1)

            def h_evac(s, o, h):
                dve.wait_ge(S["filt_mm"], s + 1)
                dve.wait_ge(S[f"h3_in_{h}"], 64 * o + 64)
                link(V.tensor_tensor(prod_y[:, 0:2], bank[:, 4:6], dec[:], ALU.mult))
                V.tensor_tensor(prod_y[0:1, 0], prod_y[0:1, 0], hp_skip[:], ALU.add).then_inc(S["hsd_ready"], 1)
                V.tensor_tensor(prod_y[:, 2:4], bank[:, 6:8], dec[:], ALU.mult).then_inc(S["hsd_ready"], 1)

            def response_sums(s):
                for f in range(2):
                    dve.wait_ge(S["k_mm"], 2 * s + f + 1)
                    dve.wait_ge(S["k_odd"], 2 * s + f + 1)
                    even = bank[:, 4 + 2 * f]
                    V.tensor_tensor(k_resp[:, 2 * f], even, odd[:, f], ALU.add)
                    if f == 0:
                        V.tensor_tensor(k_resp[:, 1], even, odd[:, 0], ALU.subtract).then_inc(S["k_ready"], 1)
                    else:
                        V.tensor_tensor(k_resp[:, 3], odd[:, 1], even, ALU.subtract).then_inc(S["k_ready"], 1)

            def spectrum_sums(s):
                dve.wait_ge(S["u_mm"], 2 * s + 1)
                dve.wait_ge(S["u_odd"], 2 * s + 1)
                V.tensor_tensor(bank[:, 5], bank[:, 4], odd[:, 0], ALU.subtract)
                V.tensor_tensor(bank[:, 4], bank[:, 4], odd[:, 0], ALU.add)
                dve.wait_ge(S["u_mm"], 2 * s + 2)
                dve.wait_ge(S["u_odd"], 2 * s + 2)
                V.tensor_tensor(bank[:, 7], odd[:, 1], bank[:, 6], ALU.subtract)
                link(V.tensor_tensor(bank[:, 6], bank[:, 6], odd[:, 1], ALU.add))
                dve.wait_ge(S["k_ready"], 2 * s + 2)

            uc, us = bank[:, 4:6], bank[:, 6:8]
            kc, ks = k_resp[:, 0:2], k_resp[:, 2:4]
            yc, ys = prod_y[:, 0:2], prod_y[:, 2:4]

            def products_cos(s):
                link(V.tensor_tensor(yc, uc, kc, ALU.mult))
                link(V.tensor_tensor(odd[:], us, ks, ALU.mult))
                link(V.tensor_tensor(yc, yc, odd[:], ALU.subtract))

            def products_sin(s):
                link(V.tensor_tensor(ys, uc, ks, ALU.mult))
                link(V.tensor_tensor(odd[:], us, kc, ALU.mult))
                link(V.tensor_tensor(ys, ys, odd[:], ALU.add))

            def product_sums(s):
                V.tensor_tensor(k_resp[:, 0], yc[:, 0], yc[:, 1], ALU.add)
                V.tensor_tensor(k_resp[:, 1], yc[:, 0], yc[:, 1], ALU.subtract)
                V.tensor_tensor(k_resp[:, 2], ys[:, 0], ys[:, 1], ALU.subtract)
                V.tensor_tensor(k_resp[:, 3], ys[:, 0], ys[:, 1], ALU.add).then_inc(S["y_ready"], 1)

            def ot(s, o, h):
                dve.wait_ge(S["inv_mm"], s + 1)
                src = bank[:, 4:6].rearrange("p b (j two t) -> p (b j) two t", j=2, two=2)
                dst = z_flat[:, h * 4 * L:(h + 1) * 4 * L].rearrange("p (j t two) -> p j two t", j=4, two=2)
                x_o = z_flat[:, bass.ds(o * CT * L + (CT + 4 * h) * L, 4 * L)].rearrange(
                    "p (j t two) -> p j two t", j=4, two=2)
                for par in range(2):
                    ins = V.tensor_tensor(dst[:, :, par], src[:, :, par], x_o[:, :, par], ALU.mult)
                ins.then_inc(S["ot_ready"], 1)

            def gate_add(n, par, turn):
                dve.wait_ge(bias_in[par], 16 * (turn + 3))
                for b in range(TB):
                    ins = V.scalar_tensor_tensor(sig[:, b], bank[:, b], rstd[:, 0, b:b + 1], bias[:, par],
                                                 ALU.mult, ALU.add)
                ins.then_inc(S["biased"], 1)

            def merge(n, chunk, add):
                dve.wait_ge(S["sig_ready"], n + 1)
                dst = wide_t[:, :, bass.ds(chunk * N, N)]
                if add:
                    link(V.tensor_tensor(sig[:], bank[:, 2:4], sig[:], ALU.mult))
                    V.tensor_tensor(dst, dst, sig[:], ALU.add).then_inc(S["merged_ready"], 1)
                else:
                    V.tensor_tensor(dst, bank[:, 2:4], sig[:], ALU.mult).then_inc(S["merged_ready"], 1)

            def gate_done(i8, u):
                dve.wait_ge(unit_done, 8 * i8 + u)

            def turn(i8, n0, t0, o, add, extra):
                hooks = {}
                def g0():
                    gate_done(i8, 8)
                    gate_add(n0, 0, t0)
                def p0():
                    gate_done(i8, 12)
                    merge(n0, 2 * o, add)
                def g1():
                    gate_done(i8, 20)
                    gate_add(n0 + 1, 1, t0)
                hooks[10] = [g0]
                hooks[15] = [p0]
                hooks[23] = [g1]
                def p1():
                    gate_done(i8, 24)
                    merge(n0 + 1, 2 * o + 1, add)
                hooks[27] = [p1]
                for u, fs in extra.items():
                    hooks[u] = fs + hooks.get(u, [])
                splits(i8, 4, 28, hooks)

            k0 = order.base + order.k
            per = 2 * (1 + 1 + 6)
            with dve.Fori(0, 2) as o:
                order.enter(k0 + per * o)
                turn(C8 + 3 * o, 2 * o, o, o, False, {
                    5: [lambda: h_evac(2 * o, o, 0)],
                    6: [lambda: response_sums(2 * o)],
                    8: [lambda: spectrum_sums(2 * o)],
                    9: [lambda: products_cos(2 * o)],
                    11: [lambda: products_sin(2 * o)],
                    12: [lambda: product_sums(2 * o)],
                    15: [lambda: ot(2 * o, o, 0)],
                    16: [lambda: h_evac(2 * o + 1, o, 1)],
                    17: [lambda: response_sums(2 * o + 1)],
                    19: [lambda: spectrum_sums(2 * o + 1)],
                    20: [lambda: products_cos(2 * o + 1)],
                    21: [lambda: products_sin(2 * o + 1)],
                    23: [lambda: product_sums(2 * o + 1)],
                    26: [lambda: ot(2 * o + 1, o, 1)]})
                assert order.k == per, order.k
            order.enter(k0 + 2 * per)
            dve.wait_ge(S["yhy_hi_s"], 1)
            V.tensor_tensor(yhy_lo[:], vt, yhy_hi[:], ALU.subtract).then_inc(S["yhy_lo_s"], 1)

            def m_evac(n, hi, lo):
                dve.wait_ge(S["m_hi"], n + 1)
                for q in range(2):
                    ins = V.tensor_tensor(lo[:, q * N:(q + 1) * N], bank[:, 4 + q], hi[:, q * N:(q + 1) * N],
                                          ALU.subtract)
                ins.then_inc(S["m_lo"], 1)

            for o in range(2):
                turn(D8 + 3 * o, 4 + 2 * o, 2 + o, o, True,
                     {19: [lambda: m_evac(o, *(m[:, o * 2 * N:(o + 1) * 2 * N] for m in (mid_hi, mid_lo)))]})
            m_evac(2, feat_hi[:, 2 * N:4 * N], feat_lo[:, 2 * N:4 * N])

            def residual(c):
                dve.wait_ge(unit_done, 8 * (E8 + c) + 8)
                if c == 0:
                    dve.wait_ge(S["x_again"], 16 * TB)
                    dve.wait_ge(S["gf_in"], 16)
                cols = slice(c * N, (c + 1) * N)
                dst = x2_tok[:, :, cols]
                V.tensor_tensor(dst, bank[:, 2 * (c % 2):2 * (c % 2) + 2], dst, ALU.add).then_inc(S["x_mid"], 1)
                dve.wait_ge(S["x_mid"], c + 1)
                for b in range(TB):
                    ins = V.tensor_tensor(wide_t[:, b, cols], x2_tok[:, b, cols], gf_row[:, cols], ALU.mult)
                ins.then_inc(S["h_ready"], 1)

            def h_evac(c):
                dve.wait_ge(S["h_tr"], c + 1)
                V.tensor_copy(h_t[:, 4 * c + 2:4 * c + 4].rearrange("p k t -> p (k t)"), bank[:, 5]
                              ).then_inc(S["h_ev_dve"], 1)

            hooks = {4: [lambda: m_evac(3, feat_hi[:, 6 * N:8 * N], feat_lo[:, 6 * N:8 * N])]}
            for c in range(3):
                hooks[8 * c + 11] = [lambda c=c: residual(c)]
                hooks[8 * c + 15] = [lambda c=c: h_evac(c)]
            splits(E8, 4, 35, hooks)
            residual(3)
            h_evac(3)

            dve.wait_ge(S["sumsq2"], 4 * TB)
            link(V.tensor_reduce(stat[:, 4:6], stat[:, 48:56].rearrange("p (b c) -> p b c", b=TB), AX, ALU.add))
            mean_square(2, stat[:, 4:6])
            link(V.memset(posi[:, 8], -1.0))
            dve.wait_ge(S["rstd_ready"], 3)
            dve.wait_ge(S["r_mm"], 1)
            for b in range(TB):
                ins = V.scalar_tensor_tensor(logits[:, b], bank[:, 6 + b, 0:20], rstd[:, 2, b:b + 1], brt[:, b],
                                             ALU.mult, ALU.add)
            link(ins)
            lg = logits[:, :, 0:4]
            le = logits[:, :, 4:20].rearrange("p b (g e) -> p b g e", g=GROUPS)

            def bc4(v):
                return v.unsqueeze(2).to_broadcast([P, TB, 4])

            mg, m1, m2 = stat[:, 24:26], stat[:, 26:28], stat[:, 28:30]
            tie = stat[:, 30:32]

            def first_max(dst, vals, m):
                link(V.tensor_reduce(m, vals, AX, ALU.max))
                link(V.tensor_tensor(dst, vals, bc4(m), ALU.is_equal))
                link(V.tensor_tensor(dst, dst, rank[:], ALU.mult))
                link(V.tensor_reduce(tie, dst, AX, ALU.max))
                link(V.tensor_tensor(dst, dst, bc4(tie), ALU.is_equal))

            def make_perm(i):
                pv = posi[:, bass.ds(i, 1), :].rearrange("p i b -> p (i b)")
                for b in range(TB):
                    ins = V.tensor_scalar(perm[:, b], slots[:], pv[:, b:b + 1], None, ALU.is_equal)
                ins.then_inc(S["perm_ready"], 1)

            G1 = oh[:, 2]
            E1, E2, le1, le2 = oh[:, 3], oh[:, 4], oh[:, 5], oh[:, 6]
            first_max(G1, lg, mg)
            dve.sem_inc(S["oh_ready"], 1)
            link(V.tensor_tensor(oh[:, 0], lg, bc4(mg), ALU.subtract))
            dve.sem_inc(S["r_log"], 1)
            sel = lesel[:].rearrange("p b (g e) -> p b g e", g=GROUPS)
            for b in range(TB):
                ins = V.tensor_tensor(sel[:, b], le[:, b], G1[:, b].unsqueeze(2).to_broadcast([P, 4, 4]), ALU.mult)
            link(ins)
            link(V.tensor_reduce(le1, sel.rearrange("p b g e -> p b e g"), AX, ALU.add))
            dve.wait_ge(S["pos_mm"], 1)
            pos = oh[:, 8]
            for b in range(TB):
                ins = V.scalar_tensor_tensor(pos[:, b], bank[:, 2 + b, 32:36], 1.0, G1[:, b], ALU.add, ALU.mult)
            link(ins)
            for r in range(2):
                for b in range(TB):
                    ins = V.tensor_scalar(posi[:, 4 * r:4 * r + 4, b], pos[:, b], 1.0 + CAP * r, None, ALU.subtract)
                link(ins)
                if r == 0:
                    make_perm(0)
            link(V.tensor_copy(oh[:, 9, 0], bank[:, 2, 64:68]))
            link(V.tensor_reduce(stat[:, 40:41], oh[:, 9, 0], AX, ALU.max))
            link(V.tensor_scalar(stat[:, 41:42], stat[:, 40:41], CAP + 0.5, None, ALU.is_gt))
            link(V.tensor_copy(rounds[:], stat[:, 41:42]))
            first_max(E1, le1, m1)
            link(V.scalar_tensor_tensor(le2, E1, -3.0e38, le1, ALU.mult, ALU.add))
            first_max(E2, le2, m2)
            link(V.tensor_tensor(stat[:, 14:16], m2, m1, ALU.subtract))
            dve.sem_inc(S["r_m12"], 1)
            dve.wait_ge(S["r_exp"], 1)
            psel = stat[:, 32:34]
            link(V.tensor_reduce(psel, oh[:, 1], AX, ALU.add))
            dve.wait_ge(S["r_exp2"], 1)
            t2, w1_, w2_ = stat[:, 16:18], stat[:, 34:36], stat[:, 36:38]
            link(V.tensor_scalar(w1_, t2, 1.0, None, ALU.add))
            link(V.tensor_tensor(w1_, w1_, psel, ALU.mult))
            link(V.reciprocal(w1_, w1_))
            link(V.tensor_tensor(w2_, w1_, t2, ALU.mult))
            link(V.tensor_tensor(comb[:], E1, bc4(w1_), ALU.mult))
            link(V.tensor_tensor(oh[:, 7], E2, bc4(w2_), ALU.mult))
            link(V.tensor_tensor(comb[:], comb[:], oh[:, 7], ALU.add))
            dve.sem_inc(S["route_ready"], 1)

            def gather_evac(n, q, src):
                dve.wait_ge(S["ga_hi"], 4 * n + q + 1)
                V.tensor_tensor(mid_lo[:, q * N:(q + 1) * N], bank[:, src], mid_hi[:, q * N:(q + 1) * N],
                                ALU.subtract).then_inc(S["ga_lo"], 1)

            def y_evac(n, q):
                dve.wait_ge(S["yg_hi"], 4 * n + q + 1)
                V.tensor_tensor(y_lo[:, q * N:(q + 1) * N], bank[:, 4 + q], y_hi[:, q * N:(q + 1) * N],
                                ALU.subtract).then_inc(S["yg_lo"], 1)

            def scatter_add(n, s, src):
                dve.wait_ge(S["sc_mm"], 8 * n + s + 1)
                dst = x2_tok[:, s % 2, (s // 2) * N:(s // 2 + 1) * N]
                V.tensor_tensor(dst, bank[:, src], dst, ALU.add).then_inc(S["sc_add"], 1)

            def combg_copy(n):
                dve.wait_ge(S["comb_mm"], n + 1)
                if not static_le(n, 0):
                    dve.wait_ge(S["prod_done"], PER * n)
                V.tensor_copy(combg[:], bank[:, 2, 0:4]).then_inc(S["combg_s"], 1)

            splits(E8, 35, 36)
            dve.wait_ge(S["yg_hi"], 4)
            dve.sem_inc(S["yg_lo"], 4)
            for q in range(4):
                gather_evac(0, q, 4 + q)
            combg_copy(0)

            def group(i8, i):
                def product(e):
                    dve.wait_ge(S["silu_done"], PER * i + e + 1)
                    dve.wait_ge(unit_done, 8 * i8 + GATE_AT[e] + 16)
                    if e:
                        dve.wait_ge(S["act_t"], PER * i + e)
                    else:
                        dve.wait_ge(S["combg_s"], i + 1)
                    V.scalar_tensor_tensor(prod[:], bank[:, 1], combg[:, e:e + 1], sil[:],
                                           ALU.mult, ALU.mult).then_inc(S["prod_done"], 1)

                def act_split_lo(e):
                    dve.wait_ge(S["act_hi_s"], PER * i + e + 1)
                    V.tensor_tensor(act_lo[:, e % 2], bank[:, 2], act_hi[:, e % 2],
                                    ALU.subtract).then_inc(S["act_lo_s"], 1)

                def next_perm():
                    dve.wait_ge(S["perm_tr"], i + 1)
                    make_perm(i + 1)

                hooks = {60: [next_perm], 84: [lambda: combg_copy(i + 1)]}
                for e in range(PER):
                    hooks.setdefault(GATE_AT[e] + 19, []).append(lambda e=e: product(e))
                for e in range(1, PER):
                    hooks.setdefault(GATE_AT[e] + 11, []).append(lambda e=e: act_split_lo(e - 1))
                hooks[87] = [lambda: act_split_lo(PER - 1)]
                for q in range(4):
                    hooks.setdefault(GATHER_AT[q] + 4, []).append(lambda q=q: gather_evac(i + 1, q, GATHER_BANK[q]))
                    hooks.setdefault((93, 95, 97, 98)[q], []).append(lambda q=q: y_evac(i + 1, q))
                for s in range(8):
                    hooks.setdefault(s + 7, []).append(lambda s=s: scatter_add(i, s, 2 + s % 2))
                splits(i8, SPLIT, 96 + SPLIT, hooks, slot_m)

            with dve.Fori(0, GROUPS) as g:
                group(M8 + 12 * g, g)
            more = dve.value_load(rounds[0:1, 0:1], min_val=0, max_val=1)
            with dve.If(more != 0):
                with dve.Fori(0, GROUPS) as g:
                    group(M8 + 12 * GROUPS + 12 * g, GROUPS + g)
            n = more * GROUPS + GROUPS
            for s in range(8):
                scatter_add(n, s, s % 4)
            dve.wait_ge(S["sc_add"], 8 * n + 8)
            dve.wait_ge(S["sumsq3"], 4 * TB)
            link(V.tensor_reduce(stat[:, 20:22], stat[:, 56:64].rearrange("p (b q) -> p b q", b=TB), AX, ALU.add))
            mean_square(3, stat[:, 20:22])
            dve.wait_ge(S["gl_in"], 16)
            dve.wait_ge(S["rstd_ready"], 4)
            for b in range(TB):
                for h in range(D // N):
                    cols = slice(h * N, (h + 1) * N)
                    V.scalar_tensor_tensor(wide_t[:, b, cols], x2_tok[:, b, cols], rstd[:, 3, b:b + 1],
                                           gl_row[:, cols], ALU.mult, ALU.mult).then_inc(S["y_out"], 1)

        @block.tensor
        def _(pe):
            mm = nc.tensor.matmul

            def gemm(i8, u0, n, lhs, acc, hooks={}, rows=TB, start=True, stop=True, k0=0, kend=None):
                hi, lo = lhs
                for u in range(n):
                    pe.wait_ge(lo_done, 8 * i8 + u0 + u + 1)
                    s = (u0 + u) % SPLIT
                    for j in range(UK):
                        k = k0 + UK * u + j
                        first, last_k = start and u == 0 and j == 0, stop and u == n - 1 and j == UK - 1
                        for b in range(rows):
                            cols = slice(b * P, (b + 1) * P)
                            mm(acc[b], hi[:, k, cols], w_hi[:, s, j], start=first, stop=False)
                            mm(acc[b], hi[:, k, cols], w_lo[:, s, j], start=False, stop=False)
                            last = mm(acc[b], lo[:, k, cols], w_hi[:, s, j], start=False, stop=last_k)
                    last.then_inc(unit_done, 1)
                    for f in hooks.get(u0 + u, ()):
                        f()
                return last

            def acc(p):
                return [bank[:, 2 * p], bank[:, 2 * p + 1]]

            feat = (feat_hi_k, feat_lo_k)
            mid = (mid_hi_k, mid_lo_k)
            yhy = (yhy_hi_k, yhy_lo_k)

            def x_transpose(q):
                if q % 2 == 0:
                    pe.wait_ge(x_in[q // 2], 16)
                if q >= 4:
                    pe.wait_ge(S["x_lo"], 2 * (q - 4) + 2)
                for j in range(2):
                    for b in range(TB):
                        k = 2 * q + j
                        last = nc.tensor.transpose(bank[:, 4 + q % 4, j * L + b * P:j * L + (b + 1) * P],
                                                   x_tok[:, b, k * P:(k + 1) * P], ident[:])
                last.then_inc(S["x_t"], 1)

            def filter_first():
                pe.wait_ge(S["filt_in"], 64)
                mm(bank[0:HID, 4, 0:L], w1s[:], zp[:], start=True, stop=True).then_inc(S["f_mm"], 1)

            def filter_second():
                pe.wait_ge(S["f_sin"], 1)
                mm(bank[:, 4, 0:L], w2s[:], filt_a[0:HID], start=True, stop=True).then_inc(S["f_mm"], 1)

            pe.wait_ge(S["ident_ready"], 16)
            x_transpose(0)
            x_transpose(1)
            for u in range(8):
                pe.wait_ge(S["x_lo"], 2 * u + 2)
                ahead = (2, 4, 5, 6, 7, 8)[min(u, 5)], (4, 5, 6, 7, 8)[min(u, 4)]
                gemm(A8, u, 1, feat, acc(0), {u: [lambda q=q: x_transpose(q) for q in range(*ahead)]},
                     start=u == 0, stop=u == 7, k0=UK * u)
            gemm(A8 + 1, 0, 8, feat, acc(1), {2: [filter_first], 6: [filter_second]})
            for c in range(2, 4):
                pe.wait_ge(S["biased"], c - 1)
                gemm(A8 + c, 0, 8, feat, acc(c % 2))

            def sgu_mix():
                pe.wait_ge(S["ln_done"], TB)
                pe.wait_ge(S["zpad_ready"], 1)
                pe.wait_ge(S["f_arg"], 2)
                for g in range(8):
                    last = mm(bank[:, 4 + g // 2, (g % 2) * L:(g % 2 + 1) * L].rearrange("p (b k) -> p b k", b=TB),
                              sgw[:, g], wide_t[:, :, W + g * P:W + (g + 1) * P], start=True, stop=True)
                last.then_inc(S["mix_done"], 1)

            def sgu_transpose():
                pe.wait_ge(S["ysg"], 8)
                for k in range(CT):
                    for b in range(TB):
                        last = nc.tensor.transpose(bank[:, 4 + k // 2, (k % 2) * L + b * P:(k % 2) * L + (b + 1) * P],
                                                   wide_t[:, b, k * P:(k + 1) * P], ident[:])
                last.then_inc(S["ysg_t"], 1)

            def z_transpose(c):
                pe.wait_ge(S["zt_ready"], c + 1)
                if isinstance(c, int) and c == 0:
                    pe.wait_ge(S["f_arg"], 2)
                else:
                    pe.wait_ge(S["zpad_ready"], c)
                    pe.wait_ge(S["ysg_lo"], 4)
                for j in range(4):
                    for b in range(TB):
                        last = nc.tensor.transpose(bank[:, 4 + j // 2, (j % 2) * L + b * P:(j % 2) * L + (b + 1) * P],
                                                   zt[:, b, j * P:(j + 1) * P], ident[:])
                last.then_inc(S["z_t"], 1)

            pe.wait_ge(S["biased"], 3)
            gemm(B8, 0, 8, feat, acc(0), {})
            pe.wait_ge(S["biased"], 4)
            gemm(B8 + 1, 0, 8, feat, acc(1), {1: [lambda: z_transpose(0)], 4: [sgu_mix]})
            sgu_transpose()
            with pe.Fori(1, 3) as h:
                for p in range(2):
                    pe.wait_ge(S["zt_ready"], 2 * h + p - 1)
                    gemm(B8 + 2 * h + p, 0, 8, feat, acc(p), {2: [lambda: z_transpose(2 * h + p - 1)]})
            z_transpose(5)

            def v_transpose(o):
                pe.wait_ge(S["ot_ready"], 2 * o + 1)
                for q in range(4):
                    c, b = 4 * (q // 2), q % 2
                    for j in range(4):
                        last = nc.tensor.transpose(bank[:, 4 + q, j * P:(j + 1) * P],
                                                   vt_c[:, c + j, b::2], ident[:])
                    last.then_inc(S["v_t"], 1)

            def filt(s, o, h):
                pe.wait_ge(S["h3_in_%d" % h], 64 * o + 64)
                if h == 0:
                    pe.wait_ge(S["vtok_ready"], 4 * o + 4)
                else:
                    pe.wait_ge(S["ot_ready"], 2 * o + 2)
                for d in range(2):
                    for b in range(TB):
                        last = mm(bank[:, 4 + 2 * d + b], a2[:, d, b::2], w3s[:], start=True, stop=True)
                last.then_inc(S["filt_mm"], 1)

            def transform(s, rhs_c, rhs_s, ready, done):
                for f, rhs in enumerate((rhs_c, rhs_s)):
                    pe.wait_ge(S[ready], 2 * s + f + 1)
                    for b in range(2):
                        last = mm(bank[:, 4 + 2 * f + b], dft_f[:, b, f * P:(f + 1) * P], rhs[b], start=True, stop=True)
                    last.then_inc(S[done], 1)

            def response(s):
                pe.wait_ge(S["tables_in"], 32)
                transform(s, [prod_y[:, 0], prod_y[:, 1]], [prod_y[:, 2], prod_y[:, 3]], "hsd_ready", "k_mm")

            def spectrum(s, h):
                v = [v_tok[:, b, h * N:(h + 1) * N] for b in range(2)]
                transform(s, v, v, "k_ready", "u_mm")

            def inverse(s):
                pe.wait_ge(S["y_ready"], s + 2)
                for j in range(4):
                    for b in range(2):
                        at = (j % 2) * L + b * P
                        for f in range(2):
                            last = mm(bank[:, 4 + j // 2, at:at + P], k_resp[:, 2 * f + b, j * P:(j + 1) * P],
                                      dft_i[:, 2 * f + b], start=f == 0, stop=f == 1)
                last.then_inc(S["inv_mm"], 1)

            def turn(i8, n0, o, proj, hooks):
                pe.wait_ge(S["biased"], n0 + 4)
                gemm(i8, 0, 8, feat, acc(0), hooks)
                pe.wait_ge(S["merged_ready"], n0 + 1)
                gemm(i8, 8, 4, proj, acc(1), hooks)
                pe.wait_ge(S["biased"], n0 + 5)
                gemm(i8, 12, 8, feat, acc(0), hooks)
                pe.wait_ge(S["merged_ready"], n0 + 2)
                gemm(i8, 20, 4, proj, acc(1), hooks)

            pe.wait_ge(S["zt_ready"], 6)
            pe.wait_ge(S["ysg_lo"], 4)
            with pe.Fori(0, 2) as o:
                turn(C8 + 3 * o, 2 * o, o, mid, {
                    1: [lambda: v_transpose(o)],
                    2: [lambda: filt(2 * o, o, 0)],
                    3: [lambda: response(2 * o)],
                    4: [lambda: spectrum(2 * o, 0)],
                    12: [lambda: inverse(2 * o)],
                    13: [lambda: filt(2 * o + 1, o, 1)],
                    14: [lambda: response(2 * o + 1)],
                    15: [lambda: spectrum(2 * o + 1, 1)],
                    23: [lambda: inverse(2 * o + 1)]})

            def m_transpose(n, chunk):
                pe.wait_ge(S["yhy_lo_s"], 1)
                if not static_le(n, 0):
                    pe.wait_ge(S["m_lo"], n)
                for j in range(4):
                    for b in range(TB):
                        last = nc.tensor.transpose(bank[:, 4 + j // 2, (j % 2) * L + b * P:(j % 2) * L + (b + 1) * P],
                                                   wide_t[:, b, chunk * N + j * P:chunk * N + (j + 1) * P], ident[:])
                last.then_inc(S["m_t"], 1)

            def m_first(o):
                pe.wait_ge(S["merged_ready"], 4 + 2 * o + 2)
                m_transpose(o, 2 * o)

            for o in range(2):
                turn(D8 + 3 * o, 4 + 2 * o, o, yhy, {15: [lambda: m_first(o)]})
            m_transpose(2, 1)

            def h_transpose(c):
                pe.wait_ge(S["h_ready"], c + 1)
                if c:
                    pe.wait_ge(S["h_ev_act"], c)
                    pe.wait_ge(S["h_ev_dve"], c)
                for j in range(4):
                    for b in range(TB):
                        k = 4 * c + j
                        last = nc.tensor.transpose(bank[:, 4 + j // 2, (j % 2) * L + b * P:(j % 2) * L + (b + 1) * P],
                                                   wide_t[:, b, k * P:(k + 1) * P], ident[:])
                last.then_inc(S["h_tr"], 1)

            def router(c):
                pe.wait_ge(S["consts_in"], 16 * CONSTS)
                pe.wait_ge(S["h_ev_act"], c + 1)
                pe.wait_ge(S["h_ev_dve"], c + 1)
                for b in range(TB):
                    for k in range(4 * c, 4 * c + 4):
                        last = mm(bank[:, 6 + b, 0:20], h_t[:, k, b * P:(b + 1) * P], wr[:, k],
                                  start=k == 0, stop=k == KD - 1)
                return last

            hooks = {}
            for c in range(3):
                hooks[8 * c + 12] = [lambda c=c: h_transpose(c)]
                if c < 2:
                    hooks[8 * c + 17] = [lambda c=c: router(c)]
            def m_last():
                pe.wait_ge(S["merged_ready"], 9)
                m_transpose(3, 3)

            hooks[1] = [m_last]
            for c in range(4):
                if c >= 2:
                    pe.wait_ge(S["x_mid"], c - 1)
                for q, (lhs, k0) in enumerate(((mid, 0), (feat, 4), (mid, 4), (feat, 12))):
                    if c == 0:
                        pe.wait_ge(S["m_lo"], (1, 3, 2, 4)[q])
                    if c == 0 and q == 0:
                        pe.wait_ge(S["biased"], 12)
                    if c == 1 and q == 0:
                        pe.wait_ge(S["merged_ready"], 9)
                    gemm(E8, 8 * c + 2 * q, 2, lhs, acc(c % 2), hooks, start=q == 0, stop=q == 3, k0=k0)
            router(2)
            h_transpose(3)
            router(3).then_inc(S["r_mm"], 1)
            pe.wait_ge(S["oh_ready"], 1)
            mm(bank[:, 2, 32:36], before[:], oh[:, 2, 0], start=True, stop=True)
            mm(bank[:, 3, 32:36], ones[:], oh[:, 2, 0], start=True, stop=False)
            mm(bank[:, 3, 32:36], before[:], oh[:, 2, 1], start=False, stop=True)
            mm(bank[:, 2, 64:68], ones[:], oh[:, 2, 0], start=True, stop=False)
            mm(bank[:, 2, 64:68], ones[:], oh[:, 2, 1], start=False, stop=True).then_inc(S["pos_mm"], 1)

            def gather(n, q, dst):
                for kk in range(4):
                    k = 4 * q + kk
                    for b in range(TB):
                        last = mm(bank[:, dst, kk * CAP:(kk + 1) * CAP], wide_t[:, b, k * P:(k + 1) * P], perm[:, b],
                                  start=b == 0, stop=b == TB - 1)
                last.then_inc(S["ga_mm"], 1)

            def comb_gather(n):
                pe.wait_ge(S["perm_ready"], n + 1)
                for b in range(TB):
                    last = mm(bank[:, 2, 0:4], perm[:, b], comb[:, b], start=b == 0, stop=b == TB - 1)
                last.then_inc(S["comb_mm"], 1)

            def scatter(s, dst):
                b, q = s % 2, s // 2
                mm(bank[:, dst], perm_t[:, b * P:(b + 1) * P], y_hi[:, q * N:(q + 1) * N], start=True, stop=False)
                mm(bank[:, dst], perm_t[:, b * P:(b + 1) * P], y_lo[:, q * N:(q + 1) * N], start=False,
                   stop=True).then_inc(S["sc_mm"], 1)

            pe.wait_ge(S["perm_ready"], 1)
            pe.wait_ge(S["h_norm"], TB)
            for q in range(4):
                gather(0, q, 4 + q)
            pe.wait_ge(S["route_ready"], 1)
            comb_gather(0)

            def group(i8, i):
                def gate(e):
                    if e == 0:
                        for q in range(4):
                            pe.wait_ge(S["ga_lo"], 4 * i + max(q, 1) + 1)
                            gemm(i8, 2 * q, 2, (xg_hi, xg_lo), [bank[:, 0]], hooks, rows=1, start=q == 0, stop=q == 3,
                                 k0=4 * q)
                        return
                    pe.wait_ge(S["silu_done"], PER * i + e)
                    gemm(i8, GATE_AT[e], 8, (xg_hi, xg_lo), [bank[:, 0]], hooks, rows=1)

                def up(e):
                    if e:
                        pe.wait_ge(S["prod_done"], PER * i + e)
                    gemm(i8, GATE_AT[e] + 8, 8, (xg_hi, xg_lo), [bank[:, 1]], hooks, rows=1)

                def act_transpose(e):
                    pe.wait_ge(S["prod_done"], PER * i + e + 1)
                    if e:
                        pe.wait_ge(S["act_lo_s"], PER * i + e)
                    else:
                        pe.wait_ge(S["sc_add"], 8 * i + 8)
                    if e == PER - 1:
                        pe.wait_ge(S["combg_s"], i + 2)
                    for k in range(4):
                        last = nc.tensor.transpose(bank[:, 2, k * P:(k + 1) * P], prod[:, k * P:(k + 1) * P], ident[:])
                    last.then_inc(S["act_t"], 1)

                def down(e):
                    pe.wait_ge(S["act_lo_s"], PER * i + e + 1)
                    for c in range(4):
                        gemm(i8, DOWN_AT[e] + 2 * c, 2,
                             (act_hi[:, e % 2].rearrange("p (k s) -> p k s", k=4),
                              act_lo[:, e % 2].rearrange("p (k s) -> p k s", k=4)),
                             [bank[:, 4 + c]], hooks, rows=1, start=e == 0, stop=e == PER - 1)

                def scatter_last(s):
                    if s == 0:
                        pe.wait_ge(S["combg_s"], i + 1)
                    if s % 2 == 0:
                        pe.wait_ge(S["yg_lo"], 4 * i + s // 2 + 1)
                    if s >= 2:
                        pe.wait_ge(S["sc_add"], 8 * i + s - 1)
                    scatter(s, 2 + s % 2)

                def perm_transpose():
                    pe.wait_ge(S["sc_add"], 8 * i + 8)
                    for b in range(TB):
                        last = nc.tensor.transpose(bank[:, 3, b * P:(b + 1) * P], perm[:, b], ident[:])
                    last.then_inc(S["perm_tr"], 1)

                def comb_next():
                    pe.wait_ge(S["act_lo_s"], PER * i + PER - 1)
                    comb_gather(i + 1)

                def gather_next(q):
                    pe.wait_ge(*((S["perm_t_s"], i + 2), (S["silu_done"], PER * i + PER),
                                 (S["prod_done"], PER * i + PER), (S["ga_lo"], 4 * i + 5))[q])
                    gather(i + 1, q, GATHER_BANK[q])

                hooks = {s + 3: [lambda s=s: scatter_last(s)] for s in range(8)}
                hooks[15] = [perm_transpose]
                hooks[79] = [comb_next]
                hooks[85] = [lambda: act_transpose(PER - 1)]
                for q in range(4):
                    hooks[GATHER_AT[q]] = [lambda q=q: gather_next(q)]
                gate(0)
                up(0)
                for e in range(1, PER):
                    gate(e)
                    act_transpose(e - 1)
                    up(e)
                    down(e - 1)
                down(PER - 1)

            pe.wait_ge(S["perm_t_s"], 1)
            with pe.Fori(0, GROUPS) as g:
                group(M8 + 12 * g, g)
            more = pe.value_load(rounds[0:1, 0:1], min_val=0, max_val=1)
            with pe.If(more != 0):
                with pe.Fori(0, GROUPS) as g:
                    group(M8 + 12 * GROUPS + 12 * g, GROUPS + g)
            n = more * GROUPS + GROUPS
            for s in range(8):
                if s % 2 == 0:
                    pe.wait_ge(S["yg_lo"], 4 * n + s // 2 + 1)
                if s >= 4:
                    pe.wait_ge(S["sc_add"], 8 * n + s - 3)
                scatter(s, s % 4)


def tables():
    import numpy as np
    f32 = np.float32
    t = np.linspace(0.0, 1.0, L, dtype=f32)[:, None]
    bands = np.linspace(1e-4, (EMB - 1) // 2 - 1, (EMB - 1) // 2, dtype=f32)
    w = (f32(2.0 * math.pi / L) * np.arange(L, dtype=f32))[:, None]
    z = np.concatenate([t, np.cos(bands * w), -np.sin(bands * w)], axis=-1).astype(f32)
    deltas = np.abs(np.linspace(math.log(1e-2) / 1.5, math.log(1e-2) / 0.3, W, dtype=f32))
    decay = np.exp(-t * deltas).astype(f32)
    angle = np.outer(np.arange(L), 2 * np.arange(L) + 1) * (2.0 * math.pi / (4 * L))
    f = np.stack([np.cos(angle), np.sin(angle)], axis=1)[:, :, :P].reshape(P, 2, 2, P)
    row = np.arange(P)
    return {
        "zpos": np.ascontiguousarray(z.T),
        "decay": np.ascontiguousarray(decay.reshape(P, 2, W)),
        "dft": np.ascontiguousarray(f.astype(f32).reshape(P, 2, 2 * P)),
        "idft": np.ascontiguousarray((f / L).astype(f32).transpose(3, 2, 1, 0).reshape(P, 4, P)),
        "ident_in": np.eye(P, dtype=f32),
        "before_in": (row[:, None] < row[None, :]).astype(f32),
        "ones_in": np.ones((P, P), f32),
        "slots_in": np.ascontiguousarray(np.broadcast_to(np.arange(CAP, dtype=f32), (P, CAP))),
        "rank_in": np.ascontiguousarray(np.broadcast_to(np.arange(4, 0, -1, dtype=f32), (P, TB, 4))),
    }


def kernel(**inputs):
    import numpy as np
    import concourse.bacc as bacc
    from concourse.bass_utils import run_bass_kernel_spmd as run

    a = {k: np.asarray(v) for k, v in inputs.items()}

    def cols(v, order=None):
        m = v.reshape(-1, P).T
        return m if order is None else m[:, order]

    vfirst = list(range(2 * CT, 3 * CT)) + list(range(2 * CT))
    laid = {n: a[n] for n in ("x", "w_in", "w_hy_out", "w_sg_out", "w_out", "w_gate", "w_up", "w_down", "b_in",
                              "filt_w3", "hy_skip")}
    laid.update(
        ln_g=a["sg_ln_g"], ln_b=a["sg_ln_b"], g_ffn=a["g_ffn"], g_final=a["g_final"][None],
        b_router=np.tile(np.concatenate([a["b_rg"][0], a["b_re"][0].reshape(-1)])[None], (1, TB)).reshape(1, TB, 20),
        g_mix_c=cols(a["g_mix"][0]),
        conv_w_c=np.stack([cols(a["conv_w"][0, j], vfirst) for j in range(3)], axis=-1),
        conv_b_c=cols(a["conv_b"][0], vfirst),
        b_hy_c=cols(a["b_in"][0, :3 * W], vfirst),
        filt_w1=a["filt_w1"],
        filt_w2=np.concatenate([a["filt_w2"][0]] * 2, axis=1),
        filt_vec=np.stack([np.tile(a["filt_freq"][0], 2), np.tile(a["filt_b1"][0], 2), np.tile(a["filt_b2"][0], 2),
                           np.repeat(np.array([1.0, -1.0], np.float32), HID)], axis=1),
        sg_w_t=a["sg_w"][0].transpose(2, 0, 1),
        sg_b_t=a["sg_b"][0].T,
        w_router=np.concatenate([a["w_rg"][0], a["w_re"][0].transpose(1, 0, 2).reshape(D, -1)], axis=1)
        .reshape(KD, P, 20).transpose(1, 0, 2))
    laid.update(tables())

    nc = bacc.Bacc("TRN2", target_bir_lowering=False, num_devices=1)
    arrays, args = {}, {}
    for name, v in laid.items():
        v = np.ascontiguousarray(v)
        arrays["in_" + name] = v
        args[name] = nc.dram_tensor("in_" + name, v.shape, mybir.dt.from_np(v.dtype), kind="ExternalInput").ap()
    args["out"] = nc.dram_tensor("out_0", (1, L, D), F32, kind="ExternalOutput").ap()
    build(nc, **args)
    r = run(nc, [arrays], core_ids=[0])
    return r.results[0]["out_0"]
```
